# Optimizing a Trainium2 kernel written in Bass

```python
import jax, jax.numpy as jnp
from jax import lax
import numpy as np

D_MODEL = 1024
BATCH = 1
SEQ = 256
DEPTH = 1
DEC_BATCH = 8
DEC_SEQ = 8
PAST_LEN = 2048
PAGE_SIZE = 128

MIX_WIDTH = D_MODEL
POOL_WIDTH = MIX_WIDTH // 2
POOL_WINDOWS = (2, 4, 8, 16)
POOL_GROUPS = len(POOL_WINDOWS)
POOL_GROUP_DIM = POOL_WIDTH // POOL_GROUPS
POOL_MAX = max(POOL_WINDOWS)
DN_WIDTH = MIX_WIDTH - POOL_WIDTH
DN_HEAD_DIM = 128
DN_HEADS = DN_WIDTH // DN_HEAD_DIM
CONV_W = 4
DN_CHUNK = 64
IN_WIDTH = POOL_WIDTH + 4 * DN_WIDTH + 2 * DN_HEADS
N_EXPERTS = 32
TOP_K = 4
D_FF = D_MODEL
SWIGLU_LIMIT = 7.0
SWIGLU_ALPHA = 1.702
MOE_BLOCK = 128
PLE_DIM = 256
NORM_EPS = 1e-6

kernel_name = "hybrid_pool_gdn_moe_ple_step"

def rmsnorm(x, g):
    x32 = x.astype(jnp.float32)
    y = x32 * lax.rsqrt(jnp.mean(x32 * x32, axis=-1, keepdims=True) + NORM_EPS)
    return (y * g.astype(jnp.float32)).astype(x.dtype)

def l2norm(x):
    return x * lax.rsqrt(jnp.sum(x * x, axis=-1, keepdims=True) + NORM_EPS)

def pool_mixer(u, buf, pos0, pool_w, pool_scale):
    Bn, L, _ = u.shape
    P = POOL_MAX - 1
    ext = jnp.concatenate([buf.astype(u.dtype), u], axis=1)
    cs = jnp.cumsum(ext.astype(jnp.float32), axis=1)
    cs = jnp.concatenate([jnp.zeros((Bn, 1, POOL_WIDTH), jnp.float32), cs], axis=1)
    pos = (pos0 + jnp.arange(L)).astype(jnp.float32)
    pooled = []
    for j, w in enumerate(POOL_WINDOWS):
        sl = slice(j * POOL_GROUP_DIM, (j + 1) * POOL_GROUP_DIM)
        s = cs[:, P + 1:P + 1 + L, sl] - cs[:, P + 1 - w:P + 1 - w + L, sl]
        cnt = jnp.minimum(pos + 1.0, float(w))
        pooled.append(s / cnt[None, :, None])
    pooled = jnp.concatenate(pooled, axis=-1)
    d = (pooled - u.astype(jnp.float32)).astype(u.dtype).reshape(Bn, L, POOL_GROUPS, POOL_GROUP_DIM)
    out = jnp.einsum('blgc,gcd->blgd', d, pool_w).reshape(Bn, L, POOL_WIDTH) * pool_scale
    return out, ext[:, -P:]

def chunk_gated_delta(q, k, v, g, beta, S0):
    Bn, L, H, Dk = q.shape
    Dv = v.shape[-1]
    C = min(DN_CHUNK, L)
    n = -(-L // C)
    pad = n * C - L

    def prep(t):
        t = jnp.pad(t, [(0, 0), (0, pad)] + [(0, 0)] * (t.ndim - 2))
        t = jnp.moveaxis(t, 1, 2)
        return t.reshape(t.shape[:2] + (n, C) + t.shape[3:])

    q, k, v, g, beta = prep(q), prep(k), prep(v), prep(g), prep(beta)
    g_cum = jnp.cumsum(g, axis=-1)
    causal = jnp.tril(jnp.ones((C, C), bool))
    strict = jnp.tril(jnp.ones((C, C), bool), -1)
    diff = g_cum[..., :, None] - g_cum[..., None, :]
    decay = jnp.where(causal, jnp.exp(jnp.where(causal, diff, 0.0)), 0.0)
    k_beta = k * beta[..., None]
    M = jnp.where(strict, jnp.einsum('bhnid,bhnjd->bhnij', k_beta, k) * decay, 0.0)
    A = M + jnp.eye(C, dtype=M.dtype)
    rhs = jnp.concatenate([k_beta * jnp.exp(g_cum)[..., None], v * beta[..., None]], axis=-1)
    sol = lax.linalg.triangular_solve(A, rhs, left_side=True, lower=True)
    w_c, u_c = sol[..., :Dk], sol[..., Dk:]
    qk = jnp.einsum('bhnid,bhnjd->bhnij', q, k) * decay
    q_dec = q * jnp.exp(g_cum)[..., None]
    k_dec = k * jnp.exp(g_cum[..., -1:] - g_cum)[..., None]
    g_last = jnp.exp(g_cum[..., -1])
    xs = tuple(jnp.moveaxis(t, 2, 0) for t in (w_c, u_c, q_dec, qk, k_dec, g_last))

    def step(S, inp):
        wi, ui, qi, qki, ki, gl = inp
        v_new = ui - jnp.einsum('bhcd,bhde->bhce', wi, S)
        o = jnp.einsum('bhcd,bhde->bhce', qi, S) + jnp.einsum('bhij,bhje->bhie', qki, v_new)
        S = S * gl[..., None, None] + jnp.einsum('bhcd,bhce->bhde', ki, v_new)
        return S, o

    S, o = lax.scan(step, S0, xs)
    o = jnp.moveaxis(o, 0, 2).reshape(Bn, H, n * C, Dv)[:, :, :L]
    return jnp.moveaxis(o, 1, 2), S

def gated_deltanet(qkv, z, b, a, conv_buf, S0, conv_w, a_log, dt_bias, dn_norm):
    Bn, L, _ = qkv.shape
    ext = jnp.concatenate([conv_buf.astype(qkv.dtype), qkv], axis=1)
    acc = ext[:, 0:L] * conv_w[0]
    for j in range(1, CONV_W):
        acc = acc + ext[:, j:j + L] * conv_w[j]
    conv = jax.nn.silu(acc.astype(jnp.float32))
    new_conv = ext[:, -(CONV_W - 1):]
    q, k, v = jnp.split(conv, 3, axis=-1)
    q = l2norm(q.reshape(Bn, L, DN_HEADS, DN_HEAD_DIM)) * (DN_HEAD_DIM ** -0.5)
    k = l2norm(k.reshape(Bn, L, DN_HEADS, DN_HEAD_DIM))
    v = v.reshape(Bn, L, DN_HEADS, DN_HEAD_DIM)
    beta = jax.nn.sigmoid(b.astype(jnp.float32))
    g = -jnp.exp(a_log.astype(jnp.float32)) * jax.nn.softplus(a.astype(jnp.float32) + dt_bias.astype(jnp.float32))
    o, S = chunk_gated_delta(q, k, v, g, beta, S0.astype(jnp.float32))
    o = o * lax.rsqrt(jnp.mean(o * o, axis=-1, keepdims=True) + NORM_EPS) * dn_norm.astype(jnp.float32)
    o = o * jax.nn.silu(z.astype(jnp.float32)).reshape(Bn, L, DN_HEADS, DN_HEAD_DIM)
    return o.reshape(Bn, L, DN_WIDTH).astype(qkv.dtype), new_conv, S.astype(S0.dtype)

def moe_ffn(h, router_w, router_b, w_gate, b_gate, w_up, b_up, w_down, b_down):
    shp = h.shape
    x2d = h.reshape(-1, shp[-1])
    T = x2d.shape[0]
    logits = (x2d @ router_w + router_b).astype(jnp.float32)
    top_vals, top_idx = lax.top_k(logits, TOP_K)
    gates = jax.nn.softmax(top_vals, axis=-1).reshape(-1)
    flat_e = top_idx.reshape(-1).astype(jnp.int32)
    TK = T * TOP_K
    order = jnp.argsort(flat_e, stable=True).astype(jnp.int32)
    sorted_e = flat_e[order]
    sorted_tok = order // TOP_K
    counts = jnp.bincount(flat_e, length=N_EXPERTS).astype(jnp.int32)
    padded = (counts + MOE_BLOCK - 1) // MOE_BLOCK * MOE_BLOCK
    pad_end = jnp.cumsum(padded)
    pad_start = pad_end - padded
    start = jnp.cumsum(counts) - counts
    dest = pad_start[sorted_e] + jnp.arange(TK, dtype=jnp.int32) - start[sorted_e]
    n_blocks = -(-TK // MOE_BLOCK) + N_EXPERTS
    P = n_blocks * MOE_BLOCK
    slot_tok = jnp.full((P,), T, jnp.int32).at[dest].set(sorted_tok)
    slot_gate = jnp.zeros((P,), jnp.float32).at[dest].set(gates[order])
    block_e = jnp.minimum(jnp.searchsorted(pad_end, jnp.arange(n_blocks) * MOE_BLOCK, side='right'), N_EXPERTS - 1)
    x_pad = jnp.concatenate([x2d, jnp.zeros((1, shp[-1]), x2d.dtype)], axis=0)
    xb = x_pad[slot_tok].reshape(n_blocks, MOE_BLOCK, shp[-1])

    def expert_block(args):
        xblk, e = args
        gt = jnp.minimum(xblk @ w_gate[e] + b_gate[e], SWIGLU_LIMIT)
        up = jnp.clip(xblk @ w_up[e] + b_up[e], -SWIGLU_LIMIT, SWIGLU_LIMIT)
        hid = (up + 1.0) * (gt * jax.nn.sigmoid(SWIGLU_ALPHA * gt))
        return hid @ w_down[e] + b_down[e]

    yb = lax.map(expert_block, (xb, block_e)).reshape(P, shp[-1])
    y = jax.ops.segment_sum(yb * slot_gate[:, None].astype(yb.dtype), slot_tok, num_segments=T + 1)[:T]
    return y.reshape(shp)

def hybrid_layer(x, p, pool_buf, conv_buf, ssm0, pos0, ln_mix, w_in, pool_w, pool_scale, conv_w, a_log,
                 dt_bias, dn_norm, w_out, ln_moe, router_w, router_b, w_gate, b_gate, w_up, b_up, w_down,
                 b_down, ln_ple, w_ple_gate, w_ple):
    h = rmsnorm(x, ln_mix)
    proj = h @ w_in
    o0 = POOL_WIDTH
    o1 = o0 + 3 * DN_WIDTH
    o2 = o1 + DN_WIDTH
    o3 = o2 + DN_HEADS
    u, qkv, z, b, a = proj[..., :o0], proj[..., o0:o1], proj[..., o1:o2], proj[..., o2:o3], proj[..., o3:]
    pool_out, new_pool = pool_mixer(u, pool_buf, pos0, pool_w, pool_scale)
    dn_out, new_conv, new_ssm = gated_deltanet(qkv, z, b, a, conv_buf, ssm0, conv_w, a_log, dt_bias, dn_norm)
    x = x + jnp.concatenate([pool_out, dn_out], axis=-1) @ w_out
    x = x + moe_ffn(rmsnorm(x, ln_moe), router_w, router_b, w_gate, b_gate, w_up, b_up, w_down, b_down)
    gate = jax.nn.sigmoid((rmsnorm(x, ln_ple) @ w_ple_gate).astype(jnp.float32)).astype(x.dtype)
    x = x + (p @ w_ple) * gate
    return x, new_pool, new_conv, new_ssm

def setup_inputs(seed: int = 0) -> dict:
    key = jax.random.key(seed)
    ks = iter(jax.random.split(key, 40))

    def nrm(shape, scale):
        return jax.random.normal(next(ks), shape, jnp.float32) * scale

    dt = jnp.exp(jax.random.uniform(next(ks), (DEPTH, DN_HEADS), jnp.float32, np.log(1e-3), np.log(1e-1)))
    return {
        'x_prompt': nrm((BATCH, SEQ, D_MODEL), 1.0),
        'x_sample': nrm((DEC_BATCH, DEC_SEQ, D_MODEL), 1.0),
        'state_pool': nrm((DEPTH, DEC_BATCH, POOL_MAX - 1, POOL_WIDTH), 1.0),
        'state_conv': nrm((DEPTH, DEC_BATCH, CONV_W - 1, 3 * DN_WIDTH), 1.0),
        'state_ssm': nrm((DEPTH, DEC_BATCH, DN_HEADS, DN_HEAD_DIM, DN_HEAD_DIM), 0.1),
        'p_prompt': nrm((DEPTH, BATCH, SEQ, PLE_DIM), 1.0),
        'p_sample': nrm((DEPTH, DEC_BATCH, DEC_SEQ, PLE_DIM), 1.0),
        'ln_mix': 1.0 + nrm((DEPTH, D_MODEL), 0.02),
        'w_in': nrm((DEPTH, D_MODEL, IN_WIDTH), D_MODEL ** -0.5),
        'pool_w': nrm((DEPTH, POOL_GROUPS, POOL_GROUP_DIM, POOL_GROUP_DIM), POOL_GROUP_DIM ** -0.5),
        'pool_scale': 1.0 + nrm((DEPTH, POOL_WIDTH), 0.1),
        'conv_w': nrm((DEPTH, CONV_W, 3 * DN_WIDTH), CONV_W ** -0.5),
        'a_log': jnp.log(jax.random.uniform(next(ks), (DEPTH, DN_HEADS), jnp.float32, 1.0, 16.0)),
        'dt_bias': dt + jnp.log(-jnp.expm1(-dt)),
        'dn_norm': 1.0 + nrm((DEPTH, DN_HEAD_DIM), 0.02),
        'w_out': nrm((DEPTH, MIX_WIDTH, D_MODEL), MIX_WIDTH ** -0.5),
        'ln_moe': 1.0 + nrm((DEPTH, D_MODEL), 0.02),
        'router_w': nrm((DEPTH, D_MODEL, N_EXPERTS), D_MODEL ** -0.5),
        'router_b': nrm((DEPTH, N_EXPERTS), 0.01),
        'w_gate': nrm((DEPTH, N_EXPERTS, D_MODEL, D_FF), D_MODEL ** -0.5),
        'b_gate': nrm((DEPTH, N_EXPERTS, D_FF), 0.01),
        'w_up': nrm((DEPTH, N_EXPERTS, D_MODEL, D_FF), D_MODEL ** -0.5),
        'b_up': nrm((DEPTH, N_EXPERTS, D_FF), 0.01),
        'w_down': nrm((DEPTH, N_EXPERTS, D_FF, D_MODEL), D_FF ** -0.5),
        'b_down': nrm((DEPTH, N_EXPERTS, D_MODEL), 0.01),
        'ln_ple': 1.0 + nrm((DEPTH, D_MODEL), 0.02),
        'w_ple_gate': nrm((DEPTH, D_MODEL, D_MODEL), D_MODEL ** -0.5),
        'w_ple': nrm((DEPTH, PLE_DIM, D_MODEL), PLE_DIM ** -0.5),
        'final_norm': 1.0 + nrm((D_MODEL,), 0.02),
    }

def reference(x_prompt, x_sample, state_pool, state_conv, state_ssm, p_prompt, p_sample, ln_mix, w_in,
              pool_w, pool_scale, conv_w, a_log, dt_bias, dn_norm, w_out, ln_moe, router_w, router_b,
              w_gate, b_gate, w_up, b_up, w_down, b_down, ln_ple, w_ple_gate, w_ple, final_norm):
    hp, hs = x_prompt, x_sample
    Bp = x_prompt.shape[0]
    pool_p, conv_p, ssm_p, pool_s, conv_s, ssm_s = [], [], [], [], [], []
    for i in range(DEPTH):
        lw = (ln_mix[i], w_in[i], pool_w[i], pool_scale[i], conv_w[i], a_log[i], dt_bias[i], dn_norm[i],
              w_out[i], ln_moe[i], router_w[i], router_b[i], w_gate[i], b_gate[i], w_up[i], b_up[i],
              w_down[i], b_down[i], ln_ple[i], w_ple_gate[i], w_ple[i])
        zero_pool = jnp.zeros((Bp, POOL_MAX - 1, POOL_WIDTH), x_prompt.dtype)
        zero_conv = jnp.zeros((Bp, CONV_W - 1, 3 * DN_WIDTH), x_prompt.dtype)
        zero_ssm = jnp.zeros((Bp, DN_HEADS, DN_HEAD_DIM, DN_HEAD_DIM), state_ssm.dtype)
        hp, a1, b1, c1 = hybrid_layer(hp, p_prompt[i], zero_pool, zero_conv, zero_ssm, 0, *lw)
        hs, a2, b2, c2 = hybrid_layer(hs, p_sample[i], state_pool[i], state_conv[i], state_ssm[i], PAST_LEN, *lw)
        pool_p.append(a1)
        conv_p.append(b1)
        ssm_p.append(c1)
        pool_s.append(a2)
        conv_s.append(b2)
        ssm_s.append(c2)
    y_prompt = rmsnorm(hp, final_norm)
    y_sample = rmsnorm(hs, final_norm)
    return (y_prompt, y_sample, jnp.stack(pool_p), jnp.stack(conv_p), jnp.stack(ssm_p),
            jnp.stack(pool_s), jnp.stack(conv_s), jnp.stack(ssm_s))


_drawn_inputs = setup_inputs


def setup_inputs(seed=0):
    import zlib

    import numpy as np

    out = dict(_drawn_inputs(seed))
    spreads = {}
    factors = {'dn_norm': 2.791,
     'router_b': 2.723,
     'b_gate': 8.0,
     'b_up': 27.334,
     'b_down': 8.0,
     'ln_ple': 160.231,
     'final_norm': 20.489}
    for name, (base, spread) in spreads.items():
        noise = np.random.default_rng([zlib.crc32(name.encode()), seed]).standard_normal(out[name].shape)
        drawn = base * np.exp(spread * noise) if base else spread * noise
        out[name] = __import__('jax').numpy.asarray(drawn.astype(out[name].dtype))
    for name, factor in factors.items():
        out[name] = (out[name] * factor).astype(out[name].dtype)
    return out
```

```python
from contextlib import ExitStack

import concourse.bass as bass
from concourse import mybir

F32 = mybir.dt.float32
I32 = mybir.dt.int32
ALU = mybir.AluOpType
ACT = mybir.ActivationFunctionType
AX_X = mybir.AxisListType.X

P = 128
D_MODEL = 1024
KT = D_MODEL // P
SEQ = 256
DB, DS = 8, 8
NSAMP = DB * DS
T = SEQ + NSAMP
TILES = [(0, P), (P, P), (SEQ, NSAMP)]
NT = len(TILES)
POOL_W = 512
WINDOWS = (2, 4, 8, 16)
PG = len(WINDOWS)
PH = max(WINDOWS) - 1
HEADS = 4
CONV = 4
CH = CONV - 1
QKV_T = 3 * HEADS
IN_W = POOL_W + 4 * HEADS * P + 2 * HEADS
NB_IN = 5
E = 32
TOPK = 4
FF = 1024
LIMIT = 7.0
ALPHA = 1.702
PLE = 256
EPS = 1e-6
CAP = 64
PAIRS = E // 2
EPAD = E + 2
RING = 8
SLOT = 4096
CPM = 4
CPP = 3 * CPM
NCH = PAIRS * CPP
UEW = (PH + SEQ) + DB * (PH + DS)
QEW = (CH + SEQ) + DB * (CH + DS)
LEVELS = 7
OV_MAX = (T * TOPK - 1) // CAP
OV_OFF = [CAP, CAP + P]
OV_CHUNKS = 6

IN_ORDER = [2, 1, 3, 0, 4]


def chain(eng, own):
    counts = {}

    def step(ins, s=None, value=None):
        s = own if s is None else s
        counts[s.name] = counts.get(s.name, 0) + 1
        ins.then_inc(s, 1)
        eng.wait_ge(s, counts[s.name] if value is None else value)
    return step


def trunk_kernel(nc, d, o):
    with ExitStack() as ctx:
        def sb(name, shape, dt=F32):
            return ctx.enter_context(nc.sbuf_tensor(name, shape, dt))

        def sem(name):
            return ctx.enter_context(nc.semaphore(name))

        ring = sb("ring", [P, RING, SLOT])
        X = sb("x_resid", [P, NT * D_MODEL])
        H = sb("h_region", [P, QKV_T * T])
        HT = sb("ht_region", [P, KT * T])
        Q = sb("q_region", [P, QKV_T * QEW])
        U = sb("u_region", [P, PG * UEW])
        Z = sb("z_region", [P, 2 * D_MODEL])
        ident = sb("ident", [P, P])
        ones = sb("ones", [P, P])
        causal = sb("causal", [P, P])
        strict = sb("strict", [P, P])
        seg = sb("seg", [NSAMP, NSAMP])
        segcausal = sb("segcausal", [NSAMP, NSAMP])
        lmask = sb("lmask", [P, LEVELS, P])
        iotaf = sb("iotaf", [P, P])
        vecs = sb("vecs", [P, 77])
        wrout = sb("wrout", [P, KT, E])
        small = sb("small", [P, 160])
        rank = sb("rank", [P, EPAD, NT])
        gate = sb("gate", [P, EPAD, NT])
        ov_off = sb("ov_off", [P, OV_MAX])
        ov_e = sb("ov_e", [P, OV_MAX], I32)
        ov_n = sb("ov_n", [P, 1], I32)

        ptmp = sb("ptmp", [P, UEW])
        iti = ptmp[:, 0:P].bitcast(I32)

        PS = ctx.enter_context(nc.psum_tensor("ps", [P, 8, 512], F32))

        x3 = X[:, :].rearrange("p (t d) -> p t d", t=NT)
        h3 = H[:, 0:NT * D_MODEL].rearrange("p (t d) -> p t d", t=NT)
        ct = H[:, :].rearrange("p (c t) -> p c t", c=QKV_T)
        hT = HT[:, :].rearrange("p (k t) -> p k t", k=KT)
        qe = Q[:, :].rearrange("p (c t) -> p c t", c=QKV_T)
        ue = U[:, :].rearrange("p (c t) -> p c t", c=PG)
        zT = Z[:, 0:PG * T].rearrange("p (c t) -> p c t", c=PG)
        ptmp2 = Z[:, PG * T:PG * T + UEW]
        wtail = Z[:, 1736:1800].rearrange("p (k c) -> p k c", k=KT)
        VEC = {"ln_mix": 0, "ln_moe": 8, "ln_ple": 16, "pool_scale": 24, "dn_norm": 28, "conv_w": 29}

        def vec(name, i=0, n=1):
            return vecs[:, VEC[name] + i:VEC[name] + i + n]

        def sm(at, *shape):
            n = 1
            for s in shape:
                n *= s
            v = small[:, at:at + n]
            return v.rearrange("p (a b) -> p a b", a=shape[0]) if len(shape) == 2 else v
        ss = sm(0, NT)
        rstd = sm(3, NT)
        beta = sm(6, NT, HEADS)
        gl = sm(18, NT, HEADS)
        gc = sm(30, NT, HEADS)
        egc = sm(42, NT, HEADS)
        kdec = sm(54, NT, HEADS)
        egl = sm(66, NT, HEADS)
        egs = sm(78, HEADS, DB)
        alog = sm(110, HEADS)
        dtb = sm(114, HEADS)
        inv16 = sm(118, 16)
        rb = small[0:E, 134:135]
        tmp12 = sm(136, NT, HEADS)
        pcol = small[:, 148:149]
        scol = small[:, 149:150]
        oss = sm(150, 4)

        sqb = [X[:, 0:T], X[:, T:2 * T]]
        rnb = [X[:, o_:o_ + T] for o_ in (640, 2304, 2624)]
        poolw = X[:, 1024:1536].rearrange("p (g d) -> p g d", g=PG)
        clast = X[:, 1536:1536 + QKV_T * DB * CH].rearrange("p (c r) -> p c r", c=QKV_T)
        ulast = X[:, 2048:2048 + PG * NSAMP].rearrange("p (c r) -> p c r", c=PG)
        convord = {c: i for i, c in enumerate([4, 5, 6, 7, 0, 1, 2, 3, 8, 9, 10, 11])}

        def prompt_cols(v, c, hist):
            return v[:, c, hist:hist + SEQ]

        def sample_cols(v, c, hist, lo=None, n=DS):
            lo = hist if lo is None else lo
            base = hist + SEQ
            return v[:, c, base:base + DB * (hist + DS)].rearrange("p (b w) -> p b w", b=DB)[:, :, lo:lo + n]

        def quads(region, n):
            return [region[0:n, i * HEADS * n:(i + 1) * HEADS * n].rearrange("p (h t) -> p h t", h=HEADS)
                    for i in range(6)]
        scratch = [quads(X[:, :], P), quads(ring[:, 4, :], P), quads(U[:, :], NSAMP)]
        kN = Q[:, 0:1536].rearrange("p (t h d) -> p t h d", t=NT, h=HEADS)
        vN = Q[:, 1536:3072].rearrange("p (t h d) -> p t h d", t=NT, h=HEADS)
        S1 = Q[:, 3072:3584].rearrange("p (h d) -> p h d", h=HEADS)
        kqS = Q[:, 3584:4096].rearrange("p (h t) -> p h t", h=HEADS)
        oN = [scratch[0][5], scratch[1][5],
              ring[0:NSAMP, 4, 3072:3584].rearrange("p (h d) -> p h d", h=HEADS)]
        qS2 = ring[0:NSAMP, 4, 3584:4096].rearrange("p (h d) -> p h d", h=HEADS)
        vmask = U[0:NSAMP, 0:1024].rearrange("p (b d) -> p b d", b=DB)
        s0 = ring[:, 7, :].rearrange("p (b h e) -> p b h e", b=DB, h=HEADS)
        tilepart = [(causal, ones, 0, P), (causal, ones, P, P), (segcausal, seg, SEQ, NSAMP)]

        st_conv = ring[0:DB * CH, 7, 0:QKV_T * P]
        st_pool = ring[0:DB * PH, 7, 1536:2048]
        vrows = ring[0:77, 7, 2048:2176]
        outrow = ring[:, 6, :]

        xg = HT[:, 0:1024]
        xgT = HT[:, 1024:2048].rearrange("p (k s) -> p k s", k=KT)
        ind = HT[0:E, 2048:2304].rearrange("p (b s) -> p b s", b=2)
        gbuf, ubuf, sbuf_, hidf = (Q[:, i * 1024:(i + 1) * 1024] for i in range(4))
        hidT = hidf.rearrange("p (k s) -> p k s", k=KT)
        ybuf = U[:, 0:1024]
        Ssel = U[:, 1024:1408].rearrange("p (t s) -> p t s", t=NT)
        Sgat = U[:, 1408:1792].rearrange("p (t s) -> p t s", t=NT)
        SgT = [H[:, 3072 + 384 * b:3456 + 384 * b].rearrange("p (t s) -> p t s", t=NT) for b in range(2)]
        bgu = Z[0:E, :].rearrange("p (m f) -> p m f", m=2)
        bdn = U[0:E, 0:1024]
        GT = SgT[1][0:E]

        def rt(i):
            return Q[:, 1024 + i * 96:1120 + i * 96].rearrange("p (t e) -> p t e", t=NT)
        logT = Q[0:E, 0:T]
        Lg, gtm, eqm, cum, sel, exq = (rt(i) for i in range(6))
        m8 = Q[:, 1700:1724].rearrange("p (t e) -> p t e", t=NT)
        ngt = Q[:, 1724:1727]
        den = Q[:, 1727:1730]
        cnt = Q[:, 1730:1762]
        flg = Q[:, 1762:1826].rearrange("p (e b) -> p e b", b=2)
        pos = Q[:, 1826:1890]
        evec = Q[:, 1890:1954].rearrange("p (e b) -> p e b", b=2)
        ovec = Q[:, 1954:2018].rearrange("p (e b) -> p e b", b=2)
        ove_f = Q[:, 2018:2018 + OV_MAX]
        cmp_ = Q[:, 2048:2048 + OV_MAX * 64].rearrange("p (j x) -> p j x", j=OV_MAX)

        wple = ring[:, 0, 0:2048].rearrange("p (k f) -> p k f", k=2)
        pin = ring[:, 1, 0:768].rearrange("p (t f) -> p t f", t=NT)
        pT = ring[:, 1, 1024:1024 + 2 * T].rearrange("p (k t) -> p k t", k=2)
        wpg = ring[:, 6:8, :].rearrange("p s (k f) -> p (s k) f", k=4)
        sg3 = Q[:, 0:3072].rearrange("p (t f) -> p t f", t=NT)
        fnb = U[:, 0:1024]

        vecs_in = sem("vecs_in")
        x_in = [sem(f"x_in{t}") for t in range(NT)]
        win_in = [sem(f"win_in{b}") for b in range(NB_IN)]
        wtail_in = sem("wtail_in")
        smalls_in = sem("smalls_in")
        hist_in = sem("hist_in")
        wout_in = sem("wout_in")
        s0_in = sem("s0_in")
        xagain_in = sem("xagain_in")
        bias_in = sem("bias_in")
        chunk_in = [sem(f"chunk_in{c}") for c in range(2 * CPP)]
        ovch_in = [sem(f"ovch_in{c}") for c in range(OV_CHUNKS)]
        wpg_in = sem("wpg_in")
        tail_in = sem("tail_in")
        out_done = sem("out_done")
        chunk_used = sem("chunk_used")
        ov_used = sem("ov_used")
        win_used = sem("win_used")
        filled = [sem(f"filled{b}") for b in range(8)]
        drained = [sem(f"drained{b}") for b in range(8)]
        consts = sem("consts")
        h_ready = sem("h_ready")
        ext_zero = sem("ext_zero")
        acc_ready = sem("acc_ready")
        ct_ready = sem("ct_ready")
        sq_ready = sem("sq_ready")
        norm_ready = sem("norm_ready")
        d_ready = sem("d_ready")
        v_step = sem("v_step")
        a_step = sem("a_step")
        g_step = sem("g_step")
        v_mark = sem("v_mark")
        a_mark = sem("a_mark")
        VM = {n: i + 1 for i, n in enumerate(
            ["ba", "sp_in", "g", "gcs"] + [f"diff{t}" for t in range(NT)] + [f"U{t}" for t in range(NT)]
            + ["kd", "S2", "rs_o", "vm0", "vm1", "vm2", "vm3", "S0", "x2", "h2", "m8", "sel", "gates", "table",
               "moe_done", "h3"] + [f"y{t}" for t in range(NT)] + [f"yout{t}" for t in range(NT)])}
        AM = {n: i + 1 for i, n in enumerate(
            ["ss", "exps", "ea", "lg", "gexp"] + [f"E{t}" for t in range(NT)]
            + ["ss2", "exq", "ss3"] + [f"ss4{t}" for t in range(NT)])}
        g_ready = sem("g_ready")
        small_zero = sem("small_zero")
        inv_ready = sem("inv_ready")
        root_ready = sem("root_ready")
        acc_pool = sem("acc_pool")
        packed = sem("packed")
        poolw_in = sem("poolw_in")
        pool_stored = sem("pool_stored")
        ssm_stored = sem("ssm_stored")
        hist_stored = sem("hist_stored")
        s0_stored = sem("s0_stored")
        v_loop = sem("v_loop")
        v_ov = sem("v_ov")
        pair_sel = sem("pair_sel")
        g_act = sem("g_act")
        sig_act = sem("sig_act")
        up_act = sem("up_act")
        y_act = sem("y_act")
        ovy_act = sem("ovy_act")
        hid_act = sem("hid_act")
        ov_sel = sem("ov_sel")
        ovg_act = sem("ovg_act")
        ovs_act = sem("ovs_act")
        ovh_act = sem("ovh_act")

        uses, fills = {}, [0] * 8

        def use(name, bank):
            uses[name] = (bank, fills[bank])
            fills[bank] += 1

        rr = [0]

        def nxt(name, banks=range(8)):
            banks = list(banks)
            use(name, banks[rr[0] % len(banks)])
            rr[0] += 1

        for n in ["vec", "sc", "sp"] + [f"hT{t}{hf}" for t in range(NT) for hf in range(2)] + ["ba"]:
            nxt(n)
        for b in IN_ORDER:
            for c in range(4):
                nxt(f"pr{4 * b + c}")
            if b == 1:
                for c in range(8):
                    nxt(f"ss{c}")
        for n in (["cnp0", "cnp1", "cnp2", "cns0", "cns1", "cns2", "npp", "nps"]
                  + [f"kN{t}" for t in range(NT)] + [f"vN{t}" for t in range(NT)]
                  + [f"pm{g}" for g in range(PG)]):
            nxt(n)
        nxt("gcs")
        nxt("egs")
        for t in range(NT):
            nxt(f"G{t}")
            nxt(f"kk{t}")
            nxt(f"qk{t}")
        for t in range(NT):
            nxt(f"T{t}")
        for s in range(1, LEVELS):
            ts = [t for t in range(NT) if t < 2 or s < 3]
            for t in ts:
                nxt(f"P{s}{t}")
            for t in ts:
                if s < LEVELS - 1 and (t < 2 or s < 2):
                    nxt(f"Q{s}{t}")
                nxt(f"QT{s}{t}")
        for n in ["v0", "S1", "o0", "kqs", "kS1", "qS1", "R2k", "R2q", "v1", "v2", "o1", "S2", "o2"]:
            nxt(n)
        for t in range(NT):
            nxt(f"oT{t}")
        for h in range(HEADS):
            nxt(f"ns{h}a")
            nxt(f"ns{h}b")
        for t in range(NT):
            for hf in range(2):
                nxt(f"op{t}{hf}")
        for t in range(NT):
            for hf in range(2):
                nxt(f"rT{t}{hf}")
        for n in ["lg", "lgT", "rk", "GT"]:
            nxt(n)
        for t in range(NT):
            for hf in range(2):
                nxt(f"bd{t}{hf}")
        use("g0a", 6), use("g0b", 7), use("xt0a", 6), use("xt0b", 7), use("sgt0", 6)
        base = list(fills)
        ovbase = [n + 13 * (PAIRS // 2) + 3 for n in base]
        for n in (["pT0", "pT1"] + [f"tT{t}{hf}" for t in range(NT) for hf in range(2)]
                  + [f"{w}{t}{hf}" for t in range(NT) for hf in range(2) for w in ("pg", "pp")]):
            nxt(n, range(6))

        def bank(name):
            return PS[:, uses[name][0], :]

        def can_fill(eng, name):
            b, k = uses[name]
            if k:
                eng.wait_ge(drained[b], k)

        def is_filled(eng, name):
            b, k = uses[name]
            eng.wait_ge(filled[b], k + 1)

        def is_drained(eng, name):
            b, k = uses[name]
            eng.wait_ge(drained[b], k + 1)

        def fsem(name):
            return filled[uses[name][0]]

        def dsem(name):
            return drained[uses[name][0]]

        chunk_src = {"g": d["w_gate"][0], "u": d["w_up"][0], "d": d["w_down"][0]}

        def load_chunk(eng, c, e, s):
            cc = c % CPP
            r = (cc % CPM) * 2 * P
            for a_ in range(2):
                w = chunk_src["gud"[cc // CPM]][bass.ds(e + a_, 1)]
                eng.dma_start(slot(c)[:, a_], w[:, r:r + 2 * P, :].rearrange("a (k p) f -> p (a k) f", p=P)
                              ).then_inc(s, 16)

        def slot(c):
            return ring[:, c % RING, :].rearrange("p (a k f) -> p a k f", a=2, k=2)

        def ov_chunk(e, c):
            w = chunk_src["gud"[c // 2]][bass.ds(e, 1)]
            r = (c % 2) * 4 * P
            return w[:, r:r + 4 * P, :].rearrange("a (k p) f -> p (a k) f", p=P)

        block = ctx.enter_context(nc.Block())

        @block.sync
        def _(sp):
            r = 0
            for n in ("ln_mix", "ln_moe", "ln_ple", "pool_scale", "dn_norm"):
                k = d[n].shape[1] // P
                sp.dma_start(vrows[r:r + k, :], d[n][0].rearrange("(k p) -> k p", p=P)).then_inc(vecs_in, 16)
                r += k
            sp.dma_start(vrows[r:r + CONV * QKV_T, :],
                         d["conv_w"][0].rearrange("j (c p) -> (j c) p", p=P)).then_inc(vecs_in, 16)
            for t, (t0, n) in enumerate(TILES):
                src = d["x_prompt"][0, t0:t0 + n] if t < 2 else d["x_sample"].rearrange("b s d -> (b s) d")
                sp.dma_start(x3[0:n, t, :], src).then_inc(x_in[t], 16)
            sp.dma_start(st_conv, d["state_conv"][0].rearrange("b r c -> (b r) c")).then_inc(hist_in, 16)
            sp.dma_start(st_pool, d["state_pool"][0].rearrange("b r c -> (b r) c")).then_inc(hist_in, 16)
            sp.wait_ge(small_zero, 1)
            sp.dma_start(alog, d["a_log"][0:1, :].broadcast_to([P, HEADS])).then_inc(smalls_in, 16)
            sp.dma_start(dtb, d["dt_bias"][0:1, :].broadcast_to([P, HEADS])).then_inc(smalls_in, 16)
            sp.dma_start(rb, d["router_b"][0].rearrange("(e a) -> e a", a=1)).then_inc(smalls_in, 16)
            sp.dma_start(wtail[:, :, :], d["w_in"][0, :, NB_IN * 512:IN_W].rearrange("(k p) c -> p k c", p=P)
                         ).then_inc(wtail_in, 16)
            for i, b in enumerate(IN_ORDER):
                sp.dma_start(ring[:, i, :].rearrange("p (k c) -> p k c", k=KT),
                             d["w_in"][0, :, b * 512:(b + 1) * 512].rearrange("(k p) c -> p k c", p=P)
                             ).then_inc(win_in[i], 16)
            sp.dma_start(wrout[:, :, :], d["router_w"][0].rearrange("(k p) e -> p k e", p=P)).then_inc(smalls_in, 16)
            sp.wait_ge(h_ready, NT)
            sp.dma_start(poolw, d["pool_w"][0].rearrange("g c e -> c g e")).then_inc(poolw_in, 16)
            is_drained(sp, "vec"), is_drained(sp, "sc"), is_drained(sp, "sp")
            sp.dma_start(s0, d["state_ssm"][0].rearrange("b h d e -> d b h e")).then_inc(s0_in, 16)
            sp.dma_start(ring[:, 5, :].rearrange("p (k f) -> p k f", k=4),
                         d["w_out"][0, 0:512].rearrange("(k p) f -> p k f", p=P)).then_inc(wout_in, 16)
            for c in range(4):
                sp.wait_ge(win_used, c + 1)
                load_chunk(sp, c, 0, chunk_in[c])
            sp.wait_ge(hist_stored, 16 * 4)
            sp.dma_start(ring[:, 6, :].rearrange("p (k f) -> p k f", k=4),
                         d["w_out"][0, 512:1024].rearrange("(k p) f -> p k f", p=P)).then_inc(wout_in, 16)
            for t in range(NT):
                is_drained(sp, f"oT{t}")
            for t, (t0, n) in enumerate(TILES):
                src = d["x_prompt"][0, t0:t0 + n] if t < 2 else d["x_sample"].rearrange("b s d -> (b s) d")
                sp.dma_start(x3[0:n, t, :], src).then_inc(xagain_in, 16)
            sp.dma_start(bgu[:, 0, :], d["b_gate"][0]).then_inc(bias_in, 16)
            sp.dma_start(bgu[:, 1, :], d["b_up"][0]).then_inc(bias_in, 16)
            sp.wait_ge(v_mark, VM["vm3"])
            is_filled(sp, "ns3b")
            sp.dma_start(bdn, d["b_down"][0]).then_inc(bias_in, 16)
            load_chunk(sp, 4, 0, chunk_in[4])
            for c in range(5, 8):
                if c < 7:
                    is_filled(sp, "op21")
                else:
                    sp.wait_ge(s0_stored, 16)
                load_chunk(sp, c, 0, chunk_in[c])
            with sp.Fori(0, PAIRS // 2 - 1) as i:
                for c in range(2 * CPP):
                    cc = (c + RING) % (2 * CPP)
                    e = i * 4 + 4 * ((c + RING) // (2 * CPP)) + 2 * (cc // CPP)
                    sp.wait_ge(chunk_used, i * (2 * CPP) + c + 1)
                    load_chunk(sp, cc, e, chunk_in[cc])
            last = (PAIRS // 2 - 1) * 2 * CPP
            for c in range(2 * CPP - RING):
                cc = c + RING
                sp.wait_ge(chunk_used, last + c + 1)
                load_chunk(sp, cc, E - 4 + 2 * (cc // CPP), chunk_in[cc])
            sp.wait_ge(chunk_used, NCH)
            sp.dma_start(wpg, d["w_ple_gate"][0].rearrange("(k p) f -> p k f", p=P)).then_inc(wpg_in, 16)
            sp.nop().then_inc(ov_used, OV_CHUNKS)
            sp.wait_ge(v_mark, VM["table"])
            n_ov = sp.value_load(ov_n[0:1, 0:1], min_val=0, max_val=OV_MAX)
            with sp.Fori(0, OV_MAX) as j:
                with sp.If(j < n_ov):
                    e = sp.value_load(ov_e[0:1, bass.ds(j, 1)], min_val=0, max_val=E - 1)
                    for c in range(OV_CHUNKS):
                        sp.wait_ge(ov_used, j * OV_CHUNKS + c + 1)
                        sp.dma_start(ring[:, c, :].rearrange("p (k f) -> p k f", k=4), ov_chunk(e, c)
                                     ).then_inc(ovch_in[c], 16)
            sp.wait_ge(v_mark, VM["moe_done"])
            for t, (t0, n) in enumerate(TILES):
                src = d["p_prompt"][0, 0, t0:t0 + n] if t < 2 else d["p_sample"][0].rearrange("b s d -> (b s) d")
                sp.dma_start(pin[0:n, t, :], src).then_inc(tail_in, 16)
            sp.dma_start(wple, d["w_ple"][0].rearrange("(k p) f -> p k f", p=P)).then_inc(tail_in, 16)
            sp.dma_start(fnb, d["final_norm"].rearrange("(a f) -> a f", a=1).broadcast_to([P, D_MODEL])
                         ).then_inc(tail_in, 16)
            for t, (t0, n) in enumerate(TILES):
                sp.wait_ge(v_mark, VM[f"yout{t}"])
                dst = o[0][0, t0:t0 + n] if t < 2 else o[1].rearrange("b s d -> (b s) d")
                sp.dma_start(dst, h3[0:n, t, :]).then_inc(out_done, 16)
            sp.wait_ge(out_done, 16 * NT)
            sp.wait_ge(pool_stored, 16)
            sp.wait_ge(ssm_stored, 16)

        @block.gpsimd
        def _(pool):
            step = chain(pool, g_step)
            g = nc.gpsimd
            step(g.memset(ident[:, :], 0.0))
            step(g.affine_select(out=ident[:, :], in_=ident[:, :], compare_op=ALU.not_equal, fill=1.0, base=0,
                                 pattern=[[-1, P]], channel_multiplier=1), consts)
            for c in range(PG):
                g.memset(ue[:, c, 0:PH], 0.0).then_inc(ext_zero, 1)
            for c in range(QKV_T):
                g.memset(qe[:, c, 0:CH], 0.0).then_inc(ext_zero, 1)
            step(g.memset(ones[:, :], 1.0), consts)
            step(g.iota(iti[:, :], pattern=[[1, P]], base=0, channel_multiplier=0))
            step(g.tensor_copy(iotaf[:, :], iti[:, :]))
            for m, b in ((causal, 0), (strict, -1)):
                step(g.memset(m[:, :], 1.0))
                step(g.affine_select(out=m[:, :], in_=m[:, :], compare_op=ALU.is_ge, fill=0.0, base=b,
                                     pattern=[[1, P]], channel_multiplier=-1))
            step(g.memset(seg[:, :], 1.0))
            sv = seg[:, :].rearrange("p (b s) -> p b s", b=DB)
            step(g.affine_select(out=sv, in_=sv, compare_op=ALU.is_ge, fill=0.0, base=0,
                                 pattern=[[-DS, DB], [0, DS]], channel_multiplier=1))
            step(g.affine_select(out=sv, in_=sv, compare_op=ALU.is_ge, fill=0.0, base=DS - 1,
                                 pattern=[[DS, DB], [0, DS]], channel_multiplier=-1))
            step(g.tensor_tensor(segcausal[:, :], causal[0:NSAMP, 0:NSAMP], seg[:, :], ALU.mult))
            step(g.memset(lmask[:, :, :], 0.0))
            v0 = lmask[:, 0, :].rearrange("p (b h s) -> p b h s", h=2, s=1)[:, :, 1, :]
            step(g.affine_select(out=v0, in_=v0, compare_op=ALU.not_equal, fill=1.0, base=0,
                                 pattern=[[-2, P // 2], [0, 1]], channel_multiplier=1))
            for s in range(1, LEVELS):
                z = 1 << s
                nb = P // (2 * z)
                vs = lmask[:, s, :].rearrange("p (b h s) -> p b h s", h=2, s=z)[:, :, 0, :]
                step(g.memset(vs, 1.0))
                step(g.affine_select(out=vs, in_=vs, compare_op=ALU.is_ge, fill=0.0, base=-z,
                                     pattern=[[-2 * z, nb], [0, z]], channel_multiplier=1))
                step(g.affine_select(out=vs, in_=vs, compare_op=ALU.is_ge, fill=0.0, base=2 * z - 1,
                                     pattern=[[2 * z, nb], [0, z]], channel_multiplier=-1))
            step(g.memset(rank[:, E:EPAD, :], -1.0))
            step(g.memset(gate[:, E:EPAD, :], 0.0), consts)
            pool.wait_ge(h_ready, NT)
            is_drained(pool, "sc")
            for c in [4, 5, 6, 7, 0, 1, 2, 3, 8, 9, 10, 11]:
                is_drained(pool, f"pr{c + 4}")
                step(g.tensor_copy(clast[:, c, :].rearrange("p (b r) -> p b r", b=DB),
                                   sample_cols(qe, c, CH, DS, CH)), packed)
            is_drained(pool, "sp")
            for c in range(PG):
                is_drained(pool, f"pr{c}")
                step(g.tensor_copy(ulast[:, c, :].rearrange("p (b r) -> p b r", b=DB),
                                   sample_cols(ue, c, PH)), packed)
            for c in range(PG):
                if c:
                    pool.wait_ge(acc_pool, c)
                src = ue[:, c, :]
                for k in range(c + 1):
                    off = 1 << k
                    dst = (ptmp[:, :], ptmp2)[(c - k) % 2]
                    step(g.tensor_copy(dst[:, 0:off], src[:, 0:off]))
                    step(g.tensor_tensor(dst[:, off:UEW], src[:, off:UEW], src[:, 0:UEW - off], ALU.add),
                         g_ready if k == c else None)
                    src = dst
            pool.wait_ge(s0_in, 16)
            is_drained(pool, "egs")
            is_filled(pool, "kqs")
            for h in range(HEADS):
                step(g.tensor_tensor(s0[:, :, h, :], s0[:, :, h, :],
                                     egs[:, h, :].unsqueeze(2).broadcast_to([P, DB, P]), ALU.mult), g_ready)

        @block.scalar
        def _(act):
            step = chain(act, a_step)
            a = nc.scalar

            rooted = [0]

            def root(ap):
                rooted[0] += 1
                act.wait_ge(inv_ready, rooted[0])
                step(a.activation(ap, ap, ACT.Sqrt), root_ready)

            def copy(out, in_, name):
                is_filled(act, name)
                step(a.activation(out, in_, ACT.Copy), dsem(name), uses[name][1] + 1)

            for t, (t0, n) in enumerate(TILES):
                act.wait_ge(x_in[t], 16)
                act.wait_ge(small_zero, 1)
                step(a.activation(h3[0:n, t, :], x3[0:n, t, :], ACT.Square, accum_out=ss[0:n, t:t + 1]),
                     a_mark if t == NT - 1 else None, AM["ss"] if t == NT - 1 else None)
            root(rstd[:, :])
            copy(vecs[:, :], bank("vec")[:, 0:77], "vec")
            act.wait_ge(ext_zero, PG + QKV_T)
            is_filled(act, "sc")
            scv = bank("sc")[:, 0:QKV_T * DB * CH].rearrange("p (c b r) -> p c b r", c=QKV_T, b=DB)
            for c in range(QKV_T):
                ins = a.activation(sample_cols(qe, c, CH, 0, CH), scv[:, c], ACT.Copy)
                step(ins, dsem("sc") if c == QKV_T - 1 else None, uses["sc"][1] + 1)
            is_filled(act, "sp")
            spv = bank("sp")[:, 0:PG * DB * PH].rearrange("p (c b r) -> p c b r", c=PG, b=DB)
            for c in range(PG):
                ins = a.activation(sample_cols(ue, c, PH, 0, PH), spv[:, c], ACT.Copy)
                step(ins, dsem("sp") if c == PG - 1 else None, uses["sp"][1] + 1)

            def silu_conv(c):
                act.wait_ge(acc_ready, convord[c] + 1)
                step(a.activation(ct[:, c, :], ct[:, c, :], ACT.Silu), ct_ready)

            def square(c):
                if c >= 2:
                    is_filled(act, f"ss{c - 2}")
                step(a.activation(sqb[c % 2], ct[:, c, :], ACT.Square), sq_ready)

            prev = []
            for b in IN_ORDER:
                for c in range(4 * b, 4 * b + 4):
                    name = f"pr{c}"
                    is_filled(act, name)
                    src = bank(name)
                    if b == 4:
                        step(a.activation(zT[:, c - 16, :], src[:, 0:T], ACT.Silu), dsem(name), uses[name][1] + 1)
                        continue
                    v, cc, hist = (ue, c, PH) if b == 0 else (qe, c - 4, CH)
                    step(a.activation(prompt_cols(v, cc, hist), src[:, 0:SEQ], ACT.Copy))
                    step(a.activation(sample_cols(v, cc, hist), src[:, SEQ:T].rearrange("p (b s) -> p b s", b=DB),
                                      ACT.Copy), dsem(name), uses[name][1] + 1)
                    if prev:
                        silu_conv(prev.pop(0))
                    if b:
                        prev.append(cc)
                if b == 1:
                    silu_conv(prev.pop(0))
                    for c in range(8 + 1):
                        if c < 8:
                            square(c)
                        if c:
                            root(rnb[(c - 1) % 3])
            assert not prev
            act.wait_ge(v_mark, VM["ba"])
            step(a.activation(beta[:, :, :], beta[:, :, :], ACT.Exp, scale=-1.0), a_mark, AM["exps"])
            act.wait_ge(smalls_in, 64)
            step(a.activation(alog, alog, ACT.Exp), a_mark, AM["ea"])
            act.wait_ge(v_mark, VM["sp_in"])
            step(a.activation(tmp12[:, :, :], tmp12[:, :, :], ACT.Exp, scale=-1.0))
            step(a.activation(tmp12[:, :, :], tmp12[:, :, :], ACT.Ln, bias=1.0), a_mark, AM["lg"])
            for i in range(3):
                copy(outrow[0:CH, i * 512:(i + 1) * 512], bank(f"cnp{i}")[0:CH, :], f"cnp{i}")
            for i in range(3):
                copy(outrow[0:DB * CH, 1536 + i * 512:2048 + i * 512], bank(f"cns{i}")[0:DB * CH, :], f"cns{i}")
            copy(outrow[0:PH, 3072:3584], bank("npp")[0:PH, :], "npp")
            copy(outrow[0:NSAMP, 3584:4096], bank("nps")[0:NSAMP, :], "nps")
            act.dma_start(o[3][0, 0], outrow[0:CH, 0:1536]).then_inc(hist_stored, 16)
            act.dma_start(o[6][0].rearrange("b r c -> (b r) c"), outrow[0:DB * CH, 1536:3072]).then_inc(hist_stored, 16)
            act.dma_start(o[2][0, 0], outrow[0:PH, 3072:3584]).then_inc(hist_stored, 16)
            act.dma_start(o[5][0, :, PH - DS:PH, :], outrow[0:NSAMP, 3584:4096]).then_inc(hist_stored, 16)
            act.dma_start(o[5][0, :, 0:PH - DS, :], d["state_pool"][0, :, DS:PH, :]).then_inc(pool_stored, 16)
            for t, (t0, n) in enumerate(TILES):
                copy(kN[0:n, t], bank(f"kN{t}")[0:n, :].rearrange("p (h d) -> p h d", h=HEADS), f"kN{t}")
            for t, (t0, n) in enumerate(TILES):
                copy(vN[0:n, t], bank(f"vN{t}")[0:n, :].rearrange("p (h d) -> p h d", h=HEADS), f"vN{t}")
            act.wait_ge(v_mark, VM["gcs"])
            step(a.activation(egc[:, :, :], gc[:, :, :], ACT.Exp))
            step(a.activation(kdec[:, :, :], kdec[:, :, :], ACT.Exp))
            step(a.activation(egl[:, :, :], egl[:, :, :], ACT.Exp), a_mark, AM["gexp"])
            is_filled(act, "egs")
            step(a.activation(egs[:, :, :], bank("egs")[:, 0:HEADS * DB].rearrange("p (h b) -> p h b", h=HEADS),
                              ACT.Exp), dsem("egs"), uses["egs"][1] + 1)
            for t, (t0, n) in enumerate(TILES):
                act.wait_ge(v_mark, VM[f"diff{t}"])
                step(a.activation(scratch[t][0], scratch[t][0], ACT.Exp), a_mark, AM[f"E{t}"])
            root(tmp12[:, :, :])
            act.wait_ge(v_mark, VM["S2"])
            act.dma_start(o[4][0, 0].rearrange("h d e -> d h e"), S1).then_inc(ssm_stored, 16)
            act.wait_ge(v_mark, VM["S0"])
            act.dma_start(o[7][0].rearrange("b h d e -> d b h e"), s0).then_inc(s0_stored, 16)
            act.wait_ge(v_mark, VM["x2"])
            for t, (t0, n) in enumerate(TILES):
                step(a.activation(h3[0:n, t, :], x3[0:n, t, :], ACT.Square, accum_out=ss[0:n, t:t + 1]),
                     a_mark if t == NT - 1 else None, AM["ss2"] if t == NT - 1 else None)
            root(rstd[:, :])
            is_filled(act, "lg")
            step(a.activation(logT, bank("lg")[0:E, 0:T], ACT.Identity, bias=rb), dsem("lg"), uses["lg"][1] + 1)
            act.wait_ge(v_mark, VM["m8"])
            step(a.activation(exq[:, :, :], exq[:, :, :], ACT.Exp), a_mark, AM["exq"])
            copy(GT[:, :, :], bank("GT")[0:E, 0:NT * P].rearrange("p (t s) -> p t s", t=NT), "GT")
            copy(xg[:, 0:512], bank("g0a"), "g0a")
            copy(xg[:, 512:1024], bank("g0b"), "g0b")
            copy(SgT[0][:, :, :], bank("sgt0")[:, 0:384].rearrange("p (t s) -> p t s", t=NT), "sgt0")

            NSTEP = 8
            with act.Fori(0, PAIRS // 2) as i:
                for half in range(2):
                    n0 = [0]

                    def lstep(ins, s, v):
                        ins.then_inc(s, 1)
                        act.wait_ge(s, v)

                    def aux(k, out, in_):
                        l = 13 * half + k
                        b, m = 6 + l % 2, l // 2
                        act.wait_ge(filled[b], base[b] + 1 + m + i * 13)
                        lstep(a.activation(out, in_, ACT.Copy), drained[b], base[b] + 1 + m + i * 13)

                    act.wait_ge(g_act, i * 2 + half + 2)
                    lstep(a.activation(sbuf_, gbuf, ACT.Sigmoid, scale=ALPHA), sig_act, i * 2 + half + 1)
                    aux(0, xg[:, 0:512], PS[:, 6 + (13 * half) % 2, :])
                    aux(1, xg[:, 512:1024], PS[:, 6 + (13 * half + 1) % 2, :])
                    aux(8, hidf[:, 0:512], PS[:, 6 + (13 * half + 8) % 2, :])
                    aux(9, hidf[:, 512:1024], PS[:, 6 + (13 * half + 9) % 2, :])
                    aux(10, SgT[1 - half][:, :, :],
                        PS[:, 6 + (13 * half + 10) % 2, 0:384].rearrange("p (t s) -> p t s", t=NT))
                    act.wait_ge(chunk_used, i * (2 * CPP) + (half + 1) * CPP)
                    lstep(a.activation(ybuf, PS[:, 4:6, :].rearrange("p b f -> p (b f)"), ACT.Copy),
                          y_act, i * 2 + half + 2)
            act.wait_ge(v_mark, VM["table"])
            n_ov = act.value_load(ov_n[0:1, 0:1], min_val=0, max_val=OV_MAX)
            with act.Fori(0, OV_MAX) as j:
                with act.If(j < n_ov):
                    def ovaux(k, out, in_):
                        b, m = 6 + k % 2, k // 2
                        act.wait_ge(filled[b], ovbase[b] + 1 + m + j * 7)
                        ins = a.activation(out, in_, ACT.Copy)
                        ins.then_inc(drained[b], 1)
                        act.wait_ge(drained[b], ovbase[b] + 1 + m + j * 7)
                    ovaux(0, xg[:, 0:512], PS[:, 6, :])
                    ovaux(1, xg[:, 512:1024], PS[:, 7, :])
                    act.wait_ge(ovg_act, j + 1)
                    a.activation(sbuf_, gbuf, ACT.Sigmoid, scale=ALPHA).then_inc(ovs_act, 1)
                    ovaux(4, hidf[:, 0:512], PS[:, 6, :])
                    ovaux(5, hidf[:, 512:1024], PS[:, 7, :])
                    ovaux(6, SgT[0][:, 0:2, :], PS[:, 6, 0:256].rearrange("p (t s) -> p t s", t=2))
                    ovaux(7, SgT[0][:, 2, :], PS[:, 7, 0:128])
                    act.wait_ge(ov_used, j * OV_CHUNKS + 2 * OV_CHUNKS)
                    a.activation(ybuf, PS[:, 4:6, :].rearrange("p b f -> p (b f)"), ACT.Copy).then_inc(ovy_act, 1)
            act.wait_ge(v_mark, VM["moe_done"])
            for t, (t0, n) in enumerate(TILES):
                step(a.activation(h3[0:n, t, :], x3[0:n, t, :], ACT.Square, accum_out=ss[0:n, t:t + 1]),
                     a_mark if t == NT - 1 else None, AM["ss3"] if t == NT - 1 else None)
            root(rstd[:, :])
            copy(pT[:, 0, :], bank("pT0")[:, 0:T], "pT0")
            copy(pT[:, 1, :], bank("pT1")[:, 0:T], "pT1")
            for t, (t0, n) in enumerate(TILES):
                for hf in range(2):
                    nm = f"pg{t}{hf}"
                    is_filled(act, nm)
                    step(a.activation(sg3[0:n, t, hf * 512:(hf + 1) * 512], bank(nm)[0:n, :], ACT.Sigmoid),
                         dsem(nm), uses[nm][1] + 1)
            for t, (t0, n) in enumerate(TILES):
                act.wait_ge(v_mark, VM[f"y{t}"])
                step(a.activation(h3[0:n, t, :], x3[0:n, t, :], ACT.Square, accum_out=ss[0:n, t:t + 1]),
                     a_mark, AM[f"ss4{t}"])
                root(rstd[0:n, t:t + 1])

        @block.tensor
        def _(pe):
            mm = nc.tensor.matmul
            seen = [0] * 8

            def fill(name):
                b, k = uses[name]
                assert k == seen[b], (name, k, seen[b])
                seen[b] += 1
                can_fill(pe, name)
                return PS[:, b, :]

            def tr(out, in_):
                n = in_.shape[0]
                return nc.tensor.transpose(out, in_, ident[0:n, 0:n])

            pe.wait_ge(consts, 1)
            pe.wait_ge(vecs_in, 16 * 6)
            tr(fill("vec")[:, 0:77], vrows).then_inc(fsem("vec"), 1)
            pe.wait_ge(hist_in, 32)
            ps = fill("sc")
            for c in range(QKV_T):
                last = tr(ps[:, c * 24:(c + 1) * 24], st_conv[:, c * P:(c + 1) * P])
            last.then_inc(fsem("sc"), 1)
            ps = fill("sp")
            for c in range(PG):
                last = tr(ps[:, c * 120:(c + 1) * 120], st_pool[:, c * P:(c + 1) * P])
            last.then_inc(fsem("sp"), 1)

            def transposes(prefix):
                for t, (t0, n) in enumerate(TILES):
                    for hf in range(2):
                        ps = fill(f"{prefix}{t}{hf}")
                        for k in range(4):
                            c0 = (hf * 4 + k) * P
                            last = tr(ps[:, k * n:(k + 1) * n], h3[0:n, t, c0:c0 + P])
                        last.then_inc(fsem(f"{prefix}{t}{hf}"), 1)

            pe.wait_ge(h_ready, NT)
            transposes("hT")
            for t in range(NT):
                for hf in range(2):
                    is_drained(pe, f"hT{t}{hf}")
            pe.wait_ge(wtail_in, 16)
            ps = fill("ba")
            for t, (t0, n) in enumerate(TILES):
                for k in range(KT):
                    last = mm(ps[0:n, t * 8:(t + 1) * 8], hT[:, k, t0:t0 + n], wtail[:, k, :],
                              start=(k == 0), stop=(k == KT - 1))
            last.then_inc(fsem("ba"), 1)
            for i, b in enumerate(IN_ORDER):
                pe.wait_ge(win_in[i], 16)
                w = ring[:, i, :].rearrange("p (k c) -> p k c", k=KT)
                for c in range(4):
                    name = f"pr{4 * b + c}"
                    ps = fill(name)
                    for k in range(KT):
                        last = mm(ps[:, 0:T], w[:, k, c * P:(c + 1) * P], hT[:, k, :], start=(k == 0), stop=(k == KT - 1))
                    last.then_inc(fsem(name), 1)
                is_filled(pe, f"pr{4 * b + 3}")
                pe.nop().then_inc(win_used, 1)
                if b == 1:
                    pe.wait_ge(consts, 2)
                    for c in range(8):
                        ps = fill(f"ss{c}")
                        pe.wait_ge(sq_ready, c + 1)
                        mm(ps[:, 0:T], ones[:, :], sqb[c % 2], start=True, stop=True).then_inc(fsem(f"ss{c}"), 1)
            for i in range(3):
                ps = fill(f"cnp{i}")
                for c in range(4):
                    last = tr(ps[0:CH, c * P:(c + 1) * P], qe[:, 4 * i + c, SEQ:SEQ + CH])
                last.then_inc(fsem(f"cnp{i}"), 1)
            pe.wait_ge(packed, QKV_T + PG)
            for i in range(3):
                ps = fill(f"cns{i}")
                for c in range(4):
                    last = tr(ps[0:DB * CH, c * P:(c + 1) * P], clast[:, 4 * i + c, :])
                last.then_inc(fsem(f"cns{i}"), 1)
            ps = fill("npp")
            for c in range(PG):
                last = tr(ps[0:PH, c * P:(c + 1) * P], ue[:, c, SEQ:SEQ + PH])
            last.then_inc(fsem("npp"), 1)
            ps = fill("nps")
            for c in range(PG):
                last = tr(ps[0:NSAMP, c * P:(c + 1) * P], ulast[:, c, :])
            last.then_inc(fsem("nps"), 1)
            pe.wait_ge(norm_ready, 8)
            pe.wait_ge(ct_ready, QKV_T)
            for pre, c0 in (("kN", 4), ("vN", 8)):
                for t, (t0, n) in enumerate(TILES):
                    ps = fill(f"{pre}{t}")
                    for h in range(HEADS):
                        last = tr(ps[0:n, h * P:(h + 1) * P], ct[:, c0 + h, t0:t0 + n])
                    last.then_inc(fsem(f"{pre}{t}"), 1)
            pe.wait_ge(poolw_in, 16)
            for g in range(PG):
                pe.wait_ge(d_ready, g + 1)
                ps = fill(f"pm{g}")
                mm(ps[:, 0:SEQ], poolw[:, g, :], prompt_cols(ue, g, PH), start=True, stop=True)
                mm(ps[:, SEQ:T], poolw[:, g, :], sample_cols(ue, g, PH), start=True, stop=True
                   ).then_inc(fsem(f"pm{g}"), 1)
            pe.wait_ge(consts, 3)
            pe.wait_ge(v_mark, VM["g"])
            ps = fill("gcs")
            for t, (L, one, t0, n) in enumerate(tilepart):
                mm(ps[0:n, t * 4:t * 4 + 4], L[0:n, 0:n], gl[0:n, t, :], start=True, stop=True)
                last = mm(ps[0:n, 12 + t * 4:16 + t * 4], one[0:n, 0:n], gl[0:n, t, :], start=True, stop=True)
            last.then_inc(fsem("gcs"), 1)
            ps = fill("egs")
            for h in range(HEADS):
                last = mm(ps[:, h * DB:(h + 1) * DB], gl[0:NSAMP, 2, h:h + 1].broadcast_to([NSAMP, P]),
                          seg[:, 0:NSAMP:DS], start=True, stop=True)
            last.then_inc(fsem("egs"), 1)

            def per_head(name, n, m, lhs, rhs, rows=None):
                ps = fill(name)
                for h in range(HEADS):
                    last = mm(ps[0:n, h * m:(h + 1) * m], lhs(h), rhs(h), start=True, stop=True)
                last.then_inc(fsem(name), 1)

            for t, (L, one, t0, n) in enumerate(tilepart):
                per_head(f"G{t}", n, n, lambda h: gl[0:n, t, h:h + 1].broadcast_to([n, n]), lambda h: L[0:n, 0:n])
                per_head(f"kk{t}", n, n, lambda h: ct[:, 4 + h, t0:t0 + n], lambda h: ct[:, 4 + h, t0:t0 + n])
                per_head(f"qk{t}", n, n, lambda h: ct[:, 4 + h, t0:t0 + n], lambda h: ct[:, h, t0:t0 + n])
            for t, (t0, n) in enumerate(TILES):
                pe.wait_ge(v_mark, VM[f"U{t}"])
                ps = fill(f"T{t}")
                for h in range(HEADS):
                    last = tr(ps[0:n, h * n:(h + 1) * n], scratch[t][3][:, h, :])
                last.then_inc(fsem(f"T{t}"), 1)
            for s in range(1, LEVELS):
                ts = [t for t in range(NT) if t < 2 or s < 3]
                for t in ts:
                    n = TILES[t][1]
                    sc = scratch[t]
                    if s == 1:
                        is_drained(pe, f"T{t}")
                    else:
                        is_drained(pe, f"QT{s - 1}{t}")
                    per_head(f"P{s}{t}", n, n, lambda h: sc[2][:, h, :], lambda h: sc[4][:, h, :])
                for t in ts:
                    n = TILES[t][1]
                    sc = scratch[t]
                    is_drained(pe, f"P{s}{t}")
                    if f"Q{s}{t}" in uses:
                        per_head(f"Q{s}{t}", n, n, lambda h: sc[3][:, h, :], lambda h: sc[5][:, h, :])
                    per_head(f"QT{s}{t}", n, n, lambda h: sc[5][:, h, :], lambda h: sc[3][:, h, :])
            pe.wait_ge(v_mark, VM["kd"])
            is_drained(pe, f"QT{LEVELS - 1}0")
            per_head("v0", P, P, lambda h: scratch[0][3][:, h, :], lambda h: vN[:, 0, h, :])
            is_drained(pe, "v0")
            per_head("S1", P, P, lambda h: kN[:, 0, h, :], lambda h: vN[:, 0, h, :])
            per_head("o0", P, P, lambda h: scratch[0][1][:, h, :], lambda h: vN[:, 0, h, :])
            ps = fill("kqs").rearrange("p (h q t) -> p h q t", h=HEADS, q=2)
            pe.wait_ge(s0_in, 16)
            for h in range(HEADS):
                for b in range(DB):
                    c = SEQ + b * DS
                    last = mm(ps[:, h, :, b * DS:(b + 1) * DS], s0[:, b, h, :], ct[:, h:h + 5:4, c:c + DS],
                              start=True, stop=True)
            last.then_inc(fsem("kqs"), 1)
            is_drained(pe, "S1")
            per_head("kS1", P, P, lambda h: ct[:, 4 + h, P:SEQ], lambda h: S1[:, h, :])
            per_head("qS1", P, P, lambda h: ct[:, h, P:SEQ], lambda h: S1[:, h, :])
            is_drained(pe, "kqs")
            for nm, q in (("R2k", 1), ("R2q", 0)):
                ps = fill(nm)
                for h in range(HEADS):
                    last = tr(ps[0:NSAMP, h * P:(h + 1) * P], kqS[:, h, q * NSAMP:(q + 1) * NSAMP])
                last.then_inc(fsem(nm), 1)
            is_drained(pe, "kS1")
            per_head("v1", P, P, lambda h: scratch[1][3][:, h, :], lambda h: vN[:, 1, h, :])
            is_drained(pe, "R2k")
            per_head("v2", NSAMP, P, lambda h: scratch[2][3][:, h, :], lambda h: vN[0:NSAMP, 2, h, :])
            is_drained(pe, "v1")
            per_head("o1", P, P, lambda h: scratch[1][1][:, h, :], lambda h: vN[:, 1, h, :])
            per_head("S2", P, P, lambda h: kN[:, 1, h, :], lambda h: vN[:, 1, h, :])
            is_drained(pe, "v2")
            per_head("o2", NSAMP, P, lambda h: scratch[2][1][:, h, :], lambda h: vN[0:NSAMP, 2, h, :])
            pe.wait_ge(v_mark, VM["rs_o"])
            for t, (t0, n) in enumerate(TILES):
                ps = fill(f"oT{t}")
                for h in range(HEADS):
                    last = tr(ps[:, h * n:(h + 1) * n], oN[t][0:n, h, :])
                last.then_inc(fsem(f"oT{t}"), 1)
            for h in range(HEADS):
                pe.wait_ge(v_mark, VM[f"vm{h}"])
                for q in range(2):
                    nm = f"ns{h}{'ab'[q]}"
                    mm(fill(nm), kN[0:NSAMP, 2, h, :],
                       vmask[:, 4 * q:4 * q + 4, :].rearrange("p b d -> p (b d)"), start=True, stop=True
                       ).then_inc(fsem(nm), 1)
            pe.wait_ge(wout_in, 32)
            wo = ring[:, 5:7, :].rearrange("p s (k f) -> p (s k) f", k=4)
            for t in range(NT):
                is_drained(pe, f"oT{t}")
            for g in range(PG):
                is_drained(pe, f"pm{g}")
            for t, (t0, n) in enumerate(TILES):
                for hf in range(2):
                    ps = fill(f"op{t}{hf}")
                    for k in range(KT):
                        last = mm(ps[0:n, :], hT[:, k, t0:t0 + n], wo[:, k, hf * 512:(hf + 1) * 512],
                                  start=(k == 0), stop=(k == KT - 1))
                    last.then_inc(fsem(f"op{t}{hf}"), 1)
            pe.wait_ge(v_mark, VM["h2"])
            transposes("rT")
            pe.wait_ge(smalls_in, 64)
            for t in range(NT):
                for hf in range(2):
                    is_drained(pe, f"rT{t}{hf}")
            ps = fill("lg")
            for k in range(KT):
                last = mm(ps[0:E, 0:T], wrout[:, k, :], hT[:, k, :], start=(k == 0), stop=(k == KT - 1))
            last.then_inc(fsem("lg"), 1)
            is_drained(pe, "lg")
            ps = fill("lgT")
            for t, (t0, n) in enumerate(TILES):
                last = tr(ps[0:n, t * E:(t + 1) * E], logT[:, t0:t0 + n])
            last.then_inc(fsem("lgT"), 1)
            pe.wait_ge(v_mark, VM["sel"])
            ps = fill("rk")
            for t in range(NT):
                for u in range(t):
                    mm(ps[:, t * E:(t + 1) * E], ones[:, :], sel[:, u, :], start=(u == 0), stop=False)
                mm(ps[:, t * E:(t + 1) * E], strict[:, :], sel[:, t, :], start=(t == 0), stop=True)
            for u in range(NT):
                last = mm(ps[:, NT * E:(NT + 1) * E], ones[:, :], sel[:, u, :], start=(u == 0), stop=(u == NT - 1))
            last.then_inc(fsem("rk"), 1)
            pe.wait_ge(v_mark, VM["gates"])
            ps = fill("GT")
            for t in range(NT):
                last = tr(ps[0:E, t * P:(t + 1) * P], gate[:, 0:E, t])
            last.then_inc(fsem("GT"), 1)

            def gather(k0, fills, s_ready):
                for hf in range(2):
                    ps, sm_ = fills(k0 + hf)
                    for t in range(NT):
                        last = mm(ps, Ssel[:, t, :], h3[:, t, hf * 512:(hf + 1) * 512], start=(t == 0), stop=(t == NT - 1))
                    last.then_inc(sm_, 1)

            def turn(k0, fills, src):
                for hf in range(2):
                    ps, sm_ = fills(k0 + hf)
                    for k in range(4):
                        c0 = (hf * 4 + k) * P
                        last = tr(ps[:, k * P:(k + 1) * P], src[:, c0:c0 + P])
                    last.then_inc(sm_, 1)

            is_drained(pe, "GT")
            pe.wait_ge(bias_in, 48)
            for t, (t0, n) in enumerate(TILES):
                for hf in range(2):
                    mm(fill(f"bd{t}{hf}")[0:n, :], GT[:, t, 0:n], bdn[:, hf * 512:(hf + 1) * 512],
                       start=True, stop=True).then_inc(fsem(f"bd{t}{hf}"), 1)
            pe.wait_ge(pair_sel, 1)
            names = ["g0a", "g0b", "xt0a", "xt0b", "sgt0"]
            gather(0, lambda k: (fill(names[k]), fsem(names[k])), None)
            is_drained(pe, "g0a"), is_drained(pe, "g0b")
            turn(2, lambda k: (fill(names[k]), fsem(names[k])), xg)
            ps = fill("sgt0")
            for t in range(NT):
                last = tr(ps[:, t * P:(t + 1) * P], Sgat[:, t, :])
            last.then_inc(fsem("sgt0"), 1)
            is_drained(pe, "xt0b")
            is_drained(pe, "xt0a"), is_drained(pe, "sgt0")
            assert seen == base, (seen, base)

            for s in (g_act, up_act, y_act):
                pe.nop().then_inc(s, 1)
            with pe.Fori(0, PAIRS // 2) as i:
                for half in range(2):
                    pair = i * 2 + half

                    def aux(k):
                        l = 13 * half + k
                        b, m = 6 + l % 2, l // 2
                        pe.wait_ge(drained[b], base[b] + m + i * 13)
                        return PS[:, b, :], filled[b]

                    def product(c0, b0, lhs, bias):
                        if bias is not None:
                            for hf in range(2):
                                mm(PS[:, b0 + hf, :], ind[:, half, :], bgu[:, bias, hf * 512:(hf + 1) * 512],
                                   start=True, stop=False, skip_group_check=True)
                        for c in range(c0, c0 + CPM):
                            pe.wait_ge(chunk_in[half * CPP + c], i * 32 + 32)
                            w = slot(half * CPP + c)
                            for kk in range(2):
                                k = (c - c0) * 2 + kk
                                for hf in range(2):
                                    for a_ in range(2):
                                        last = mm(PS[64 * a_:64 * a_ + 64, b0 + hf, :], lhs[:, k, 64 * a_:64 * a_ + 64],
                                                  w[:, a_, kk, hf * 512:(hf + 1) * 512],
                                                  start=(bias is None and k == 0), stop=(k == KT - 1),
                                                  skip_group_check=True)
                            last.then_inc(chunk_used, 1)

                    pe.wait_ge(pair_sel, pair + 1)
                    pe.wait_ge(drained[6], base[6] + i * 13 + 7 * half)
                    pe.wait_ge(drained[7], base[7] + i * 13 + 6 * half)
                    pe.wait_ge(g_act, pair + 1)
                    product(0, 0, xgT, 0)
                    pe.wait_ge(up_act, pair + 1)
                    product(CPM, 2, xgT, 1)
                    pe.wait_ge(pair_sel, pair + 2)
                    gather(0, aux, None)
                    pe.wait_ge(y_act, pair + 1)
                    for t, (t0, n) in enumerate(TILES):
                        for hf in range(2):
                            ps, sm_ = aux(2 + 2 * t + hf)
                            mm(ps[0:n, :], SgT[1 - half][:, t, 0:n], ybuf[:, hf * 512:(hf + 1) * 512],
                               start=True, stop=True).then_inc(sm_, 1)
                    pe.wait_ge(hid_act, pair + 1)
                    turn(8, aux, ubuf)
                    ps, sm_ = aux(10)
                    for t in range(NT):
                        last = tr(ps[:, t * P:(t + 1) * P], Sgat[:, t, :])
                    last.then_inc(sm_, 1)
                    turn(11, aux, xg)
                    product(2 * CPM, 4, hidT, None)
            pe.wait_ge(y_act, PAIRS + 1)

            def scatter(fillb, sg):
                for t, (t0, n) in enumerate(TILES):
                    for hf in range(2):
                        ps, sm_ = fillb(t * 2 + hf)
                        mm(ps[0:n, :], sg[:, t, 0:n], ybuf[:, hf * 512:(hf + 1) * 512], start=True, stop=True
                           ).then_inc(sm_, 1)

            def last_bank(k):
                b, m = 6 + k % 2, k // 2
                pe.wait_ge(drained[b], base[b] + 13 * (PAIRS // 2) + m)
                return PS[:, b, :], filled[b]
            scatter(last_bank, SgT[(PAIRS - 1) % 2])
            pe.wait_ge(v_mark, VM["table"])
            n_ov = pe.value_load(ov_n[0:1, 0:1], min_val=0, max_val=OV_MAX)
            with pe.Fori(0, OV_MAX) as j:
                with pe.If(j < n_ov):
                    def ovaux(k):
                        b, m = 6 + k % 2, k // 2
                        pe.wait_ge(drained[b], ovbase[b] + m + j * 7)
                        return PS[:, b, :], filled[b]

                    def ovproduct(c0, b0, lhs, bias):
                        if bias is not None:
                            for hf in range(2):
                                mm(PS[:, b0 + hf, :], ind[:, 0, :], bgu[:, bias, hf * 512:(hf + 1) * 512],
                                   start=True, stop=False)
                        for c in range(c0, c0 + 2):
                            pe.wait_ge(ovch_in[c], j * 16 + 16)
                            w = ring[:, c, :].rearrange("p (k f) -> p k f", k=4)
                            for kk in range(4):
                                k = (c - c0) * 4 + kk
                                for hf in range(2):
                                    last = mm(PS[:, b0 + hf, :], lhs[:, k, :], w[:, kk, hf * 512:(hf + 1) * 512],
                                              start=(bias is None and k == 0), stop=(k == KT - 1))
                            last.then_inc(ov_used, 1)

                    def ovdrained(k):
                        pe.wait_ge(drained[6 + k % 2], ovbase[6 + k % 2] + k // 2 + 1 + j * 7)

                    pe.wait_ge(ov_sel, j + 1)
                    gather(0, ovaux, None)
                    ovdrained(0), ovdrained(1)
                    turn(2, ovaux, xg)
                    ovdrained(2), ovdrained(3)
                    ovproduct(0, 0, xgT, 0)
                    ovproduct(2, 2, xgT, 1)
                    pe.wait_ge(ovh_act, j + 1)
                    turn(4, ovaux, ubuf)
                    for k, ts in ((6, (0, 1)), (7, (2,))):
                        ps, sm_ = ovaux(k)
                        for q, t in enumerate(ts):
                            last = tr(ps[:, q * P:(q + 1) * P], Sgat[:, t, :])
                        last.then_inc(sm_, 1)
                    ovdrained(4), ovdrained(5)
                    ovproduct(4, 4, hidT, None)
                    pe.wait_ge(ovy_act, j + 1)
                    ovdrained(6), ovdrained(7)
                    scatter(lambda k: ovaux(8 + k), SgT[0])
            pe.wait_ge(tail_in, 16 * 5)
            for k in range(2):
                ps = fill(f"pT{k}")
                for t, (t0, n) in enumerate(TILES):
                    last = tr(ps[:, t0:t0 + n], pin[0:n, t, k * P:(k + 1) * P])
                last.then_inc(fsem(f"pT{k}"), 1)
            pe.wait_ge(v_mark, VM["h3"])
            transposes("tT")
            for t in range(NT):
                for hf in range(2):
                    is_drained(pe, f"tT{t}{hf}")
            pe.wait_ge(wpg_in, 16)
            is_drained(pe, "pT0"), is_drained(pe, "pT1")
            for t, (t0, n) in enumerate(TILES):
                for hf in range(2):
                    cs = slice(hf * 512, (hf + 1) * 512)
                    ps = fill(f"pg{t}{hf}")
                    for k in range(KT):
                        last = mm(ps[0:n, :], hT[:, k, t0:t0 + n], wpg[:, k, cs], start=(k == 0), stop=(k == KT - 1))
                    last.then_inc(fsem(f"pg{t}{hf}"), 1)
                    ps = fill(f"pp{t}{hf}")
                    for k in range(2):
                        last = mm(ps[0:n, :], pT[:, k, t0:t0 + n], wple[:, k, cs], start=(k == 0), stop=(k == 1))
                    last.then_inc(fsem(f"pp{t}{hf}"), 1)

        @block.vector
        def _(dve):
            step = chain(dve, v_step)
            v = nc.vector
            marked = [0]
            roots = [0]

            def mark(ins, name):
                marked[0] += 1
                assert VM[name] == marked[0], (name, VM[name], marked[0])
                ins.then_inc(v_mark, 1)
                dve.wait_ge(v_mark, marked[0])

            def drain(ins, name):
                step(ins, dsem(name), uses[name][1] + 1)

            def over(ap, h, m):
                n = ap.shape[0]
                return ap.unsqueeze(2).broadcast_to([n, h, m])

            def heads(ap, m):
                n = ap.shape[0]
                return ap.unsqueeze(1).broadcast_to([n, HEADS, m])

            def rsqrt_of(ap, in_, scale, eps=EPS):
                step(v.tensor_scalar(ap, in_, scale, eps, ALU.mult, ALU.add))
                step(v.reciprocal(ap, ap), inv_ready)
                roots[0] += 1
                dve.wait_ge(root_ready, roots[0])

            step(v.memset(small[:, :], 0.0), small_zero)
            dve.wait_ge(a_mark, AM["ss"])
            rsqrt_of(rstd[:, :], ss[:, :], 1.0 / D_MODEL)
            for t, (t0, n) in enumerate(TILES):
                step(v.tensor_scalar(h3[0:n, t, :], x3[0:n, t, :], rstd[0:n, t:t + 1], None, ALU.mult), h_ready)

            def evac_hT(prefix, ln):
                for t, (t0, n) in enumerate(TILES):
                    for hf in range(2):
                        name = f"{prefix}{t}{hf}"
                        is_filled(dve, name)
                        w = vec(ln, hf * 4, 4).unsqueeze(2).broadcast_to([P, 4, n])
                        drain(v.tensor_tensor(hT[:, hf * 4:hf * 4 + 4, t0:t0 + n],
                                              bank(name)[:, 0:4 * n].rearrange("p (k t) -> p k t", k=4), w,
                                              ALU.mult), name)
            is_drained(dve, "vec")
            evac_hT("hT", "ln_mix")
            is_filled(dve, "ba")
            bav = bank("ba")[:, 0:24].rearrange("p (t c) -> p t c", t=NT)
            dve.wait_ge(smalls_in, 64)
            for t, (t0, n) in enumerate(TILES):
                step(v.tensor_tensor(tmp12[0:n, t, :], bav[0:n, t, HEADS:2 * HEADS], dtb[0:n, :], ALU.add))
                ins = v.tensor_copy(beta[0:n, t, :], bav[0:n, t, 0:HEADS])
                drain(ins, "ba") if t == NT - 1 else step(ins)
            mark(v.tensor_scalar(gl[:, :, :], tmp12[:, :, :], 0.0, None, ALU.max), "ba")
            mark(v.scalar_tensor_tensor(out=tmp12[:, :, :], in0=tmp12[:, :, :], scalar=-1.0, in1=tmp12[:, :, :],
                                        op0=ALU.mult, op1=ALU.max), "sp_in")

            def conv(c):
                is_drained(dve, f"pr{c + 4}")
                is_drained(dve, "sc")
                dve.wait_ge(ext_zero, PG + QKV_T)
                for out, col in ((ct[:, c, 0:SEQ], lambda j: qe[:, c, j:j + SEQ]),
                                 (ct[:, c, SEQ:T].rearrange("p (b s) -> p b s", b=DB),
                                  lambda j: sample_cols(qe, c, CH, j))):
                    step(v.tensor_scalar(out, col(0), vec("conv_w", c), None, ALU.mult))
                    for j in range(1, CONV):
                        ins = v.scalar_tensor_tensor(out=out, in0=col(j), scalar=vec("conv_w", j * QKV_T + c),
                                                     in1=out, op0=ALU.mult, op1=ALU.add)
                        step(ins, acc_ready if j == CONV - 1 and len(out.shape) == 3 else None)

            for c in [4, 5, 6, 7, 0, 1, 2, 3]:
                conv(c)
            for c in range(8 + 2):
                if c < 8:
                    f = float(P) if c < 4 else 1.0
                    is_filled(dve, f"ss{c}")
                    drain(v.tensor_scalar(rnb[c % 3], bank(f"ss{c}")[:, 0:T], f, f * EPS, ALU.mult, ALU.add), f"ss{c}")
                    step(v.reciprocal(rnb[c % 3], rnb[c % 3]), inv_ready)
                if c >= 2:
                    roots[0] += 1
                    dve.wait_ge(root_ready, roots[0])
                    step(v.tensor_tensor(ct[:, c - 2, :], ct[:, c - 2, :], rnb[(c - 2) % 3], ALU.mult), norm_ready)
            for c in range(8, 12):
                conv(c)
            dve.wait_ge(a_mark, AM["lg"])
            step(v.tensor_scalar(beta[:, :, :], beta[:, :, :], 1.0, None, ALU.add))
            step(v.reciprocal(beta[:, :, :], beta[:, :, :]))
            step(v.tensor_tensor(gl[:, :, :], gl[:, :, :], tmp12[:, :, :], ALU.add))
            step(v.tensor_tensor(gl[:, :, :], gl[:, :, :], alog.unsqueeze(1).broadcast_to([P, NT, HEADS]), ALU.mult))
            mark(v.tensor_scalar(gl[:, :, :], gl[:, :, :], -1.0, None, ALU.mult), "g")
            dve.wait_ge(consts, 3)
            step(v.tensor_scalar(inv16, iotaf[:, 0:16], 1.0, None, ALU.add))
            step(v.reciprocal(inv16, inv16))
            is_filled(dve, "npp"), is_filled(dve, "nps")
            for c, w in enumerate(WINDOWS):
                dve.wait_ge(g_ready, c + 1)
                pv = ptmp[:, :].unsqueeze(1)
                iv = inv16[:, 0:w]
                step(v.tensor_tensor(ptmp[:, PH:PH + w], ptmp[:, PH:PH + w], iv, ALU.mult))
                u0 = ue[:, c, PH:PH + w]
                step(v.tensor_tensor(u0, ptmp[:, PH:PH + w], u0, ALU.subtract))
                u1 = ue[:, c, PH + w:PH + SEQ]
                step(v.scalar_tensor_tensor(out=u1, in0=ptmp[:, PH + w:PH + SEQ], scalar=1.0 / w, in1=u1,
                                            op0=ALU.mult, op1=ALU.subtract))
                u2 = sample_cols(ue, c, PH)
                step(v.scalar_tensor_tensor(out=u2, in0=sample_cols(pv, 0, PH), scalar=1.0 / w, in1=u2,
                                            op0=ALU.mult, op1=ALU.subtract), d_ready)
                step(v.memset(small[:, 159:160], 0.0), acc_pool)
            is_filled(dve, "gcs")
            for t, (t0, n) in enumerate(TILES):
                step(v.tensor_copy(gc[0:n, t, :], bank("gcs")[0:n, t * 4:t * 4 + 4]))
                ins = v.tensor_copy(egl[0:n, t, :], bank("gcs")[0:n, 12 + t * 4:16 + t * 4])
                drain(ins, "gcs") if t == NT - 1 else step(ins)
            mark(v.tensor_tensor(kdec[:, :, :], egl[:, :, :], gc[:, :, :], ALU.subtract), "gcs")
            for g in range(PG):
                is_filled(dve, f"pm{g}")
                drain(v.tensor_scalar(hT[:, g, :], bank(f"pm{g}")[:, 0:T], vec("pool_scale", g), None, ALU.mult), f"pm{g}")

            def ps4(name, n, m):
                return bank(name)[0:n, 0:HEADS * m].rearrange("p (h t) -> p h t", h=HEADS)

            for t, (t0, n) in enumerate(TILES):
                D = scratch[t][0]
                is_filled(dve, f"G{t}")
                drain(v.tensor_tensor(D, ps4(f"G{t}", n, n), over(gc[0:n, t, :], HEADS, n), ALU.subtract), f"G{t}")
                mark(v.tensor_scalar(D, D, 0.0, None, ALU.min), f"diff{t}")
            for t, (L, one, t0, n) in enumerate(tilepart):
                D, At, N, Um, Tm, Pm = scratch[t]
                dve.wait_ge(a_mark, AM[f"E{t}"])
                step(v.tensor_tensor(D, D, heads(L[0:n, 0:n], n), ALU.mult))
                is_filled(dve, f"kk{t}")
                drain(v.tensor_tensor(N, ps4(f"kk{t}", n, n), D, ALU.mult), f"kk{t}")
                is_filled(dve, f"qk{t}")
                drain(v.tensor_tensor(At, ps4(f"qk{t}", n, n), D, ALU.mult), f"qk{t}")
                step(v.tensor_tensor(N, N, over(beta[0:n, t, :], HEADS, n), ALU.mult))
                step(v.tensor_tensor(Pm, N, heads(lmask[0:n, 0, 0:n], n), ALU.mult))
                mark(v.tensor_tensor(Um, heads(ident[0:n, 0:n], n), Pm, ALU.subtract), f"U{t}")
            for t, (t0, n) in enumerate(TILES):
                is_filled(dve, f"T{t}")
                drain(v.tensor_copy(scratch[t][4], ps4(f"T{t}", n, n)), f"T{t}")
            for s in range(1, LEVELS):
                ts = [t for t in range(NT) if t < 2 or s < 3]
                for t in ts:
                    n = TILES[t][1]
                    is_filled(dve, f"P{s}{t}")
                    drain(v.tensor_tensor(scratch[t][5], ps4(f"P{s}{t}", n, n), heads(lmask[0:n, s, 0:n], n), ALU.mult),
                          f"P{s}{t}")
                for t in ts:
                    n = TILES[t][1]
                    for nm, m in ((f"Q{s}{t}", 4), (f"QT{s}{t}", 3)):
                        if nm in uses:
                            is_filled(dve, nm)
                            drain(v.tensor_tensor(scratch[t][m], scratch[t][m], ps4(nm, n, n), ALU.subtract), nm)
            for t, (t0, n) in enumerate(TILES):
                is_drained(dve, f"kN{t}")
                dve.wait_ge(a_mark, AM["gexp"])
                ins = v.tensor_tensor(kN[0:n, t], kN[0:n, t], over(kdec[0:n, t, :], HEADS, P), ALU.mult)
                mark(ins, "kd") if t == NT - 1 else step(ins)

            def new_value(t, name):
                n = TILES[t][1]
                is_filled(dve, name)
                drain(v.tensor_tensor(vN[0:n, t], ps4(name, n, P), over(beta[0:n, t, :], HEADS, P), ALU.mult), name)

            new_value(0, "v0")
            is_filled(dve, "S1")
            drain(v.tensor_copy(S1, ps4("S1", P, P)), "S1")
            is_filled(dve, "kqs")
            drain(v.tensor_copy(kqS, bank("kqs").rearrange("p (h t) -> p h t", h=HEADS)), "kqs")
            is_filled(dve, "o0")
            drain(v.tensor_copy(oN[0], ps4("o0", P, P)), "o0")
            E1, T1 = scratch[1][0], scratch[1][4]
            is_filled(dve, "kS1")
            step(v.tensor_tensor(E1, ps4("kS1", P, P), over(egc[:, 1, :], HEADS, P), ALU.mult))
            drain(v.tensor_tensor(vN[:, 1], vN[:, 1], E1, ALU.subtract), "kS1")
            is_filled(dve, "qS1")
            drain(v.tensor_tensor(T1, ps4("qS1", P, P), over(egc[:, 1, :], HEADS, P), ALU.mult), "qS1")
            step(v.tensor_tensor(S1, S1, over(egl[:, 1, :], HEADS, P), ALU.mult))
            is_filled(dve, "R2k")
            step(v.tensor_tensor(oN[2], ps4("R2k", NSAMP, P), over(egc[0:NSAMP, 2, :], HEADS, P), ALU.mult))
            drain(v.tensor_tensor(vN[0:NSAMP, 2], vN[0:NSAMP, 2], oN[2], ALU.subtract), "R2k")
            is_filled(dve, "R2q")
            drain(v.tensor_tensor(qS2, ps4("R2q", NSAMP, P), over(egc[0:NSAMP, 2, :], HEADS, P), ALU.mult), "R2q")
            new_value(1, "v1")
            new_value(2, "v2")
            is_filled(dve, "o1")
            drain(v.tensor_tensor(oN[1], ps4("o1", P, P), T1, ALU.add), "o1")
            is_filled(dve, "S2")
            mark(v.tensor_tensor(S1, S1, ps4("S2", P, P), ALU.add), "S2")
            drain(v.tensor_copy(oss[:, 0:1], bank("S2")[:, 0:1]), "S2")
            is_filled(dve, "o2")
            drain(v.tensor_tensor(oN[2], ps4("o2", NSAMP, P), qS2, ALU.add), "o2")
            for t, (t0, n) in enumerate(TILES):
                sq = (scratch[0][0], scratch[1][0], ring[0:NSAMP, 4, 512:1024].rearrange("p (h d) -> p h d", h=HEADS))[t]
                step(v.tensor_tensor(sq, oN[t][0:n], oN[t][0:n], ALU.mult))
                step(v.tensor_reduce(tmp12[0:n, t, :], sq, AX_X, ALU.add))
            rsqrt_of(tmp12[:, :, :], tmp12[:, :, :], 1.0 / P)
            for t, (t0, n) in enumerate(TILES):
                ins = v.tensor_tensor(oN[t][0:n], oN[t][0:n], over(tmp12[0:n, t, :], HEADS, P), ALU.mult)
                mark(ins, "rs_o") if t == NT - 1 else step(ins)
            for t, (t0, n) in enumerate(TILES):
                is_filled(dve, f"oT{t}")
                is_drained(dve, "pr19")
                drain(v.scalar_tensor_tensor(out=hT[:, 4:8, t0:t0 + n], in0=ps4(f"oT{t}", P, n),
                                             scalar=vec("dn_norm"), in1=zT[:, :, t0:t0 + n],
                                             op0=ALU.mult, op1=ALU.mult), f"oT{t}")
            for h in range(HEADS):
                if h:
                    is_filled(dve, f"ns{h - 1}b")
                mark(v.tensor_tensor(vmask, vN[0:NSAMP, 2, h, :].unsqueeze(1).broadcast_to([NSAMP, DB, P]),
                                     seg[:, 0:NSAMP:DS].unsqueeze(2).broadcast_to([NSAMP, DB, P]), ALU.mult), f"vm{h}")
                dve.wait_ge(g_ready, PG + h + 1)
                for q in range(2):
                    nm = f"ns{h}{'ab'[q]}"
                    is_filled(dve, nm)
                    sv = s0[:, 4 * q:4 * q + 4, h, :]
                    drain(v.tensor_tensor(sv, sv, ps4(nm, P, P), ALU.add), nm)
            mark(v.memset(oss[:, 0:1], 0.0), "S0")
            dve.wait_ge(xagain_in, 16 * NT)
            for t, (t0, n) in enumerate(TILES):
                for hf in range(2):
                    nm = f"op{t}{hf}"
                    is_filled(dve, nm)
                    xs = x3[0:n, t, hf * 512:(hf + 1) * 512]
                    drain(v.tensor_tensor(xs, bank(nm)[0:n, :], xs, ALU.add), nm)
            mark(v.memset(H[64:P, 2048:3072], 0.0), "x2")
            dve.wait_ge(a_mark, AM["ss2"])
            rsqrt_of(rstd[:, :], ss[:, :], 1.0 / D_MODEL)
            for t, (t0, n) in enumerate(TILES):
                ins = v.tensor_scalar(h3[0:n, t, :], x3[0:n, t, :], rstd[0:n, t:t + 1], None, ALU.mult)
                mark(ins, "h2") if t == NT - 1 else step(ins)
            evac_hT("rT", "ln_moe")
            step(v.memset(Lg[:, :, :], 0.0))
            is_filled(dve, "lgT")
            for t, (t0, n) in enumerate(TILES):
                ins = v.tensor_copy(Lg[0:n, t, :], bank("lgT")[0:n, t * E:(t + 1) * E])
                drain(ins, "lgT") if t == NT - 1 else step(ins)
            for t in range(NT):
                step(v.max(m8[:, t, :], Lg[:, t, :]))
            mark(v.tensor_tensor(exq[:, :, :], Lg[:, :, :], m8[:, :, 0:1].broadcast_to([P, NT, E]), ALU.subtract), "m8")
            kth = m8[:, :, TOPK - 1:TOPK].broadcast_to([P, NT, E])
            step(v.tensor_tensor(gtm[:, :, :], Lg[:, :, :], kth, ALU.is_gt))
            step(v.tensor_tensor(eqm[:, :, :], Lg[:, :, :], kth, ALU.is_equal))
            step(v.tensor_reduce(ngt, gtm[:, :, :], AX_X, ALU.add))
            for t in range(NT):
                step(v.tensor_tensor_scan(cum[:, t, :], ones[:, 0:E], eqm[:, t, :], 0.0, ALU.mult, ALU.add))
            step(v.tensor_tensor(cum[:, :, :], cum[:, :, :], ngt.unsqueeze(2).broadcast_to([P, NT, E]), ALU.add))
            step(v.tensor_scalar(cum[:, :, :], cum[:, :, :], float(TOPK), None, ALU.is_le))
            step(v.tensor_tensor(eqm[:, :, :], eqm[:, :, :], cum[:, :, :], ALU.mult))
            step(v.tensor_tensor(sel[:, :, :], gtm[:, :, :], eqm[:, :, :], ALU.add))
            mark(v.memset(sel[NSAMP:P, NT - 1, :], 0.0), "sel")
            dve.wait_ge(a_mark, AM["exq"])
            step(v.tensor_tensor(exq[:, :, :], exq[:, :, :], sel[:, :, :], ALU.mult))
            step(v.tensor_reduce(den, exq[:, :, :], AX_X, ALU.add))
            step(v.tensor_scalar(den, den, 1e-30, None, ALU.max))
            step(v.reciprocal(den, den))
            mark(v.tensor_tensor(gate[:, 0:E, :].rearrange("p e t -> p t e"), exq[:, :, :],
                                 den.unsqueeze(2).broadcast_to([P, NT, E]), ALU.mult), "gates")
            is_filled(dve, "rk")
            rkv = bank("rk")[:, 0:NT * E].rearrange("p (t e) -> p t e", t=NT)
            rankv = rank[:, 0:E, :].rearrange("p e t -> p t e")
            step(v.scalar_tensor_tensor(out=exq[:, :, :], in0=rkv, scalar=1.0, in1=sel[:, :, :],
                                        op0=ALU.add, op1=ALU.mult))
            step(v.tensor_scalar(rankv, exq[:, :, :], -1.0, None, ALU.add))
            drain(v.tensor_copy(cnt, bank("rk")[:, NT * E:(NT + 1) * E]), "rk")

            def select(out_sem, value, half, rank_pair, gate_pair, experts):
                io = iotaf[:, 0:CAP].unsqueeze(1).unsqueeze(1).broadcast_to([P, NT, 2, CAP])
                sv = Ssel.rearrange("p t (a s) -> p t a s", a=2)
                gv = Sgat.rearrange("p t (a s) -> p t a s", a=2)
                rv = rank_pair.rearrange("p a t -> p t a").unsqueeze(3).broadcast_to([P, NT, 2, CAP])
                ev = gate_pair.rearrange("p a t -> p t a").unsqueeze(3).broadcast_to([P, NT, 2, CAP])
                return [v.tensor_tensor, (sv, io, rv, ALU.is_equal)], [v.tensor_tensor, (gv, sv, ev, ALU.mult)], \
                    [v.tensor_copy, (ind[:, half, :].rearrange("p (a s) -> p a s", a=2),
                                     experts.unsqueeze(2).broadcast_to([E, 2, CAP]))]

            def run(op):
                return op[0](*op[1])

            for t, (t0, n) in enumerate(TILES):
                for hf in range(2):
                    nm = f"bd{t}{hf}"
                    is_filled(dve, nm)
                    xs = x3[0:n, t, hf * 512:(hf + 1) * 512]
                    drain(v.tensor_tensor(xs, bank(nm)[0:n, :], xs, ALU.add), nm)
            step(v.memset(ybuf, 0.0))
            a1, a2, a3 = select(None, None, 0, rank[:, 0:2, :], gate[:, 0:2, :], ident[0:E, 0:2])
            step(run(a1)), step(run(a2)), step(run(a3), pair_sel)

            def scaled_turn(name, k0):
                w = vec("ln_moe", k0, 4).unsqueeze(2).broadcast_to([P, 4, P])
                return (xgT[:, k0:k0 + 4, :], name.rearrange("p (k s) -> p k s", k=4), w, ALU.mult)
            for nm, k0 in (("xt0a", 0), ("xt0b", 4)):
                is_filled(dve, nm)
                drain(v.tensor_tensor(*scaled_turn(bank(nm), k0)), nm)
            for bi, off in enumerate(OV_OFF):
                step(v.tensor_scalar(flg[:, :, bi], cnt, float(off), None, ALU.is_gt))
                step(v.memset(ovec[:, :, bi], float(off)))
                step(v.tensor_copy(evec[:, :, bi], iotaf[:, 0:E]))
            flat = flg.rearrange("p e b -> p (e b)")
            step(v.tensor_tensor_scan(pos, ones[:, 0:2 * E], flat, 0.0, ALU.mult, ALU.add))
            step(v.tensor_tensor(evec, evec, flg, ALU.mult))
            step(v.tensor_tensor(ovec, ovec, flg, ALU.mult))
            dve.wait_ge(ssm_stored, 16)
            for src, dst in ((evec, ove_f), (ovec, ov_off[:, :])):
                step(v.tensor_tensor(cmp_, pos.unsqueeze(1).broadcast_to([P, OV_MAX, 64]),
                                     iotaf[:, 1:OV_MAX + 1].unsqueeze(2).broadcast_to([P, OV_MAX, 64]), ALU.is_equal))
                step(v.tensor_tensor(cmp_, cmp_, src.rearrange("p e b -> p (e b)").unsqueeze(1)
                                     .broadcast_to([P, OV_MAX, 64]), ALU.mult))
                step(v.tensor_reduce(dst, cmp_, AX_X, ALU.add))
            step(v.tensor_copy(ov_e[:, :], ove_f))
            mark(v.tensor_copy(ov_n[:, :], pos[:, 63:64]), "table")

            is_filled(dve, "sgt0")
            with dve.Fori(0, PAIRS // 2) as i:
                VPP = 3 + 2
                for half in range(2):
                    pair = i * 2 + half
                    cnt_ = [0]

                    def lstep(ins):
                        cnt_[0] += 1
                        k = half * VPP + cnt_[0]
                        ins.then_inc(v_loop, 1)
                        dve.wait_ge(v_loop, i * (2 * VPP) + k)

                    def lmark(ins, s, value):
                        ins.then_inc(s, 1)
                        dve.wait_ge(s, value)

                    def aux(k, op, *args):
                        l = 13 * half + k
                        b, m = 6 + l % 2, l // 2
                        dve.wait_ge(filled[b], base[b] + 1 + m + i * 13)
                        lmark(op(*args), drained[b], base[b] + 1 + m + i * 13)

                    def auxbank(k):
                        return PS[:, 6 + (13 * half + k) % 2, :]
                    e = i * 4 + 2 * half + 2
                    a1, a2, a3 = select(None, None, 1 - half, rank[:, bass.ds(e, 2), :], gate[:, bass.ds(e, 2), :],
                                        ident[0:E, bass.ds(e, 2)])
                    lstep(run(a1)), lstep(run(a2))
                    lmark(run(a3), pair_sel, pair + 2)
                    dve.wait_ge(chunk_used, i * (2 * CPP) + half * CPP + CPM)
                    lmark(v.tensor_scalar(gbuf, PS[:, 0:2, :].rearrange("p b f -> p (b f)"), LIMIT, None, ALU.min),
                          g_act, pair + 2)
                    dve.wait_ge(chunk_used, i * (2 * CPP) + half * CPP + 2 * CPM)
                    lmark(v.tensor_scalar(ubuf, PS[:, 2:4, :].rearrange("p b f -> p (b f)"), LIMIT, -LIMIT,
                                          ALU.min, ALU.max), up_act, pair + 2)
                    lstep(v.scalar_tensor_tensor(out=ubuf, in0=ubuf, scalar=1.0, in1=gbuf, op0=ALU.add, op1=ALU.mult))
                    dve.wait_ge(sig_act, pair + 1)
                    lmark(v.tensor_tensor(ubuf, ubuf, sbuf_, ALU.mult), hid_act, pair + 1)
                    for t, (t0, n) in enumerate(TILES):
                        for hf in range(2):
                            k = 2 + 2 * t + hf
                            xs = x3[0:n, t, hf * 512:(hf + 1) * 512]
                            aux(k, v.tensor_tensor, xs, auxbank(k)[0:n, :], xs, ALU.add)
                    aux(11, v.tensor_tensor, *scaled_turn(auxbank(11), 0))
                    aux(12, v.tensor_tensor, *scaled_turn(auxbank(12), 4))
                    while cnt_[0] < VPP:
                        lstep(v.memset(small[:, 159:160], 0.0))

            def add_y(fillb, value):
                for t, (t0, n) in enumerate(TILES):
                    for hf in range(2):
                        b, at = fillb(t * 2 + hf)
                        dve.wait_ge(filled[b], at)
                        xs = x3[0:n, t, hf * 512:(hf + 1) * 512]
                        v.tensor_tensor(xs, PS[0:n, b, :], xs, ALU.add).then_inc(drained[b], 1)
                        dve.wait_ge(drained[b], at)
            add_y(lambda k: (6 + k % 2, base[6 + k % 2] + 13 * (PAIRS // 2) + k // 2 + 1), None)
            n_ov = dve.value_load(ov_n[0:1, 0:1], min_val=0, max_val=OV_MAX)
            with dve.Fori(0, OV_MAX) as j:
                with dve.If(j < n_ov):
                    e = dve.value_load(ov_e[0:1, bass.ds(j, 1)], min_val=0, max_val=E - 1)
                    oc = [0]

                    def ostep(ins):
                        oc[0] += 1
                        ins.then_inc(v_ov, 1)
                        dve.wait_ge(v_ov, j * 5 + oc[0])

                    def omark(ins, s):
                        ins.then_inc(s, 1)
                        dve.wait_ge(s, j + 1)

                    def ovaux(k, op, *args):
                        b, m = 6 + k % 2, k // 2
                        dve.wait_ge(filled[b], ovbase[b] + 1 + m + j * 7)
                        op(*args).then_inc(drained[b], 1)
                        dve.wait_ge(drained[b], ovbase[b] + 1 + m + j * 7)
                    rel = small[:, 156:159]
                    ostep(v.tensor_scalar(rel, rank[:, bass.ds(e, 1), :].rearrange("p a t -> p (a t)"),
                                          ov_off[:, bass.ds(j, 1)], None, ALU.subtract))
                    ostep(v.tensor_tensor(Ssel, iotaf[:, :].unsqueeze(1).broadcast_to([P, NT, P]),
                                          rel.unsqueeze(2).broadcast_to([P, NT, P]), ALU.is_equal))
                    ostep(v.tensor_tensor(Sgat, Ssel, gate[:, bass.ds(e, 1), :].rearrange("p a t -> p (a t)")
                                          .unsqueeze(2).broadcast_to([P, NT, P]), ALU.mult))
                    omark(v.tensor_copy(ind[:, 0, :], ident[0:E, bass.ds(e, 1)].broadcast_to([E, P])), ov_sel)
                    ovaux(2, v.tensor_tensor, *scaled_turn(PS[:, 6, :], 0))
                    ovaux(3, v.tensor_tensor, *scaled_turn(PS[:, 7, :], 4))
                    dve.wait_ge(ov_used, j * OV_CHUNKS + OV_CHUNKS + 2)
                    omark(v.tensor_scalar(gbuf, PS[:, 0:2, :].rearrange("p b f -> p (b f)"), LIMIT, None, ALU.min), ovg_act)
                    dve.wait_ge(ov_used, j * OV_CHUNKS + OV_CHUNKS + 4)
                    ostep(v.tensor_scalar(ubuf, PS[:, 2:4, :].rearrange("p b f -> p (b f)"), LIMIT, -LIMIT,
                                          ALU.min, ALU.max))
                    ostep(v.scalar_tensor_tensor(out=ubuf, in0=ubuf, scalar=1.0, in1=gbuf, op0=ALU.add, op1=ALU.mult))
                    assert oc[0] == 5
                    dve.wait_ge(ovs_act, j + 1)
                    omark(v.tensor_tensor(ubuf, ubuf, sbuf_, ALU.mult), ovh_act)
                    for t, (t0, n) in enumerate(TILES):
                        for hf in range(2):
                            k = 8 + t * 2 + hf
                            xs = x3[0:n, t, hf * 512:(hf + 1) * 512]
                            ovaux(k, v.tensor_tensor, xs, PS[0:n, 6 + k % 2, :], xs, ALU.add)
                    v.memset(small[:, 155:156], 0.0)
            mark(v.memset(small[:, 159:160], 0.0), "moe_done")
            dve.wait_ge(a_mark, AM["ss3"])
            rsqrt_of(rstd[:, :], ss[:, :], 1.0 / D_MODEL)
            for t, (t0, n) in enumerate(TILES):
                ins = v.tensor_scalar(h3[0:n, t, :], x3[0:n, t, :], rstd[0:n, t:t + 1], None, ALU.mult)
                mark(ins, "h3") if t == NT - 1 else step(ins)
            evac_hT("tT", "ln_ple")
            for t, (t0, n) in enumerate(TILES):
                for hf in range(2):
                    cs = slice(hf * 512, (hf + 1) * 512)
                    is_drained(dve, f"pg{t}{hf}")
                    nm = f"pp{t}{hf}"
                    is_filled(dve, nm)
                    drain(v.tensor_tensor(sg3[0:n, t, cs], bank(nm)[0:n, :], sg3[0:n, t, cs], ALU.mult), nm)
                    ins = v.tensor_tensor(x3[0:n, t, cs], x3[0:n, t, cs], sg3[0:n, t, cs], ALU.add)
                    mark(ins, f"y{t}") if hf else step(ins)
            dve.wait_ge(tail_in, 16 * 5)
            for t, (t0, n) in enumerate(TILES):
                dve.wait_ge(a_mark, AM[f"ss4{t}"])
                r = rstd[0:n, t:t + 1]
                rsqrt_of(r, ss[0:n, t:t + 1], 1.0 / D_MODEL)
                mark(v.scalar_tensor_tensor(out=h3[0:n, t, :], in0=x3[0:n, t, :], scalar=r, in1=fnb[0:n, :],
                                            op0=ALU.mult, op1=ALU.mult), f"yout{t}")


_INS = ['x_prompt', 'x_sample', 'state_pool', 'state_conv', 'state_ssm', 'p_prompt', 'p_sample', 'ln_mix', 'w_in',
        'pool_w', 'pool_scale', 'conv_w', 'a_log', 'dt_bias', 'dn_norm', 'w_out', 'ln_moe', 'router_w', 'router_b',
        'w_gate', 'b_gate', 'w_up', 'b_up', 'w_down', 'b_down', 'ln_ple', 'w_ple_gate', 'w_ple', 'final_norm']
_OUTS = [(1, SEQ, D_MODEL), (DB, DS, D_MODEL), (1, 1, PH, POOL_W), (1, 1, CH, QKV_T * P), (1, 1, HEADS, P, P),
         (1, DB, PH, POOL_W), (1, DB, CH, QKV_T * P), (1, DB, HEADS, P, P)]


def kernel(**inputs):
    import numpy as _np
    import concourse.bacc as _bacc
    from concourse import mybir as _mybir
    from concourse.bass_utils import run_bass_kernel_spmd as _run

    nc = _bacc.Bacc("TRN2", target_bir_lowering=False, num_devices=1)
    arrays, d = {}, {}
    for name in _INS:
        a = _np.ascontiguousarray(inputs[name])
        arrays[f"in_{name}"] = a
        d[name] = nc.dram_tensor(f"in_{name}", a.shape, _mybir.dt.from_np(a.dtype), kind="ExternalInput").ap()
    o = [nc.dram_tensor(f"out_{i}", shape, _mybir.dt.float32, kind="ExternalOutput").ap()
         for i, shape in enumerate(_OUTS)]
    trunk_kernel(nc, d, o)
    r = _run(nc, [arrays], core_ids=[0])
    return tuple(r.results[0][f"out_{i}"] for i in range(len(_OUTS)))
```

```python
from contextlib import ExitStack

import concourse.bass as bass
from concourse import mybir

F32 = mybir.dt.float32
I32 = mybir.dt.int32
BF16 = mybir.dt.bfloat16
ALU = mybir.AluOpType
ACT = mybir.ActivationFunctionType
AX_X = mybir.AxisListType.X

P = 128
D_MODEL = 1024
KT = D_MODEL // P
SEQ = 256
DB, DS = 8, 8
NSAMP = DB * DS
T = SEQ + NSAMP
TILES = [(0, P), (P, P), (SEQ, NSAMP)]
NT = len(TILES)
POOL_W = 512
WINDOWS = (2, 4, 8, 16)
PG = len(WINDOWS)
PH = max(WINDOWS) - 1
HEADS = 4
CONV = 4
CH = CONV - 1
QKV_T = 3 * HEADS
IN_W = POOL_W + 4 * HEADS * P + 2 * HEADS
NB_IN = 5
E = 32
TOPK = 4
FF = 1024
LIMIT = 7.0
ALPHA = 1.702
PLE = 256
EPS = 1e-6
CAP = 64
PAIRS = E // 2
TURNS = PAIRS // 2
MID = TURNS // 2
EPAD = E + 2
RING = 8
SLOT = 4096
CPM = 4
CPP = 3 * CPM
NCH = PAIRS * CPP
TURN = 2 * CPP
UEW = (PH + SEQ) + DB * (PH + DS)
QEW = (CH + SEQ) + DB * (CH + DS)
LEVELS = 7
OV_MAX = (T * TOPK - 1) // CAP
OV_PER = 4
OV_GROUPS = -(-OV_MAX // OV_PER)
OV_SLOTS = OV_PER * OV_GROUPS
OV_OFF = [CAP, CAP + P]
OV_CHUNKS = 6

IN_ORDER = [2, 1, 3, 0, 4]


def chain(eng, own):
    counts = {}

    def step(ins, s=None, value=None):
        s = own if s is None else s
        counts[s.name] = counts.get(s.name, 0) + 1
        ins.then_inc(s, 1)
        eng.wait_ge(s, counts[s.name] if value is None else value)
    return step


def trunk_kernel(nc, d, o):
    with ExitStack() as ctx:
        def sb(name, shape, dt=F32):
            return ctx.enter_context(nc.sbuf_tensor(name, shape, dt))

        def sem(name):
            return ctx.enter_context(nc.semaphore(name))

        ring = sb("ring", [P, RING, SLOT])
        X = sb("x_resid", [P, NT * D_MODEL])
        H = sb("h_region", [P, QKV_T * T])
        HT = sb("ht_region", [P, KT * T])
        Q = sb("q_region", [P, QKV_T * QEW])
        U = sb("u_region", [P, PG * UEW])
        Z = sb("z_region", [P, 2 * D_MODEL])
        ident = sb("ident", [P, P])
        ones = sb("ones", [P, P])
        causal = sb("causal", [P, P])
        strict = sb("strict", [P, P])
        seg = sb("seg", [NSAMP, NSAMP])
        segcausal = sb("segcausal", [NSAMP, NSAMP])
        ident3 = sb("ident3", [3 * E, EPAD])
        lmask = sb("lmask", [P, LEVELS, P])
        iotaf = sb("iotaf", [P, P])
        vecs = sb("vecs", [P, 77])
        wrout = sb("wrout", [P, KT, E])
        small = sb("small", [P, 160])
        rank = sb("rank", [P, EPAD, NT])
        gate = sb("gate", [P, EPAD, NT])
        ov_off = sb("ov_off", [P, OV_SLOTS])
        ov_e = sb("ov_e", [P, OV_SLOTS], I32)
        ov_n = sb("ov_n", [P, 1], I32)

        ptmp = sb("ptmp", [P, UEW])
        iti = ptmp[:, 0:P].bitcast(I32)

        PS = ctx.enter_context(nc.psum_tensor("ps", [P, 8, 512], F32))

        x3 = X[:, :].rearrange("p (t d) -> p t d", t=NT)
        h3 = H[:, 0:NT * D_MODEL].rearrange("p (t d) -> p t d", t=NT)
        ct = H[:, :].rearrange("p (c t) -> p c t", c=QKV_T)
        hT = HT[:, :].rearrange("p (k t) -> p k t", k=KT)
        qe = Q[:, :].rearrange("p (c t) -> p c t", c=QKV_T)
        ue = U[:, :].rearrange("p (c t) -> p c t", c=PG)
        zT = Z[:, 0:PG * T].rearrange("p (c t) -> p c t", c=PG)
        ptmp2 = Z[:, PG * T:PG * T + UEW]
        wtail = Z[:, 1736:1800].rearrange("p (k c) -> p k c", k=KT)
        VEC = {"ln_mix": 0, "ln_moe": 8, "ln_ple": 16, "pool_scale": 24, "dn_norm": 28, "conv_w": 29}

        def vec(name, i=0, n=1):
            return vecs[:, VEC[name] + i:VEC[name] + i + n]

        def sm(at, *shape):
            n = 1
            for s in shape:
                n *= s
            v = small[:, at:at + n]
            return v.rearrange("p (a b) -> p a b", a=shape[0]) if len(shape) == 2 else v
        ss = sm(0, NT)
        rstd = sm(3, NT)
        beta = sm(6, NT, HEADS)
        gl = sm(18, NT, HEADS)
        gc = sm(30, NT, HEADS)
        egc = sm(42, NT, HEADS)
        kdec = sm(54, NT, HEADS)
        egl = sm(66, NT, HEADS)
        egs = sm(78, HEADS, DB)
        alog = sm(110, HEADS)
        dtb = sm(114, HEADS)
        inv16 = sm(118, 16)
        rb = small[0:E, 134:135]
        tmp12 = sm(136, NT, HEADS)
        pcol = small[:, 148:149]
        scol = small[:, 149:150]
        oss = sm(150, 4)

        sqb = [X[:, 0:T], X[:, T:2 * T]]
        rnb = [X[:, o_:o_ + T] for o_ in (640, 2304, 2624)]
        poolw = X[:, 1024:1536].rearrange("p (g d) -> p g d", g=PG)
        clast = X[:, 1536:1536 + QKV_T * DB * CH].rearrange("p (c r) -> p c r", c=QKV_T)
        ulast = X[:, 2048:2048 + PG * NSAMP].rearrange("p (c r) -> p c r", c=PG)
        convord = {c: i for i, c in enumerate([4, 5, 6, 7, 0, 1, 2, 3, 8, 9, 10, 11])}

        def prompt_cols(v, c, hist):
            return v[:, c, hist:hist + SEQ]

        def sample_cols(v, c, hist, lo=None, n=DS):
            lo = hist if lo is None else lo
            base = hist + SEQ
            return v[:, c, base:base + DB * (hist + DS)].rearrange("p (b w) -> p b w", b=DB)[:, :, lo:lo + n]

        def quads(region, n):
            return [region[0:n, i * HEADS * n:(i + 1) * HEADS * n].rearrange("p (h t) -> p h t", h=HEADS)
                    for i in range(6)]
        scratch = [quads(X[:, :], P), quads(ring[:, 4, :], P), quads(U[:, :], NSAMP)]
        kN = Q[:, 0:1536].rearrange("p (t h d) -> p t h d", t=NT, h=HEADS)
        vN = Q[:, 1536:3072].rearrange("p (t h d) -> p t h d", t=NT, h=HEADS)
        S1 = Q[:, 3072:3584].rearrange("p (h d) -> p h d", h=HEADS)
        kqS = Q[:, 3584:4096].rearrange("p (h t) -> p h t", h=HEADS)
        oN = [scratch[0][5], scratch[1][5],
              ring[0:NSAMP, 4, 3072:3584].rearrange("p (h d) -> p h d", h=HEADS)]
        qS2 = ring[0:NSAMP, 4, 3584:4096].rearrange("p (h d) -> p h d", h=HEADS)
        vmask = U[0:NSAMP, 0:1024].rearrange("p (b d) -> p b d", b=DB)
        s0 = ring[:, 7, :].rearrange("p (b h e) -> p b h e", b=DB, h=HEADS)
        tilepart = [(causal, ones, 0, P), (causal, ones, P, P), (segcausal, seg, SEQ, NSAMP)]

        st_conv = ring[0:DB * CH, 7, 0:QKV_T * P]
        st_pool = ring[0:DB * PH, 7, 1536:2048]
        vrows = ring[0:77, 7, 2048:2176]
        outrow = ring[:, 6, :]

        xg = HT[:, 0:1024]
        xgT = HT[:, 1024:2048].rearrange("p (k s) -> p k s", k=KT)
        ind = HT[0:3 * E, 2048:2176].bitcast(BF16).rearrange("p (b s) -> p b s", b=2)
        gbuf, ubuf, sbuf_, hidf = (Q[:, i * 1024:(i + 1) * 1024] for i in range(4))
        hidT = hidf.rearrange("p (k s) -> p k s", k=KT)
        ybuf = U[:, 0:1024]
        Ssel = U[:, 1024:1408].rearrange("p (t s) -> p t s", t=NT)
        Sgat = U[:, 1408:1792].rearrange("p (t s) -> p t s", t=NT)
        SgT = [H[:, 3072 + 384 * b:3456 + 384 * b].rearrange("p (t s) -> p t s", t=NT) for b in range(2)]
        bias3 = Z[0:3 * E, 0:1536].bitcast(BF16)
        biases = [bias3[:, m * FF:(m + 1) * FF] for m in range(3)]
        bias_f = ring[0:3 * E, 4, 0:3072]

        def rt(i):
            return Q[:, 1024 + i * 96:1120 + i * 96].rearrange("p (t e) -> p t e", t=NT)
        logT = Q[0:E, 0:T]
        Lg, gtm, eqm, cum, sel, exq = (rt(i) for i in range(6))
        m8 = Q[:, 1700:1724].rearrange("p (t e) -> p t e", t=NT)
        ngt = Q[:, 1724:1727]
        den = Q[:, 1727:1730]
        cnt = Q[:, 1730:1762]
        flg = Q[:, 1762:1826].rearrange("p (e b) -> p e b", b=2)
        pos = Q[:, 1826:1890]
        evec = Q[:, 1890:1954].rearrange("p (e b) -> p e b", b=2)
        ovec = Q[:, 1954:2018].rearrange("p (e b) -> p e b", b=2)
        ove_f = Q[:, 2018:2018 + OV_SLOTS]
        cmp_ = Q[:, 2048:2048 + OV_SLOTS * 64].rearrange("p (j x) -> p j x", j=OV_SLOTS)

        wple = ring[:, 0, 0:2048].rearrange("p (k f) -> p k f", k=2)
        pin = ring[:, 1, 0:768].rearrange("p (t f) -> p t f", t=NT)
        pT = ring[:, 1, 1024:1024 + 2 * T].rearrange("p (k t) -> p k t", k=2)
        wpg = ring[:, 2:4, :].rearrange("p s (k f) -> p (s k) f", k=4)
        ppb = ring[:, 4, 0:3072].rearrange("p (t f) -> p t f", t=NT)
        sg3 = Q[:, 0:3072].rearrange("p (t f) -> p t f", t=NT)
        fnb = ring[:, 1, 2048:3072]

        vecs_in = sem("vecs_in")
        x_in = [sem(f"x_in{t}") for t in range(NT)]
        win_in = [sem(f"win_in{b}") for b in range(NB_IN)]
        wtail_in = sem("wtail_in")
        smalls_in = sem("smalls_in")
        hist_in = sem("hist_in")
        wout_in = sem("wout_in")
        s0_in = sem("s0_in")
        xagain_in = sem("xagain_in")
        bias_in = sem("bias_in")
        chunk_in = [sem(f"chunk_in{c}") for c in range(TURN)]
        ovch_in = [sem(f"ovch_in{c}") for c in range(OV_CHUNKS)]
        wpg_in = sem("wpg_in")
        tail_in = sem("tail_in")
        fnb_in = sem("fnb_in")
        out_done = sem("out_done")
        chunk_used = sem("chunk_used")
        ov_used = sem("ov_used")
        ov_filled = [sem(f"ov_filled{b}") for b in range(2)]
        ov_drained = [sem(f"ov_drained{b}") for b in range(2)]
        win_used = sem("win_used")
        filled = [sem(f"filled{b}") for b in range(8)]
        drained = [sem(f"drained{b}") for b in range(8)]
        consts = sem("consts")
        h_ready = sem("h_ready")
        ext_zero = sem("ext_zero")
        acc_ready = sem("acc_ready")
        ct_ready = sem("ct_ready")
        sq_ready = sem("sq_ready")
        norm_ready = sem("norm_ready")
        d_ready = sem("d_ready")
        v_step = sem("v_step")
        a_step = sem("a_step")
        g_step = sem("g_step")
        v_mark = sem("v_mark")
        a_mark = sem("a_mark")
        VM = {n: i + 1 for i, n in enumerate(
            ["ba", "sp_in", "g", "gcs"] + [f"diff{t}" for t in range(NT)] + [f"U{t}" for t in range(NT)]
            + ["kd", "S2", "rs_o", "vm0", "vm1", "vm2", "vm3", "S0", "split", "x2", "h2", "m8", "sel", "gates", "ybuf_zero", "table",
               "sel_mid", "ybuf_zero_mid"] + [f"moe{t}" for t in range(NT)] + [f"h3{t}" for t in range(NT)] + [f"y{t}" for t in range(NT)] + [f"yout{t}" for t in range(NT)])}
        AM = {n: i + 1 for i, n in enumerate(
            ["ss", "exps", "ea", "lg", "gexp"] + [f"E{t}" for t in range(NT)]
            + ["ss2", "exq"] + [f"ss3{t}" for t in range(NT)] + [f"ss4{t}" for t in range(NT)])}
        g_ready = sem("g_ready")
        small_zero = sem("small_zero")
        inv_ready = sem("inv_ready")
        root_ready = sem("root_ready")
        acc_pool = sem("acc_pool")
        packed = sem("packed")
        poolw_in = sem("poolw_in")
        pool_stored = sem("pool_stored")
        ssm_stored = sem("ssm_stored")
        hist_stored = sem("hist_stored")
        s0_stored = sem("s0_stored")
        v_loop = sem("v_loop")
        v_ov = sem("v_ov")
        pair_sel = sem("pair_sel")
        g_act = sem("g_act")
        sig_act = sem("sig_act")
        up_act = sem("up_act")
        y_act = sem("y_act")
        ovy_act = sem("ovy_act")
        hid_act = sem("hid_act")
        ov_sel = sem("ov_sel")
        ovg_act = sem("ovg_act")
        ovs_act = sem("ovs_act")
        ovh_act = sem("ovh_act")

        uses, fills = {}, [0] * 8

        def use(name, bank):
            uses[name] = (bank, fills[bank])
            fills[bank] += 1

        rr = [0]

        def nxt(name, banks=range(8)):
            banks = list(banks)
            use(name, banks[rr[0] % len(banks)])
            rr[0] += 1

        for n in ["vec", "sc", "sp"] + [f"hT{t}{hf}" for t in range(NT) for hf in range(2)] + ["ba"]:
            nxt(n)
        for b in IN_ORDER:
            for c in range(4):
                nxt(f"pr{4 * b + c}")
            if b == 1:
                for c in range(8):
                    nxt(f"ss{c}")
        for n in (["cnp0", "cnp1", "cnp2", "cns0", "cns1", "cns2", "npp", "nps"]
                  + [f"kN{t}" for t in range(NT)] + [f"vN{t}" for t in range(NT)]
                  + [f"pm{g}" for g in range(PG)]):
            nxt(n)
        nxt("gcs")
        nxt("egs")
        for t in range(NT):
            nxt(f"G{t}")
            nxt(f"kk{t}")
            nxt(f"qk{t}")
        for t in range(NT):
            nxt(f"T{t}")
        for s in range(1, LEVELS):
            ts = [t for t in range(NT) if t < 2 or s < 3]
            for t in ts:
                nxt(f"P{s}{t}")
            for t in ts:
                if s < LEVELS - 1 and (t < 2 or s < 2):
                    nxt(f"Q{s}{t}")
                nxt(f"QT{s}{t}")
        for n in ["v0", "S1", "o0", "kqs", "kS1", "qS1", "R2k", "R2q", "v1", "v2", "o1", "S2", "o2"]:
            nxt(n)
        for t in range(NT):
            nxt(f"oT{t}")
        for h in range(HEADS):
            nxt(f"ns{h}a")
            nxt(f"ns{h}b")
        for t in range(NT):
            for hf in range(2):
                nxt(f"op{t}{hf}")
        for t in range(NT):
            for hf in range(2):
                nxt(f"rT{t}{hf}")
        for n in ["lg", "lgT", "rk"]:
            nxt(n)
        bases = []
        for r_ in range(2):
            for n, b in (("ga", 6), ("gb", 7), ("xta", 6), ("xtb", 7), ("sgt", 6)):
                use(f"{n}{r_}", b)
            bases.append([n - 13 * MID * r_ for n in fills])
            for b in (6, 7):
                fills[b] += 13 * MID
            for t in range(NT):
                for hf in range(2):
                    use(f"sc{r_}{t}{hf}", 6 + hf)
        use("pT0", 0), use("pT1", 1)
        for n in ([f"pp{t}{hf}" for t in range(NT) for hf in range(2)]
                  + [f"tT{t}{hf}" for t in range(NT) for hf in range(2)]
                  + [f"pg{t}{hf}" for t in range(NT) for hf in range(2)]):
            nxt(n)

        def bank(name):
            return PS[:, uses[name][0], :]

        def can_fill(eng, name):
            b, k = uses[name]
            if k:
                eng.wait_ge(drained[b], k)

        def is_filled(eng, name):
            b, k = uses[name]
            eng.wait_ge(filled[b], k + 1)

        def is_drained(eng, name):
            b, k = uses[name]
            eng.wait_ge(drained[b], k + 1)

        def fsem(name):
            return filled[uses[name][0]]

        def dsem(name):
            return drained[uses[name][0]]

        chunk_src = {"g": d["w_gate"][0], "u": d["w_up"][0], "d": d["w_down"][0]}

        def load_chunk(eng, c, e, s):
            cc = c % CPP
            r = (cc % CPM) * 2 * P
            for a_ in range(2):
                w = chunk_src["gud"[cc // CPM]][bass.ds(e + a_, 1)]
                eng.dma_start(slot(c)[:, a_], w[:, r:r + 2 * P, :].rearrange("a (k p) f -> p (a k) f", p=P)
                              ).then_inc(s, 16)

        def slot(c):
            return ring[:, c % RING, :].rearrange("p (a k f) -> p a k f", a=2, k=2)

        def ov_chunk(e, c):
            w = chunk_src["gud"[c // 2]][bass.ds(e, 1)]
            r = (c % 2) * 4 * P
            return w[:, r:r + 4 * P, :].rearrange("a (k p) f -> p (a k) f", p=P)

        block = ctx.enter_context(nc.Block())

        @block.sync
        def _(sp):
            r = 0
            for n in ("ln_mix", "ln_moe", "ln_ple", "pool_scale", "dn_norm"):
                k = d[n].shape[1] // P
                sp.dma_start(vrows[r:r + k, :], d[n][0].rearrange("(k p) -> k p", p=P)).then_inc(vecs_in, 16)
                r += k
            sp.dma_start(vrows[r:r + CONV * QKV_T, :],
                         d["conv_w"][0].rearrange("j (c p) -> (j c) p", p=P)).then_inc(vecs_in, 16)
            for t, (t0, n) in enumerate(TILES):
                src = d["x_prompt"][0, t0:t0 + n] if t < 2 else d["x_sample"].rearrange("b s d -> (b s) d")
                sp.dma_start(x3[0:n, t, :], src).then_inc(x_in[t], 16)
            sp.dma_start(st_conv, d["state_conv"][0].rearrange("b r c -> (b r) c")).then_inc(hist_in, 16)
            sp.dma_start(st_pool, d["state_pool"][0].rearrange("b r c -> (b r) c")).then_inc(hist_in, 16)
            sp.wait_ge(small_zero, 1)
            sp.dma_start(alog, d["a_log"][0:1, :].broadcast_to([P, HEADS])).then_inc(smalls_in, 16)
            sp.dma_start(dtb, d["dt_bias"][0:1, :].broadcast_to([P, HEADS])).then_inc(smalls_in, 16)
            sp.dma_start(rb, d["router_b"][0].rearrange("(e a) -> e a", a=1)).then_inc(smalls_in, 16)
            sp.dma_start(wtail[:, :, :], d["w_in"][0, :, NB_IN * 512:IN_W].rearrange("(k p) c -> p k c", p=P)
                         ).then_inc(wtail_in, 16)
            for i, b in enumerate(IN_ORDER):
                sp.dma_start(ring[:, i, :].rearrange("p (k c) -> p k c", k=KT),
                             d["w_in"][0, :, b * 512:(b + 1) * 512].rearrange("(k p) c -> p k c", p=P)
                             ).then_inc(win_in[i], 16)
            sp.dma_start(wrout[:, :, :], d["router_w"][0].rearrange("(k p) e -> p k e", p=P)).then_inc(smalls_in, 16)
            sp.wait_ge(h_ready, NT)
            sp.dma_start(poolw, d["pool_w"][0].rearrange("g c e -> c g e")).then_inc(poolw_in, 16)
            is_drained(sp, "vec"), is_drained(sp, "sc"), is_drained(sp, "sp")
            sp.dma_start(s0, d["state_ssm"][0].rearrange("b h d e -> d b h e")).then_inc(s0_in, 16)
            sp.dma_start(ring[:, 5, :].rearrange("p (k f) -> p k f", k=4),
                         d["w_out"][0, 0:512].rearrange("(k p) f -> p k f", p=P)).then_inc(wout_in, 16)
            for c in range(4):
                sp.wait_ge(win_used, c + 1)
                load_chunk(sp, c, 0, chunk_in[c])
            sp.wait_ge(hist_stored, 16 * 4)
            sp.dma_start(ring[:, 6, :].rearrange("p (k f) -> p k f", k=4),
                         d["w_out"][0, 512:1024].rearrange("(k p) f -> p k f", p=P)).then_inc(wout_in, 16)
            for t in range(NT):
                is_drained(sp, f"oT{t}")
            for t, (t0, n) in enumerate(TILES):
                src = d["x_prompt"][0, t0:t0 + n] if t < 2 else d["x_sample"].rearrange("b s d -> (b s) d")
                sp.dma_start(x3[0:n, t, :], src).then_inc(xagain_in, 16)
            for m, n in enumerate(("b_gate", "b_up", "b_down")):
                for part in range(3):
                    sp.dma_start(bias_f[part * E:(part + 1) * E, m * FF:(m + 1) * FF], d[n][0]).then_inc(bias_in, 16)
            sp.wait_ge(v_mark, VM["split"])
            load_chunk(sp, 4, 0, chunk_in[4])
            for c in range(5, 8):
                if c < 7:
                    is_filled(sp, "op21")
                else:
                    sp.wait_ge(s0_stored, 16)
                load_chunk(sp, c, 0, chunk_in[c])
            def turn_loads(lo, hi):
                with sp.Fori(lo, hi - 1) as i:
                    for c in range(TURN):
                        cc = (c + RING) % TURN
                        e = i * 4 + 4 * ((c + RING) // TURN) + 2 * (cc // CPP)
                        sp.wait_ge(chunk_used, i * TURN + c + 1)
                        load_chunk(sp, cc, e, chunk_in[cc])
                for c in range(TURN - RING):
                    cc = c + RING
                    sp.wait_ge(chunk_used, (hi - 1) * TURN + c + 1)
                    load_chunk(sp, cc, 4 * (hi - 1) + 2 * (cc // CPP), chunk_in[cc])
            turn_loads(0, MID)
            sp.nop().then_inc(ov_used, OV_CHUNKS)
            sp.wait_ge(v_mark, VM["table"])
            n_ov = sp.value_load(ov_n[0:1, 0:1], min_val=0, max_val=OV_MAX)
            with sp.Fori(0, OV_GROUPS) as grp:
                with sp.If(grp * OV_PER < n_ov):
                    with sp.Fori(0, OV_PER) as jj:
                        j = grp * OV_PER + jj
                        with sp.If(j < n_ov):
                            e = sp.value_load(ov_e[0:1, bass.ds(j, 1)], min_val=0, max_val=E - 1)
                            for c in range(OV_CHUNKS):
                                sp.wait_ge(chunk_used, MID * TURN - RING + c + 1)
                                sp.wait_ge(ov_used, j * OV_CHUNKS + c + 1)
                                sp.dma_start(ring[:, c, :].rearrange("p (k f) -> p k f", k=4), ov_chunk(e, c)
                                             ).then_inc(ovch_in[c], 16)
            for c in [6, 7] + list(range(OV_CHUNKS)):
                sp.wait_ge(chunk_used, MID * TURN - RING + c + 1)
                if c < OV_CHUNKS:
                    sp.wait_ge(ov_used, n_ov * OV_CHUNKS + (c + 1))
                load_chunk(sp, c, 4 * MID, chunk_in[c])
            turn_loads(MID, TURNS)
            sp.wait_ge(chunk_used, NCH - CPM)
            for t, (t0, n) in enumerate(TILES):
                src = d["p_prompt"][0, 0, t0:t0 + n] if t < 2 else d["p_sample"][0].rearrange("b s d -> (b s) d")
                sp.dma_start(pin[0:n, t, :], src).then_inc(tail_in, 16)
            sp.dma_start(wple, d["w_ple"][0].rearrange("(k p) f -> p k f", p=P)).then_inc(tail_in, 16)
            sp.dma_start(wpg, d["w_ple_gate"][0].rearrange("(k p) f -> p k f", p=P)).then_inc(wpg_in, 16)
            sp.dma_start(fnb, d["final_norm"].rearrange("(a f) -> a f", a=1).broadcast_to([P, D_MODEL])
                         ).then_inc(fnb_in, 16)
            for t, (t0, n) in enumerate(TILES):
                sp.wait_ge(v_mark, VM[f"yout{t}"])
                dst = o[0][0, t0:t0 + n] if t < 2 else o[1].rearrange("b s d -> (b s) d")
                sp.dma_start(dst, h3[0:n, t, :]).then_inc(out_done, 16)
            sp.wait_ge(out_done, 16 * NT)
            sp.wait_ge(pool_stored, 16)
            sp.wait_ge(ssm_stored, 16)

        @block.gpsimd
        def _(pool):
            step = chain(pool, g_step)
            g = nc.gpsimd
            step(g.memset(ident[:, :], 0.0))
            step(g.affine_select(out=ident[:, :], in_=ident[:, :], compare_op=ALU.not_equal, fill=1.0, base=0,
                                 pattern=[[-1, P]], channel_multiplier=1), consts)
            for c in range(PG):
                g.memset(ue[:, c, 0:PH], 0.0).then_inc(ext_zero, 1)
            for c in range(QKV_T):
                g.memset(qe[:, c, 0:CH], 0.0).then_inc(ext_zero, 1)
            step(g.memset(ones[:, :], 1.0), consts)
            step(g.iota(iti[:, :], pattern=[[1, P]], base=0, channel_multiplier=0))
            step(g.tensor_copy(iotaf[:, :], iti[:, :]))
            for m, b in ((causal, 0), (strict, -1)):
                step(g.memset(m[:, :], 1.0))
                step(g.affine_select(out=m[:, :], in_=m[:, :], compare_op=ALU.is_ge, fill=0.0, base=b,
                                     pattern=[[1, P]], channel_multiplier=-1))
            step(g.memset(seg[:, :], 1.0))
            sv = seg[:, :].rearrange("p (b s) -> p b s", b=DB)
            step(g.affine_select(out=sv, in_=sv, compare_op=ALU.is_ge, fill=0.0, base=0,
                                 pattern=[[-DS, DB], [0, DS]], channel_multiplier=1))
            step(g.affine_select(out=sv, in_=sv, compare_op=ALU.is_ge, fill=0.0, base=DS - 1,
                                 pattern=[[DS, DB], [0, DS]], channel_multiplier=-1))
            step(g.tensor_tensor(segcausal[:, :], causal[0:NSAMP, 0:NSAMP], seg[:, :], ALU.mult))
            step(g.memset(lmask[:, :, :], 0.0))
            v0 = lmask[:, 0, :].rearrange("p (b h s) -> p b h s", h=2, s=1)[:, :, 1, :]
            step(g.affine_select(out=v0, in_=v0, compare_op=ALU.not_equal, fill=1.0, base=0,
                                 pattern=[[-2, P // 2], [0, 1]], channel_multiplier=1))
            for s in range(1, LEVELS):
                z = 1 << s
                nb = P // (2 * z)
                vs = lmask[:, s, :].rearrange("p (b h s) -> p b h s", h=2, s=z)[:, :, 0, :]
                step(g.memset(vs, 1.0))
                step(g.affine_select(out=vs, in_=vs, compare_op=ALU.is_ge, fill=0.0, base=-z,
                                     pattern=[[-2 * z, nb], [0, z]], channel_multiplier=1))
                step(g.affine_select(out=vs, in_=vs, compare_op=ALU.is_ge, fill=0.0, base=2 * z - 1,
                                     pattern=[[2 * z, nb], [0, z]], channel_multiplier=-1))
            for part in range(3):
                rows = slice(part * E, (part + 1) * E)
                step(g.tensor_copy(ident3[rows, :], ident[rows, part * E:part * E + EPAD]))
            step(g.memset(rank[:, E:EPAD, :], -1.0))
            step(g.memset(gate[:, E:EPAD, :], 0.0), consts)
            pool.wait_ge(h_ready, NT)
            is_drained(pool, "sc")
            for c in [4, 5, 6, 7, 0, 1, 2, 3, 8, 9, 10, 11]:
                is_drained(pool, f"pr{c + 4}")
                step(g.tensor_copy(clast[:, c, :].rearrange("p (b r) -> p b r", b=DB),
                                   sample_cols(qe, c, CH, DS, CH)), packed)
            is_drained(pool, "sp")
            for c in range(PG):
                is_drained(pool, f"pr{c}")
                step(g.tensor_copy(ulast[:, c, :].rearrange("p (b r) -> p b r", b=DB),
                                   sample_cols(ue, c, PH)), packed)
            for c in range(PG):
                if c:
                    pool.wait_ge(acc_pool, c)
                src = ue[:, c, :]
                for k in range(c + 1):
                    off = 1 << k
                    dst = (ptmp[:, :], ptmp2)[(c - k) % 2]
                    step(g.tensor_copy(dst[:, 0:off], src[:, 0:off]))
                    step(g.tensor_tensor(dst[:, off:UEW], src[:, off:UEW], src[:, 0:UEW - off], ALU.add),
                         g_ready if k == c else None)
                    src = dst
            pool.wait_ge(s0_in, 16)
            is_drained(pool, "egs")
            is_filled(pool, "kqs")
            for h in range(HEADS):
                step(g.tensor_tensor(s0[:, :, h, :], s0[:, :, h, :],
                                     egs[:, h, :].unsqueeze(2).broadcast_to([P, DB, P]), ALU.mult), g_ready)

        @block.scalar
        def _(act):
            step = chain(act, a_step)
            a = nc.scalar

            rooted = [0]

            def root(ap):
                rooted[0] += 1
                act.wait_ge(inv_ready, rooted[0])
                step(a.activation(ap, ap, ACT.Sqrt), root_ready)

            def copy(out, in_, name):
                is_filled(act, name)
                step(a.activation(out, in_, ACT.Copy), dsem(name), uses[name][1] + 1)

            for t, (t0, n) in enumerate(TILES):
                act.wait_ge(x_in[t], 16)
                act.wait_ge(small_zero, 1)
                step(a.activation(h3[0:n, t, :], x3[0:n, t, :], ACT.Square, accum_out=ss[0:n, t:t + 1]),
                     a_mark if t == NT - 1 else None, AM["ss"] if t == NT - 1 else None)
            root(rstd[:, :])
            copy(vecs[:, :], bank("vec")[:, 0:77], "vec")
            act.wait_ge(ext_zero, PG + QKV_T)
            is_filled(act, "sc")
            scv = bank("sc")[:, 0:QKV_T * DB * CH].rearrange("p (c b r) -> p c b r", c=QKV_T, b=DB)
            for c in range(QKV_T):
                ins = a.activation(sample_cols(qe, c, CH, 0, CH), scv[:, c], ACT.Copy)
                step(ins, dsem("sc") if c == QKV_T - 1 else None, uses["sc"][1] + 1)
            is_filled(act, "sp")
            spv = bank("sp")[:, 0:PG * DB * PH].rearrange("p (c b r) -> p c b r", c=PG, b=DB)
            for c in range(PG):
                ins = a.activation(sample_cols(ue, c, PH, 0, PH), spv[:, c], ACT.Copy)
                step(ins, dsem("sp") if c == PG - 1 else None, uses["sp"][1] + 1)

            def silu_conv(c):
                act.wait_ge(acc_ready, convord[c] + 1)
                step(a.activation(ct[:, c, :], ct[:, c, :], ACT.Silu), ct_ready)

            def square(c):
                if c >= 2:
                    is_filled(act, f"ss{c - 2}")
                step(a.activation(sqb[c % 2], ct[:, c, :], ACT.Square), sq_ready)

            prev = []
            for b in IN_ORDER:
                for c in range(4 * b, 4 * b + 4):
                    name = f"pr{c}"
                    is_filled(act, name)
                    src = bank(name)
                    if b == 4:
                        step(a.activation(zT[:, c - 16, :], src[:, 0:T], ACT.Silu), dsem(name), uses[name][1] + 1)
                        continue
                    v, cc, hist = (ue, c, PH) if b == 0 else (qe, c - 4, CH)
                    step(a.activation(prompt_cols(v, cc, hist), src[:, 0:SEQ], ACT.Copy))
                    step(a.activation(sample_cols(v, cc, hist), src[:, SEQ:T].rearrange("p (b s) -> p b s", b=DB),
                                      ACT.Copy), dsem(name), uses[name][1] + 1)
                    if prev:
                        silu_conv(prev.pop(0))
                    if b:
                        prev.append(cc)
                if b == 1:
                    silu_conv(prev.pop(0))
                    for c in range(8 + 1):
                        if c < 8:
                            square(c)
                        if c:
                            root(rnb[(c - 1) % 3])
            assert not prev
            act.wait_ge(v_mark, VM["ba"])
            step(a.activation(beta[:, :, :], beta[:, :, :], ACT.Exp, scale=-1.0), a_mark, AM["exps"])
            act.wait_ge(smalls_in, 64)
            step(a.activation(alog, alog, ACT.Exp), a_mark, AM["ea"])
            act.wait_ge(v_mark, VM["sp_in"])
            step(a.activation(tmp12[:, :, :], tmp12[:, :, :], ACT.Exp, scale=-1.0))
            step(a.activation(tmp12[:, :, :], tmp12[:, :, :], ACT.Ln, bias=1.0), a_mark, AM["lg"])
            for i in range(3):
                copy(outrow[0:CH, i * 512:(i + 1) * 512], bank(f"cnp{i}")[0:CH, :], f"cnp{i}")
            for i in range(3):
                copy(outrow[0:DB * CH, 1536 + i * 512:2048 + i * 512], bank(f"cns{i}")[0:DB * CH, :], f"cns{i}")
            copy(outrow[0:PH, 3072:3584], bank("npp")[0:PH, :], "npp")
            copy(outrow[0:NSAMP, 3584:4096], bank("nps")[0:NSAMP, :], "nps")
            act.dma_start(o[3][0, 0], outrow[0:CH, 0:1536]).then_inc(hist_stored, 16)
            act.dma_start(o[6][0].rearrange("b r c -> (b r) c"), outrow[0:DB * CH, 1536:3072]).then_inc(hist_stored, 16)
            act.dma_start(o[2][0, 0], outrow[0:PH, 3072:3584]).then_inc(hist_stored, 16)
            act.dma_start(o[5][0, :, PH - DS:PH, :], outrow[0:NSAMP, 3584:4096]).then_inc(hist_stored, 16)
            act.dma_start(o[5][0, :, 0:PH - DS, :], d["state_pool"][0, :, DS:PH, :]).then_inc(pool_stored, 16)
            for t, (t0, n) in enumerate(TILES):
                copy(kN[0:n, t], bank(f"kN{t}")[0:n, :].rearrange("p (h d) -> p h d", h=HEADS), f"kN{t}")
            for t, (t0, n) in enumerate(TILES):
                copy(vN[0:n, t], bank(f"vN{t}")[0:n, :].rearrange("p (h d) -> p h d", h=HEADS), f"vN{t}")
            act.wait_ge(v_mark, VM["gcs"])
            step(a.activation(egc[:, :, :], gc[:, :, :], ACT.Exp))
            step(a.activation(kdec[:, :, :], kdec[:, :, :], ACT.Exp))
            step(a.activation(egl[:, :, :], egl[:, :, :], ACT.Exp), a_mark, AM["gexp"])
            is_filled(act, "egs")
            step(a.activation(egs[:, :, :], bank("egs")[:, 0:HEADS * DB].rearrange("p (h b) -> p h b", h=HEADS),
                              ACT.Exp), dsem("egs"), uses["egs"][1] + 1)
            for t, (t0, n) in enumerate(TILES):
                act.wait_ge(v_mark, VM[f"diff{t}"])
                step(a.activation(scratch[t][0], scratch[t][0], ACT.Exp), a_mark, AM[f"E{t}"])
            root(tmp12[:, :, :])
            act.wait_ge(v_mark, VM["S2"])
            act.dma_start(o[4][0, 0].rearrange("h d e -> d h e"), S1).then_inc(ssm_stored, 16)
            act.wait_ge(v_mark, VM["S0"])
            act.dma_start(o[7][0].rearrange("b h d e -> d b h e"), s0).then_inc(s0_stored, 16)
            act.wait_ge(v_mark, VM["x2"])
            for t, (t0, n) in enumerate(TILES):
                step(a.activation(h3[0:n, t, :], x3[0:n, t, :], ACT.Square, accum_out=ss[0:n, t:t + 1]),
                     a_mark if t == NT - 1 else None, AM["ss2"] if t == NT - 1 else None)
            root(rstd[:, :])
            is_filled(act, "lg")
            step(a.activation(logT, bank("lg")[0:E, 0:T], ACT.Identity, bias=rb), dsem("lg"), uses["lg"][1] + 1)
            act.wait_ge(v_mark, VM["m8"])
            step(a.activation(exq[:, :, :], exq[:, :, :], ACT.Exp), a_mark, AM["exq"])
            def first_pair(r_):
                copy(xg[:, 0:512], bank(f"ga{r_}"), f"ga{r_}")
                copy(xg[:, 512:1024], bank(f"gb{r_}"), f"gb{r_}")
                copy(SgT[0][:, :, :], bank(f"sgt{r_}")[:, 0:384].rearrange("p (t s) -> p t s", t=NT), f"sgt{r_}")

            NSTEP = 8
            def turns(lo, hi, base):
                with act.Fori(lo, hi) as i:
                    for half in range(2):
                        n0 = [0]

                        def lstep(ins, s, v):
                            ins.then_inc(s, 1)
                            act.wait_ge(s, v)

                        def aux(k, out, in_):
                            l = 13 * half + k
                            b, m = 6 + l % 2, l // 2
                            act.wait_ge(filled[b], base[b] + 1 + m + i * 13)
                            lstep(a.activation(out, in_, ACT.Copy), drained[b], base[b] + 1 + m + i * 13)

                        act.wait_ge(g_act, i * 2 + half + 2)
                        lstep(a.activation(sbuf_, gbuf, ACT.Sigmoid, scale=ALPHA), sig_act, i * 2 + half + 1)
                        aux(0, xg[:, 0:512], PS[:, 6 + (13 * half) % 2, :])
                        aux(1, xg[:, 512:1024], PS[:, 6 + (13 * half + 1) % 2, :])
                        aux(8, hidf[:, 0:512], PS[:, 6 + (13 * half + 8) % 2, :])
                        aux(9, hidf[:, 512:1024], PS[:, 6 + (13 * half + 9) % 2, :])
                        aux(10, SgT[1 - half][:, :, :],
                            PS[:, 6 + (13 * half + 10) % 2, 0:384].rearrange("p (t s) -> p t s", t=NT))
                        act.wait_ge(chunk_used, i * TURN + (half + 1) * CPP)
                        lstep(a.activation(ybuf, PS[:, 4:6, :].rearrange("p b f -> p (b f)"), ACT.Copy),
                              y_act, i * 2 + half + 2)
            first_pair(0)
            turns(0, MID, bases[0])
            act.wait_ge(v_mark, VM["table"])
            n_ov = act.value_load(ov_n[0:1, 0:1], min_val=0, max_val=OV_MAX)
            with act.Fori(0, OV_GROUPS) as grp:
                with act.If(grp * OV_PER < n_ov):
                    with act.Fori(0, OV_PER) as jj:
                        j = grp * OV_PER + jj
                        with act.If(j < n_ov):
                            def ovaux(k, out, in_):
                                b, m = k % 2, k // 2
                                act.wait_ge(ov_filled[b], 1 + m + j * 7)
                                ins = a.activation(out, in_, ACT.Copy)
                                ins.then_inc(ov_drained[b], 1)
                                act.wait_ge(ov_drained[b], 2 + m + j * 7)
                            ovaux(0, xg[:, 0:512], PS[:, 6, :])
                            ovaux(1, xg[:, 512:1024], PS[:, 7, :])
                            act.wait_ge(ovg_act, j + 1)
                            a.activation(sbuf_, gbuf, ACT.Sigmoid, scale=ALPHA).then_inc(ovs_act, 1)
                            ovaux(4, hidf[:, 0:512], PS[:, 6, :])
                            ovaux(5, hidf[:, 512:1024], PS[:, 7, :])
                            ovaux(6, SgT[0][:, 0:2, :], PS[:, 6, 0:256].rearrange("p (t s) -> p t s", t=2))
                            ovaux(7, SgT[0][:, 2, :], PS[:, 7, 0:128])
                            act.wait_ge(ov_used, j * OV_CHUNKS + 2 * OV_CHUNKS)
                            a.activation(ybuf, PS[:, 4:6, :].rearrange("p b f -> p (b f)"), ACT.Copy).then_inc(ovy_act, 1)
            first_pair(1)
            turns(MID, TURNS, bases[1])
            copy(pT[:, 0, :], bank("pT0")[:, 0:T], "pT0")
            copy(pT[:, 1, :], bank("pT1")[:, 0:T], "pT1")
            for t, (t0, n) in enumerate(TILES):
                act.wait_ge(v_mark, VM[f"moe{t}"])
                step(a.activation(h3[0:n, t, :], x3[0:n, t, :], ACT.Square, accum_out=ss[0:n, t:t + 1]),
                     a_mark, AM[f"ss3{t}"])
                root(rstd[0:n, t:t + 1])
            for t, (t0, n) in enumerate(TILES):
                for hf in range(2):
                    copy(ppb[0:n, t, hf * 512:(hf + 1) * 512], bank(f"pp{t}{hf}")[0:n, :], f"pp{t}{hf}")

            def final_square(t):
                t0, n = TILES[t]
                act.wait_ge(v_mark, VM[f"y{t}"])
                step(a.activation(h3[0:n, t, :], x3[0:n, t, :], ACT.Square, accum_out=ss[0:n, t:t + 1]),
                     a_mark, AM[f"ss4{t}"])
            for t, (t0, n) in enumerate(TILES):
                for hf in range(2):
                    nm = f"pg{t}{hf}"
                    is_filled(act, nm)
                    step(a.activation(sg3[0:n, t, hf * 512:(hf + 1) * 512], bank(nm)[0:n, :], ACT.Sigmoid),
                         dsem(nm), uses[nm][1] + 1)
                    if t and hf == 0:
                        final_square(t - 1)
            final_square(NT - 1)
            root(rstd[:, :])

        @block.tensor
        def _(pe):
            mm = nc.tensor.matmul
            seen = [0] * 8

            def fill(name):
                b, k = uses[name]
                assert k == seen[b], (name, k, seen[b])
                seen[b] += 1
                can_fill(pe, name)
                return PS[:, b, :]

            def tr(out, in_):
                n = in_.shape[0]
                return nc.tensor.transpose(out, in_, ident[0:n, 0:n])

            pe.wait_ge(consts, 1)
            pe.wait_ge(vecs_in, 16 * 6)
            tr(fill("vec")[:, 0:77], vrows).then_inc(fsem("vec"), 1)
            pe.wait_ge(hist_in, 32)
            ps = fill("sc")
            for c in range(QKV_T):
                last = tr(ps[:, c * 24:(c + 1) * 24], st_conv[:, c * P:(c + 1) * P])
            last.then_inc(fsem("sc"), 1)
            ps = fill("sp")
            for c in range(PG):
                last = tr(ps[:, c * 120:(c + 1) * 120], st_pool[:, c * P:(c + 1) * P])
            last.then_inc(fsem("sp"), 1)

            def transposes(prefix, ready=None):
                for t, (t0, n) in enumerate(TILES):
                    if ready:
                        pe.wait_ge(v_mark, VM[f"{ready}{t}"])
                    for hf in range(2):
                        ps = fill(f"{prefix}{t}{hf}")
                        for k in range(4):
                            c0 = (hf * 4 + k) * P
                            last = tr(ps[:, k * n:(k + 1) * n], h3[0:n, t, c0:c0 + P])
                        last.then_inc(fsem(f"{prefix}{t}{hf}"), 1)

            pe.wait_ge(h_ready, NT)
            transposes("hT")
            for t in range(NT):
                for hf in range(2):
                    is_drained(pe, f"hT{t}{hf}")
            pe.wait_ge(wtail_in, 16)
            ps = fill("ba")
            for t, (t0, n) in enumerate(TILES):
                for k in range(KT):
                    last = mm(ps[0:n, t * 8:(t + 1) * 8], hT[:, k, t0:t0 + n], wtail[:, k, :],
                              start=(k == 0), stop=(k == KT - 1))
            last.then_inc(fsem("ba"), 1)
            for i, b in enumerate(IN_ORDER):
                pe.wait_ge(win_in[i], 16)
                w = ring[:, i, :].rearrange("p (k c) -> p k c", k=KT)
                for c in range(4):
                    name = f"pr{4 * b + c}"
                    ps = fill(name)
                    for k in range(KT):
                        last = mm(ps[:, 0:T], w[:, k, c * P:(c + 1) * P], hT[:, k, :], start=(k == 0), stop=(k == KT - 1))
                    last.then_inc(fsem(name), 1)
                is_filled(pe, f"pr{4 * b + 3}")
                pe.nop().then_inc(win_used, 1)
                if b == 1:
                    pe.wait_ge(consts, 2)
                    for c in range(8):
                        ps = fill(f"ss{c}")
                        pe.wait_ge(sq_ready, c + 1)
                        mm(ps[:, 0:T], ones[:, :], sqb[c % 2], start=True, stop=True).then_inc(fsem(f"ss{c}"), 1)
            for i in range(3):
                ps = fill(f"cnp{i}")
                for c in range(4):
                    last = tr(ps[0:CH, c * P:(c + 1) * P], qe[:, 4 * i + c, SEQ:SEQ + CH])
                last.then_inc(fsem(f"cnp{i}"), 1)
            pe.wait_ge(packed, QKV_T + PG)
            for i in range(3):
                ps = fill(f"cns{i}")
                for c in range(4):
                    last = tr(ps[0:DB * CH, c * P:(c + 1) * P], clast[:, 4 * i + c, :])
                last.then_inc(fsem(f"cns{i}"), 1)
            ps = fill("npp")
            for c in range(PG):
                last = tr(ps[0:PH, c * P:(c + 1) * P], ue[:, c, SEQ:SEQ + PH])
            last.then_inc(fsem("npp"), 1)
            ps = fill("nps")
            for c in range(PG):
                last = tr(ps[0:NSAMP, c * P:(c + 1) * P], ulast[:, c, :])
            last.then_inc(fsem("nps"), 1)
            pe.wait_ge(norm_ready, 8)
            pe.wait_ge(ct_ready, QKV_T)
            for pre, c0 in (("kN", 4), ("vN", 8)):
                for t, (t0, n) in enumerate(TILES):
                    ps = fill(f"{pre}{t}")
                    for h in range(HEADS):
                        last = tr(ps[0:n, h * P:(h + 1) * P], ct[:, c0 + h, t0:t0 + n])
                    last.then_inc(fsem(f"{pre}{t}"), 1)
            pe.wait_ge(poolw_in, 16)
            for g in range(PG):
                pe.wait_ge(d_ready, g + 1)
                ps = fill(f"pm{g}")
                mm(ps[:, 0:SEQ], poolw[:, g, :], prompt_cols(ue, g, PH), start=True, stop=True)
                mm(ps[:, SEQ:T], poolw[:, g, :], sample_cols(ue, g, PH), start=True, stop=True
                   ).then_inc(fsem(f"pm{g}"), 1)
            pe.wait_ge(consts, 3)
            pe.wait_ge(v_mark, VM["g"])
            ps = fill("gcs")
            for t, (L, one, t0, n) in enumerate(tilepart):
                mm(ps[0:n, t * 4:t * 4 + 4], L[0:n, 0:n], gl[0:n, t, :], start=True, stop=True)
                last = mm(ps[0:n, 12 + t * 4:16 + t * 4], one[0:n, 0:n], gl[0:n, t, :], start=True, stop=True)
            last.then_inc(fsem("gcs"), 1)
            ps = fill("egs")
            for h in range(HEADS):
                last = mm(ps[:, h * DB:(h + 1) * DB], gl[0:NSAMP, 2, h:h + 1].broadcast_to([NSAMP, P]),
                          seg[:, 0:NSAMP:DS], start=True, stop=True)
            last.then_inc(fsem("egs"), 1)

            def per_head(name, n, m, lhs, rhs, rows=None):
                ps = fill(name)
                for h in range(HEADS):
                    last = mm(ps[0:n, h * m:(h + 1) * m], lhs(h), rhs(h), start=True, stop=True)
                last.then_inc(fsem(name), 1)

            for t, (L, one, t0, n) in enumerate(tilepart):
                per_head(f"G{t}", n, n, lambda h: gl[0:n, t, h:h + 1].broadcast_to([n, n]), lambda h: L[0:n, 0:n])
                per_head(f"kk{t}", n, n, lambda h: ct[:, 4 + h, t0:t0 + n], lambda h: ct[:, 4 + h, t0:t0 + n])
                per_head(f"qk{t}", n, n, lambda h: ct[:, 4 + h, t0:t0 + n], lambda h: ct[:, h, t0:t0 + n])
            for t, (t0, n) in enumerate(TILES):
                pe.wait_ge(v_mark, VM[f"U{t}"])
                ps = fill(f"T{t}")
                for h in range(HEADS):
                    last = tr(ps[0:n, h * n:(h + 1) * n], scratch[t][3][:, h, :])
                last.then_inc(fsem(f"T{t}"), 1)
            for s in range(1, LEVELS):
                ts = [t for t in range(NT) if t < 2 or s < 3]
                for t in ts:
                    n = TILES[t][1]
                    sc = scratch[t]
                    if s == 1:
                        is_drained(pe, f"T{t}")
                    else:
                        is_drained(pe, f"QT{s - 1}{t}")
                    per_head(f"P{s}{t}", n, n, lambda h: sc[2][:, h, :], lambda h: sc[4][:, h, :])
                for t in ts:
                    n = TILES[t][1]
                    sc = scratch[t]
                    is_drained(pe, f"P{s}{t}")
                    if f"Q{s}{t}" in uses:
                        per_head(f"Q{s}{t}", n, n, lambda h: sc[3][:, h, :], lambda h: sc[5][:, h, :])
                    per_head(f"QT{s}{t}", n, n, lambda h: sc[5][:, h, :], lambda h: sc[3][:, h, :])
            pe.wait_ge(v_mark, VM["kd"])
            is_drained(pe, f"QT{LEVELS - 1}0")
            per_head("v0", P, P, lambda h: scratch[0][3][:, h, :], lambda h: vN[:, 0, h, :])
            is_drained(pe, "v0")
            per_head("S1", P, P, lambda h: kN[:, 0, h, :], lambda h: vN[:, 0, h, :])
            per_head("o0", P, P, lambda h: scratch[0][1][:, h, :], lambda h: vN[:, 0, h, :])
            ps = fill("kqs").rearrange("p (h q t) -> p h q t", h=HEADS, q=2)
            pe.wait_ge(s0_in, 16)
            for h in range(HEADS):
                for b in range(DB):
                    c = SEQ + b * DS
                    last = mm(ps[:, h, :, b * DS:(b + 1) * DS], s0[:, b, h, :], ct[:, h:h + 5:4, c:c + DS],
                              start=True, stop=True)
            last.then_inc(fsem("kqs"), 1)
            is_drained(pe, "S1")
            per_head("kS1", P, P, lambda h: ct[:, 4 + h, P:SEQ], lambda h: S1[:, h, :])
            per_head("qS1", P, P, lambda h: ct[:, h, P:SEQ], lambda h: S1[:, h, :])
            is_drained(pe, "kqs")
            for nm, q in (("R2k", 1), ("R2q", 0)):
                ps = fill(nm)
                for h in range(HEADS):
                    last = tr(ps[0:NSAMP, h * P:(h + 1) * P], kqS[:, h, q * NSAMP:(q + 1) * NSAMP])
                last.then_inc(fsem(nm), 1)
            is_drained(pe, "kS1")
            per_head("v1", P, P, lambda h: scratch[1][3][:, h, :], lambda h: vN[:, 1, h, :])
            is_drained(pe, "R2k")
            per_head("v2", NSAMP, P, lambda h: scratch[2][3][:, h, :], lambda h: vN[0:NSAMP, 2, h, :])
            is_drained(pe, "v1")
            per_head("o1", P, P, lambda h: scratch[1][1][:, h, :], lambda h: vN[:, 1, h, :])
            per_head("S2", P, P, lambda h: kN[:, 1, h, :], lambda h: vN[:, 1, h, :])
            is_drained(pe, "v2")
            per_head("o2", NSAMP, P, lambda h: scratch[2][1][:, h, :], lambda h: vN[0:NSAMP, 2, h, :])
            pe.wait_ge(v_mark, VM["rs_o"])
            for t, (t0, n) in enumerate(TILES):
                ps = fill(f"oT{t}")
                for h in range(HEADS):
                    last = tr(ps[:, h * n:(h + 1) * n], oN[t][0:n, h, :])
                last.then_inc(fsem(f"oT{t}"), 1)
            for h in range(HEADS):
                pe.wait_ge(v_mark, VM[f"vm{h}"])
                for q in range(2):
                    nm = f"ns{h}{'ab'[q]}"
                    mm(fill(nm), kN[0:NSAMP, 2, h, :],
                       vmask[:, 4 * q:4 * q + 4, :].rearrange("p b d -> p (b d)"), start=True, stop=True
                       ).then_inc(fsem(nm), 1)
            pe.wait_ge(wout_in, 32)
            wo = ring[:, 5:7, :].rearrange("p s (k f) -> p (s k) f", k=4)
            for t in range(NT):
                is_drained(pe, f"oT{t}")
            for g in range(PG):
                is_drained(pe, f"pm{g}")
            for t, (t0, n) in enumerate(TILES):
                for hf in range(2):
                    ps = fill(f"op{t}{hf}")
                    for k in range(KT):
                        last = mm(ps[0:n, :], hT[:, k, t0:t0 + n], wo[:, k, hf * 512:(hf + 1) * 512],
                                  start=(k == 0), stop=(k == KT - 1))
                    last.then_inc(fsem(f"op{t}{hf}"), 1)
            pe.wait_ge(v_mark, VM["h2"])
            transposes("rT")
            pe.wait_ge(smalls_in, 64)
            for t in range(NT):
                for hf in range(2):
                    is_drained(pe, f"rT{t}{hf}")
            ps = fill("lg")
            for k in range(KT):
                last = mm(ps[0:E, 0:T], wrout[:, k, :], hT[:, k, :], start=(k == 0), stop=(k == KT - 1))
            last.then_inc(fsem("lg"), 1)
            is_drained(pe, "lg")
            ps = fill("lgT")
            for t, (t0, n) in enumerate(TILES):
                last = tr(ps[0:n, t * E:(t + 1) * E], logT[:, t0:t0 + n])
            last.then_inc(fsem("lgT"), 1)
            pe.wait_ge(v_mark, VM["sel"])
            ps = fill("rk")
            for t in range(NT):
                for u in range(t):
                    mm(ps[:, t * E:(t + 1) * E], ones[:, :], sel[:, u, :], start=(u == 0), stop=False)
                mm(ps[:, t * E:(t + 1) * E], strict[:, :], sel[:, t, :], start=(t == 0), stop=True)
            for u in range(NT):
                last = mm(ps[:, NT * E:(NT + 1) * E], ones[:, :], sel[:, u, :], start=(u == 0), stop=(u == NT - 1))
            last.then_inc(fsem("rk"), 1)

            def gather(k0, fills, s_ready):
                for hf in range(2):
                    ps, sm_ = fills(k0 + hf)
                    for t in range(NT):
                        last = mm(ps, Ssel[:, t, :], h3[:, t, hf * 512:(hf + 1) * 512], start=(t == 0), stop=(t == NT - 1))
                    last.then_inc(sm_, 1)

            def turn(k0, fills, src):
                for hf in range(2):
                    ps, sm_ = fills(k0 + hf)
                    for k in range(4):
                        c0 = (hf * 4 + k) * P
                        last = tr(ps[:, k * P:(k + 1) * P], src[:, c0:c0 + P])
                    last.then_inc(sm_, 1)

            pe.wait_ge(v_mark, VM["split"])
            def first_pair(r_):
                names = [f"{n}{r_}" for n in ("ga", "gb", "xta", "xtb", "sgt")]
                gather(0, lambda k: (fill(names[k]), fsem(names[k])), None)
                is_drained(pe, names[0]), is_drained(pe, names[1])
                turn(2, lambda k: (fill(names[k]), fsem(names[k])), xg)
                ps = fill(names[4])
                for t in range(NT):
                    last = tr(ps[:, t * P:(t + 1) * P], Sgat[:, t, :])
                last.then_inc(fsem(names[4]), 1)
                for n in names[2:]:
                    is_drained(pe, n)

            for s in (g_act, up_act, y_act):
                pe.nop().then_inc(s, 1)
            def turns(lo, hi, base):
                with pe.Fori(lo, hi) as i:
                    for half in range(2):
                        pair = i * 2 + half

                        def aux(k):
                            l = 13 * half + k
                            b, m = 6 + l % 2, l // 2
                            pe.wait_ge(drained[b], base[b] + m + i * 13)
                            return PS[:, b, :], filled[b]

                        def product(c0, b0, lhs, bias):
                            for hf in range(2):
                                mm(PS[:, b0 + hf, :], ind[:, half, :],
                                   biases[bias][:, hf * 512:(hf + 1) * 512], start=True, stop=False, skip_group_check=True)
                            for c in range(c0, c0 + CPM):
                                pe.wait_ge(chunk_in[half * CPP + c], i * 32 + 32)
                                w = slot(half * CPP + c)
                                for kk in range(2):
                                    k = (c - c0) * 2 + kk
                                    for hf in range(2):
                                        for a_ in range(2):
                                            last = mm(PS[64 * a_:64 * a_ + 64, b0 + hf, :], lhs[:, k, 64 * a_:64 * a_ + 64],
                                                      w[:, a_, kk, hf * 512:(hf + 1) * 512],
                                                      start=False, stop=(k == KT - 1),
                                                      skip_group_check=True)
                                last.then_inc(chunk_used, 1)

                        pe.wait_ge(pair_sel, pair + 1)
                        pe.wait_ge(drained[6], base[6] + i * 13 + 7 * half)
                        pe.wait_ge(drained[7], base[7] + i * 13 + 6 * half)
                        pe.wait_ge(g_act, pair + 1)
                        product(0, 0, xgT, 0)
                        pe.wait_ge(up_act, pair + 1)
                        product(CPM, 2, xgT, 1)
                        pe.wait_ge(pair_sel, pair + 2)
                        gather(0, aux, None)
                        pe.wait_ge(y_act, pair + 1)
                        pe.wait_ge(v_mark, VM["ybuf_zero" if lo == 0 else "ybuf_zero_mid"])
                        for t, (t0, n) in enumerate(TILES):
                            for hf in range(2):
                                ps, sm_ = aux(2 + 2 * t + hf)
                                mm(ps[0:n, :], SgT[1 - half][:, t, 0:n], ybuf[:, hf * 512:(hf + 1) * 512],
                                   start=True, stop=True).then_inc(sm_, 1)
                        pe.wait_ge(hid_act, pair + 1)
                        turn(8, aux, ubuf)
                        ps, sm_ = aux(10)
                        for t in range(NT):
                            last = tr(ps[:, t * P:(t + 1) * P], Sgat[:, t, :])
                        last.then_inc(sm_, 1)
                        turn(11, aux, xg)
                        product(2 * CPM, 4, hidT, 2)
            def scatter(fillb, sg):
                for t, (t0, n) in enumerate(TILES):
                    for hf in range(2):
                        ps, sm_ = fillb(t, hf)
                        mm(ps[0:n, :], sg[:, t, 0:n], ybuf[:, hf * 512:(hf + 1) * 512], start=True, stop=True
                           ).then_inc(sm_, 1)

            def run_of_pairs(r_):
                lo, hi = r_ * MID, r_ * (TURNS - MID) + MID
                first_pair(r_)
                turns(lo, hi, bases[r_])
                for b in (6, 7):
                    seen[b] += 13 * (hi - lo)

            def last_scatter(r_):
                pe.wait_ge(y_act, 2 * MID * (r_ + 1) + 1)
                scatter(lambda t, hf: (fill(f"sc{r_}{t}{hf}"), fsem(f"sc{r_}{t}{hf}")), SgT[1])

            pe.wait_ge(pair_sel, 1)
            run_of_pairs(0)
            last_scatter(0)
            for t in range(1, NT):
                is_drained(pe, f"sc0{t}0"), is_drained(pe, f"sc0{t}1")
            for s in ov_drained:
                pe.nop().then_inc(s, 1)
            pe.wait_ge(v_mark, VM["table"])
            n_ov = pe.value_load(ov_n[0:1, 0:1], min_val=0, max_val=OV_MAX)
            with pe.Fori(0, OV_GROUPS) as grp:
                with pe.If(grp * OV_PER < n_ov):
                    with pe.Fori(0, OV_PER) as jj:
                        j = grp * OV_PER + jj
                        with pe.If(j < n_ov):
                            def ovaux(k):
                                b, m = k % 2, k // 2
                                pe.wait_ge(ov_drained[b], m + 1 + j * 7)
                                return PS[:, 6 + b, :], ov_filled[b]

                            def ovproduct(c0, b0, lhs, bias):
                                for hf in range(2):
                                    mm(PS[:, b0 + hf, :], ind[:, 0, :],
                                       biases[bias][:, hf * 512:(hf + 1) * 512], start=True, stop=False)
                                for c in range(c0, c0 + 2):
                                    pe.wait_ge(ovch_in[c], j * 16 + 16)
                                    w = ring[:, c, :].rearrange("p (k f) -> p k f", k=4)
                                    for kk in range(4):
                                        k = (c - c0) * 4 + kk
                                        for hf in range(2):
                                            last = mm(PS[:, b0 + hf, :], lhs[:, k, :], w[:, kk, hf * 512:(hf + 1) * 512],
                                                      start=False, stop=(k == KT - 1))
                                    last.then_inc(ov_used, 1)

                            def ovdrained(k):
                                pe.wait_ge(ov_drained[k % 2], k // 2 + 2 + j * 7)

                            pe.wait_ge(ov_sel, j + 1)
                            gather(0, ovaux, None)
                            ovdrained(0), ovdrained(1)
                            turn(2, ovaux, xg)
                            ovdrained(2), ovdrained(3)
                            ovproduct(0, 0, xgT, 0)
                            ovproduct(2, 2, xgT, 1)
                            pe.wait_ge(ovh_act, j + 1)
                            turn(4, ovaux, ubuf)
                            for k, ts in ((6, (0, 1)), (7, (2,))):
                                ps, sm_ = ovaux(k)
                                for q, t in enumerate(ts):
                                    last = tr(ps[:, q * P:(q + 1) * P], Sgat[:, t, :])
                                last.then_inc(sm_, 1)
                            ovdrained(4), ovdrained(5)
                            ovproduct(4, 4, hidT, 2)
                            pe.wait_ge(ovy_act, j + 1)
                            ovdrained(6), ovdrained(7)
                            scatter(lambda t, hf: ovaux(8 + 2 * t + hf), SgT[0])
            pe.wait_ge(v_mark, VM["sel_mid"])
            for s in ov_drained:
                pe.wait_ge(s, n_ov * 7 + 1)
            run_of_pairs(1)
            pe.wait_ge(tail_in, 16 * 4)
            for k in range(2):
                ps = fill(f"pT{k}")
                for t, (t0, n) in enumerate(TILES):
                    last = tr(ps[:, t0:t0 + n], pin[0:n, t, k * P:(k + 1) * P])
                last.then_inc(fsem(f"pT{k}"), 1)
            last_scatter(1)
            is_drained(pe, "pT0"), is_drained(pe, "pT1")
            for t, (t0, n) in enumerate(TILES):
                for hf in range(2):
                    cs = slice(hf * 512, (hf + 1) * 512)
                    ps = fill(f"pp{t}{hf}")
                    for k in range(2):
                        last = mm(ps[0:n, :], pT[:, k, t0:t0 + n], wple[:, k, cs], start=(k == 0), stop=(k == 1))
                    last.then_inc(fsem(f"pp{t}{hf}"), 1)
            transposes("tT", "h3")
            pe.wait_ge(wpg_in, 16)
            for t, (t0, n) in enumerate(TILES):
                is_drained(pe, f"tT{t}0"), is_drained(pe, f"tT{t}1")
                for hf in range(2):
                    cs = slice(hf * 512, (hf + 1) * 512)
                    ps = fill(f"pg{t}{hf}")
                    for k in range(KT):
                        last = mm(ps[0:n, :], hT[:, k, t0:t0 + n], wpg[:, k, cs], start=(k == 0), stop=(k == KT - 1))
                    last.then_inc(fsem(f"pg{t}{hf}"), 1)

        @block.vector
        def _(dve):
            step = chain(dve, v_step)
            v = nc.vector
            marked = [0]
            roots = [0]

            def mark(ins, name):
                marked[0] += 1
                assert VM[name] == marked[0], (name, VM[name], marked[0])
                ins.then_inc(v_mark, 1)
                dve.wait_ge(v_mark, marked[0])

            def drain(ins, name):
                step(ins, dsem(name), uses[name][1] + 1)

            def over(ap, h, m):
                n = ap.shape[0]
                return ap.unsqueeze(2).broadcast_to([n, h, m])

            def heads(ap, m):
                n = ap.shape[0]
                return ap.unsqueeze(1).broadcast_to([n, HEADS, m])

            def rsqrt_of(ap, in_, scale, eps=EPS):
                step(v.tensor_scalar(ap, in_, scale, eps, ALU.mult, ALU.add))
                step(v.reciprocal(ap, ap), inv_ready)
                roots[0] += 1
                dve.wait_ge(root_ready, roots[0])

            step(v.memset(small[:, :], 0.0), small_zero)
            dve.wait_ge(a_mark, AM["ss"])
            rsqrt_of(rstd[:, :], ss[:, :], 1.0 / D_MODEL)
            for t, (t0, n) in enumerate(TILES):
                step(v.tensor_scalar(h3[0:n, t, :], x3[0:n, t, :], rstd[0:n, t:t + 1], None, ALU.mult), h_ready)

            def evac_hT(prefix, ln):
                for t, (t0, n) in enumerate(TILES):
                    for hf in range(2):
                        name = f"{prefix}{t}{hf}"
                        is_filled(dve, name)
                        w = vec(ln, hf * 4, 4).unsqueeze(2).broadcast_to([P, 4, n])
                        drain(v.tensor_tensor(hT[:, hf * 4:hf * 4 + 4, t0:t0 + n],
                                              bank(name)[:, 0:4 * n].rearrange("p (k t) -> p k t", k=4), w,
                                              ALU.mult), name)
            is_drained(dve, "vec")
            evac_hT("hT", "ln_mix")
            is_filled(dve, "ba")
            bav = bank("ba")[:, 0:24].rearrange("p (t c) -> p t c", t=NT)
            dve.wait_ge(smalls_in, 64)
            for t, (t0, n) in enumerate(TILES):
                step(v.tensor_tensor(tmp12[0:n, t, :], bav[0:n, t, HEADS:2 * HEADS], dtb[0:n, :], ALU.add))
                ins = v.tensor_copy(beta[0:n, t, :], bav[0:n, t, 0:HEADS])
                drain(ins, "ba") if t == NT - 1 else step(ins)
            mark(v.tensor_scalar(gl[:, :, :], tmp12[:, :, :], 0.0, None, ALU.max), "ba")
            mark(v.scalar_tensor_tensor(out=tmp12[:, :, :], in0=tmp12[:, :, :], scalar=-1.0, in1=tmp12[:, :, :],
                                        op0=ALU.mult, op1=ALU.max), "sp_in")

            def conv(c):
                is_drained(dve, f"pr{c + 4}")
                is_drained(dve, "sc")
                dve.wait_ge(ext_zero, PG + QKV_T)
                for out, col in ((ct[:, c, 0:SEQ], lambda j: qe[:, c, j:j + SEQ]),
                                 (ct[:, c, SEQ:T].rearrange("p (b s) -> p b s", b=DB),
                                  lambda j: sample_cols(qe, c, CH, j))):
                    step(v.tensor_scalar(out, col(0), vec("conv_w", c), None, ALU.mult))
                    for j in range(1, CONV):
                        ins = v.scalar_tensor_tensor(out=out, in0=col(j), scalar=vec("conv_w", j * QKV_T + c),
                                                     in1=out, op0=ALU.mult, op1=ALU.add)
                        step(ins, acc_ready if j == CONV - 1 and len(out.shape) == 3 else None)

            for c in [4, 5, 6, 7, 0, 1, 2, 3]:
                conv(c)
            for c in range(8 + 2):
                if c < 8:
                    f = float(P) if c < 4 else 1.0
                    is_filled(dve, f"ss{c}")
                    drain(v.tensor_scalar(rnb[c % 3], bank(f"ss{c}")[:, 0:T], f, f * EPS, ALU.mult, ALU.add), f"ss{c}")
                    step(v.reciprocal(rnb[c % 3], rnb[c % 3]), inv_ready)
                if c >= 2:
                    roots[0] += 1
                    dve.wait_ge(root_ready, roots[0])
                    step(v.tensor_tensor(ct[:, c - 2, :], ct[:, c - 2, :], rnb[(c - 2) % 3], ALU.mult), norm_ready)
            for c in range(8, 12):
                conv(c)
            dve.wait_ge(a_mark, AM["lg"])
            step(v.tensor_scalar(beta[:, :, :], beta[:, :, :], 1.0, None, ALU.add))
            step(v.reciprocal(beta[:, :, :], beta[:, :, :]))
            step(v.tensor_tensor(gl[:, :, :], gl[:, :, :], tmp12[:, :, :], ALU.add))
            step(v.tensor_tensor(gl[:, :, :], gl[:, :, :], alog.unsqueeze(1).broadcast_to([P, NT, HEADS]), ALU.mult))
            mark(v.tensor_scalar(gl[:, :, :], gl[:, :, :], -1.0, None, ALU.mult), "g")
            dve.wait_ge(consts, 3)
            step(v.tensor_scalar(inv16, iotaf[:, 0:16], 1.0, None, ALU.add))
            step(v.reciprocal(inv16, inv16))
            is_filled(dve, "npp"), is_filled(dve, "nps")
            for c, w in enumerate(WINDOWS):
                dve.wait_ge(g_ready, c + 1)
                pv = ptmp[:, :].unsqueeze(1)
                iv = inv16[:, 0:w]
                step(v.tensor_tensor(ptmp[:, PH:PH + w], ptmp[:, PH:PH + w], iv, ALU.mult))
                u0 = ue[:, c, PH:PH + w]
                step(v.tensor_tensor(u0, ptmp[:, PH:PH + w], u0, ALU.subtract))
                u1 = ue[:, c, PH + w:PH + SEQ]
                step(v.scalar_tensor_tensor(out=u1, in0=ptmp[:, PH + w:PH + SEQ], scalar=1.0 / w, in1=u1,
                                            op0=ALU.mult, op1=ALU.subtract))
                u2 = sample_cols(ue, c, PH)
                step(v.scalar_tensor_tensor(out=u2, in0=sample_cols(pv, 0, PH), scalar=1.0 / w, in1=u2,
                                            op0=ALU.mult, op1=ALU.subtract), d_ready)
                step(v.memset(small[:, 159:160], 0.0), acc_pool)
            is_filled(dve, "gcs")
            for t, (t0, n) in enumerate(TILES):
                step(v.tensor_copy(gc[0:n, t, :], bank("gcs")[0:n, t * 4:t * 4 + 4]))
                ins = v.tensor_copy(egl[0:n, t, :], bank("gcs")[0:n, 12 + t * 4:16 + t * 4])
                drain(ins, "gcs") if t == NT - 1 else step(ins)
            mark(v.tensor_tensor(kdec[:, :, :], egl[:, :, :], gc[:, :, :], ALU.subtract), "gcs")
            for g in range(PG):
                is_filled(dve, f"pm{g}")
                drain(v.tensor_scalar(hT[:, g, :], bank(f"pm{g}")[:, 0:T], vec("pool_scale", g), None, ALU.mult), f"pm{g}")

            def ps4(name, n, m):
                return bank(name)[0:n, 0:HEADS * m].rearrange("p (h t) -> p h t", h=HEADS)

            for t, (t0, n) in enumerate(TILES):
                D = scratch[t][0]
                is_filled(dve, f"G{t}")
                drain(v.tensor_tensor(D, ps4(f"G{t}", n, n), over(gc[0:n, t, :], HEADS, n), ALU.subtract), f"G{t}")
                mark(v.tensor_scalar(D, D, 0.0, None, ALU.min), f"diff{t}")
            for t, (L, one, t0, n) in enumerate(tilepart):
                D, At, N, Um, Tm, Pm = scratch[t]
                dve.wait_ge(a_mark, AM[f"E{t}"])
                step(v.tensor_tensor(D, D, heads(L[0:n, 0:n], n), ALU.mult))
                is_filled(dve, f"kk{t}")
                drain(v.tensor_tensor(N, ps4(f"kk{t}", n, n), D, ALU.mult), f"kk{t}")
                is_filled(dve, f"qk{t}")
                drain(v.tensor_tensor(At, ps4(f"qk{t}", n, n), D, ALU.mult), f"qk{t}")
                step(v.tensor_tensor(N, N, over(beta[0:n, t, :], HEADS, n), ALU.mult))
                step(v.tensor_tensor(Pm, N, heads(lmask[0:n, 0, 0:n], n), ALU.mult))
                mark(v.tensor_tensor(Um, heads(ident[0:n, 0:n], n), Pm, ALU.subtract), f"U{t}")
            for t, (t0, n) in enumerate(TILES):
                is_filled(dve, f"T{t}")
                drain(v.tensor_copy(scratch[t][4], ps4(f"T{t}", n, n)), f"T{t}")
            for s in range(1, LEVELS):
                ts = [t for t in range(NT) if t < 2 or s < 3]
                for t in ts:
                    n = TILES[t][1]
                    is_filled(dve, f"P{s}{t}")
                    drain(v.tensor_tensor(scratch[t][5], ps4(f"P{s}{t}", n, n), heads(lmask[0:n, s, 0:n], n), ALU.mult),
                          f"P{s}{t}")
                for t in ts:
                    n = TILES[t][1]
                    for nm, m in ((f"Q{s}{t}", 4), (f"QT{s}{t}", 3)):
                        if nm in uses:
                            is_filled(dve, nm)
                            drain(v.tensor_tensor(scratch[t][m], scratch[t][m], ps4(nm, n, n), ALU.subtract), nm)
            for t, (t0, n) in enumerate(TILES):
                is_drained(dve, f"kN{t}")
                dve.wait_ge(a_mark, AM["gexp"])
                ins = v.tensor_tensor(kN[0:n, t], kN[0:n, t], over(kdec[0:n, t, :], HEADS, P), ALU.mult)
                mark(ins, "kd") if t == NT - 1 else step(ins)

            def new_value(t, name):
                n = TILES[t][1]
                is_filled(dve, name)
                drain(v.tensor_tensor(vN[0:n, t], ps4(name, n, P), over(beta[0:n, t, :], HEADS, P), ALU.mult), name)

            new_value(0, "v0")
            is_filled(dve, "S1")
            drain(v.tensor_copy(S1, ps4("S1", P, P)), "S1")
            is_filled(dve, "kqs")
            drain(v.tensor_copy(kqS, bank("kqs").rearrange("p (h t) -> p h t", h=HEADS)), "kqs")
            is_filled(dve, "o0")
            drain(v.tensor_copy(oN[0], ps4("o0", P, P)), "o0")
            E1, T1 = scratch[1][0], scratch[1][4]
            is_filled(dve, "kS1")
            step(v.tensor_tensor(E1, ps4("kS1", P, P), over(egc[:, 1, :], HEADS, P), ALU.mult))
            drain(v.tensor_tensor(vN[:, 1], vN[:, 1], E1, ALU.subtract), "kS1")
            is_filled(dve, "qS1")
            drain(v.tensor_tensor(T1, ps4("qS1", P, P), over(egc[:, 1, :], HEADS, P), ALU.mult), "qS1")
            step(v.tensor_tensor(S1, S1, over(egl[:, 1, :], HEADS, P), ALU.mult))
            is_filled(dve, "R2k")
            step(v.tensor_tensor(oN[2], ps4("R2k", NSAMP, P), over(egc[0:NSAMP, 2, :], HEADS, P), ALU.mult))
            drain(v.tensor_tensor(vN[0:NSAMP, 2], vN[0:NSAMP, 2], oN[2], ALU.subtract), "R2k")
            is_filled(dve, "R2q")
            drain(v.tensor_tensor(qS2, ps4("R2q", NSAMP, P), over(egc[0:NSAMP, 2, :], HEADS, P), ALU.mult), "R2q")
            new_value(1, "v1")
            new_value(2, "v2")
            is_filled(dve, "o1")
            drain(v.tensor_tensor(oN[1], ps4("o1", P, P), T1, ALU.add), "o1")
            is_filled(dve, "S2")
            mark(v.tensor_tensor(S1, S1, ps4("S2", P, P), ALU.add), "S2")
            drain(v.tensor_copy(oss[:, 0:1], bank("S2")[:, 0:1]), "S2")
            is_filled(dve, "o2")
            drain(v.tensor_tensor(oN[2], ps4("o2", NSAMP, P), qS2, ALU.add), "o2")
            for t, (t0, n) in enumerate(TILES):
                sq = (scratch[0][0], scratch[1][0], ring[0:NSAMP, 4, 512:1024].rearrange("p (h d) -> p h d", h=HEADS))[t]
                step(v.tensor_tensor(sq, oN[t][0:n], oN[t][0:n], ALU.mult))
                step(v.tensor_reduce(tmp12[0:n, t, :], sq, AX_X, ALU.add))
            rsqrt_of(tmp12[:, :, :], tmp12[:, :, :], 1.0 / P)
            for t, (t0, n) in enumerate(TILES):
                ins = v.tensor_tensor(oN[t][0:n], oN[t][0:n], over(tmp12[0:n, t, :], HEADS, P), ALU.mult)
                mark(ins, "rs_o") if t == NT - 1 else step(ins)
            for t, (t0, n) in enumerate(TILES):
                is_filled(dve, f"oT{t}")
                is_drained(dve, "pr19")
                drain(v.scalar_tensor_tensor(out=hT[:, 4:8, t0:t0 + n], in0=ps4(f"oT{t}", P, n),
                                             scalar=vec("dn_norm"), in1=zT[:, :, t0:t0 + n],
                                             op0=ALU.mult, op1=ALU.mult), f"oT{t}")
            for h in range(HEADS):
                if h:
                    is_filled(dve, f"ns{h - 1}b")
                mark(v.tensor_tensor(vmask, vN[0:NSAMP, 2, h, :].unsqueeze(1).broadcast_to([NSAMP, DB, P]),
                                     seg[:, 0:NSAMP:DS].unsqueeze(2).broadcast_to([NSAMP, DB, P]), ALU.mult), f"vm{h}")
                dve.wait_ge(g_ready, PG + h + 1)
                for q in range(2):
                    nm = f"ns{h}{'ab'[q]}"
                    is_filled(dve, nm)
                    sv = s0[:, 4 * q:4 * q + 4, h, :]
                    drain(v.tensor_tensor(sv, sv, ps4(nm, P, P), ALU.add), nm)
            mark(v.memset(oss[:, 0:1], 0.0), "S0")
            dve.wait_ge(bias_in, 16 * 9)
            step(v.tensor_copy(bias3, bias_f))
            for lo, hi in ((E, 3 * E), (2 * E, 3 * E)):
                for p0 in range(lo, hi, E):
                    rows = slice(p0, p0 + E)
                    step(v.tensor_tensor(bias_f[rows], bias_f[rows], bias3[rows], ALU.subtract))
                    ins = v.tensor_copy(bias3[rows], bias_f[rows])
                    mark(ins, "split") if lo == 2 * E else step(ins)
            dve.wait_ge(xagain_in, 16 * NT)
            for t, (t0, n) in enumerate(TILES):
                for hf in range(2):
                    nm = f"op{t}{hf}"
                    is_filled(dve, nm)
                    xs = x3[0:n, t, hf * 512:(hf + 1) * 512]
                    drain(v.tensor_tensor(xs, bank(nm)[0:n, :], xs, ALU.add), nm)
            mark(v.memset(H[64:P, 2048:3072], 0.0), "x2")
            dve.wait_ge(a_mark, AM["ss2"])
            rsqrt_of(rstd[:, :], ss[:, :], 1.0 / D_MODEL)
            for t, (t0, n) in enumerate(TILES):
                ins = v.tensor_scalar(h3[0:n, t, :], x3[0:n, t, :], rstd[0:n, t:t + 1], None, ALU.mult)
                mark(ins, "h2") if t == NT - 1 else step(ins)
            evac_hT("rT", "ln_moe")
            step(v.memset(Lg[:, :, :], 0.0))
            is_filled(dve, "lgT")
            for t, (t0, n) in enumerate(TILES):
                ins = v.tensor_copy(Lg[0:n, t, :], bank("lgT")[0:n, t * E:(t + 1) * E])
                drain(ins, "lgT") if t == NT - 1 else step(ins)
            for t in range(NT):
                step(v.max(m8[:, t, :], Lg[:, t, :]))
            mark(v.tensor_tensor(exq[:, :, :], Lg[:, :, :], m8[:, :, 0:1].broadcast_to([P, NT, E]), ALU.subtract), "m8")
            kth = m8[:, :, TOPK - 1:TOPK].broadcast_to([P, NT, E])
            step(v.tensor_tensor(gtm[:, :, :], Lg[:, :, :], kth, ALU.is_gt))
            step(v.tensor_tensor(eqm[:, :, :], Lg[:, :, :], kth, ALU.is_equal))
            step(v.tensor_reduce(ngt, gtm[:, :, :], AX_X, ALU.add))
            for t in range(NT):
                step(v.tensor_tensor_scan(cum[:, t, :], ones[:, 0:E], eqm[:, t, :], 0.0, ALU.mult, ALU.add))
            step(v.tensor_tensor(cum[:, :, :], cum[:, :, :], ngt.unsqueeze(2).broadcast_to([P, NT, E]), ALU.add))
            step(v.tensor_scalar(cum[:, :, :], cum[:, :, :], float(TOPK), None, ALU.is_le))
            step(v.tensor_tensor(eqm[:, :, :], eqm[:, :, :], cum[:, :, :], ALU.mult))
            step(v.tensor_tensor(sel[:, :, :], gtm[:, :, :], eqm[:, :, :], ALU.add))
            mark(v.memset(sel[NSAMP:P, NT - 1, :], 0.0), "sel")
            dve.wait_ge(a_mark, AM["exq"])
            step(v.tensor_tensor(exq[:, :, :], exq[:, :, :], sel[:, :, :], ALU.mult))
            step(v.tensor_reduce(den, exq[:, :, :], AX_X, ALU.add))
            step(v.tensor_scalar(den, den, 1e-30, None, ALU.max))
            step(v.reciprocal(den, den))
            mark(v.tensor_tensor(gate[:, 0:E, :].rearrange("p e t -> p t e"), exq[:, :, :],
                                 den.unsqueeze(2).broadcast_to([P, NT, E]), ALU.mult), "gates")
            is_filled(dve, "rk")
            rkv = bank("rk")[:, 0:NT * E].rearrange("p (t e) -> p t e", t=NT)
            rankv = rank[:, 0:E, :].rearrange("p e t -> p t e")
            step(v.scalar_tensor_tensor(out=exq[:, :, :], in0=rkv, scalar=1.0, in1=sel[:, :, :],
                                        op0=ALU.add, op1=ALU.mult))
            step(v.tensor_scalar(rankv, exq[:, :, :], -1.0, None, ALU.add))
            drain(v.tensor_copy(cnt, bank("rk")[:, NT * E:(NT + 1) * E]), "rk")

            def select(out_sem, value, half, rank_pair, gate_pair, experts):
                io = iotaf[:, 0:CAP].unsqueeze(1).unsqueeze(1).broadcast_to([P, NT, 2, CAP])
                sv = Ssel.rearrange("p t (a s) -> p t a s", a=2)
                gv = Sgat.rearrange("p t (a s) -> p t a s", a=2)
                rv = rank_pair.rearrange("p a t -> p t a").unsqueeze(3).broadcast_to([P, NT, 2, CAP])
                ev = gate_pair.rearrange("p a t -> p t a").unsqueeze(3).broadcast_to([P, NT, 2, CAP])
                return [v.tensor_tensor, (sv, io, rv, ALU.is_equal)], [v.tensor_tensor, (gv, sv, ev, ALU.mult)], \
                    [v.tensor_copy, (ind[:, half, :].rearrange("p (a s) -> p a s", a=2),
                                     experts.unsqueeze(2).broadcast_to([3 * E, 2, CAP]))]

            def run(op):
                return op[0](*op[1])

            def scaled_turn(name, k0):
                w = vec("ln_moe", k0, 4).unsqueeze(2).broadcast_to([P, 4, P])
                return (xgT[:, k0:k0 + 4, :], name.rearrange("p (k s) -> p k s", k=4), w, ALU.mult)

            def first_pair(r_):
                e = 4 * MID * r_
                a1, a2, a3 = select(None, None, 0, rank[:, e:e + 2, :], gate[:, e:e + 2, :], ident3[:, e:e + 2])
                step(run(a1)), step(run(a2))
                mark(run(a3), "sel_mid") if r_ else step(run(a3), pair_sel)
                for nm, k0 in ((f"xta{r_}", 0), (f"xtb{r_}", 4)):
                    is_filled(dve, nm)
                    drain(v.tensor_tensor(*scaled_turn(bank(nm), k0)), nm)
                mark(v.memset(ybuf, 0.0), "ybuf_zero_mid" if r_ else "ybuf_zero")
                is_filled(dve, f"sgt{r_}")

            first_pair(0)
            for bi, off in enumerate(OV_OFF):
                step(v.tensor_scalar(flg[:, :, bi], cnt, float(off), None, ALU.is_gt))
                step(v.memset(ovec[:, :, bi], float(off)))
                step(v.tensor_copy(evec[:, :, bi], iotaf[:, 0:E]))
            flat = flg.rearrange("p e b -> p (e b)")
            step(v.tensor_tensor_scan(pos, ones[:, 0:2 * E], flat, 0.0, ALU.mult, ALU.add))
            step(v.tensor_tensor(evec, evec, flg, ALU.mult))
            step(v.tensor_tensor(ovec, ovec, flg, ALU.mult))
            dve.wait_ge(ssm_stored, 16)
            for src, dst in ((evec, ove_f), (ovec, ov_off[:, :])):
                step(v.tensor_tensor(cmp_, pos.unsqueeze(1).broadcast_to([P, OV_SLOTS, 64]),
                                     iotaf[:, 1:OV_SLOTS + 1].unsqueeze(2).broadcast_to([P, OV_SLOTS, 64]), ALU.is_equal))
                step(v.tensor_tensor(cmp_, cmp_, src.rearrange("p e b -> p (e b)").unsqueeze(1)
                                     .broadcast_to([P, OV_SLOTS, 64]), ALU.mult))
                step(v.tensor_reduce(dst, cmp_, AX_X, ALU.add))
            step(v.tensor_copy(ov_e[:, :], ove_f))
            mark(v.tensor_copy(ov_n[:, :], pos[:, 63:64]), "table")

            def turns(lo, hi, base):
                with dve.Fori(lo, hi) as i:
                    VPP = 3 + 2
                    for half in range(2):
                        pair = i * 2 + half
                        cnt_ = [0]

                        def lstep(ins):
                            cnt_[0] += 1
                            k = half * VPP + cnt_[0]
                            ins.then_inc(v_loop, 1)
                            dve.wait_ge(v_loop, i * (2 * VPP) + k)

                        def lmark(ins, s, value):
                            ins.then_inc(s, 1)
                            dve.wait_ge(s, value)

                        def aux(k, op, *args):
                            l = 13 * half + k
                            b, m = 6 + l % 2, l // 2
                            dve.wait_ge(filled[b], base[b] + 1 + m + i * 13)
                            lmark(op(*args), drained[b], base[b] + 1 + m + i * 13)

                        def auxbank(k):
                            return PS[:, 6 + (13 * half + k) % 2, :]
                        e = i * 4 + 2 * half + 2
                        a1, a2, a3 = select(None, None, 1 - half, rank[:, bass.ds(e, 2), :], gate[:, bass.ds(e, 2), :],
                                            ident3[:, bass.ds(e, 2)])
                        lstep(run(a1)), lstep(run(a2))
                        dve.wait_ge(chunk_used, i * TURN + half * CPP + CPM)
                        lmark(v.tensor_scalar(gbuf, PS[:, 0:2, :].rearrange("p b f -> p (b f)"), LIMIT, None, ALU.min),
                              g_act, pair + 2)
                        lmark(run(a3), pair_sel, pair + 2)
                        dve.wait_ge(chunk_used, i * TURN + half * CPP + 2 * CPM)
                        lmark(v.tensor_scalar(ubuf, PS[:, 2:4, :].rearrange("p b f -> p (b f)"), LIMIT, -LIMIT,
                                              ALU.min, ALU.max), up_act, pair + 2)
                        lstep(v.scalar_tensor_tensor(out=ubuf, in0=ubuf, scalar=1.0, in1=gbuf, op0=ALU.add, op1=ALU.mult))
                        dve.wait_ge(sig_act, pair + 1)
                        lmark(v.tensor_tensor(ubuf, ubuf, sbuf_, ALU.mult), hid_act, pair + 1)
                        for t, (t0, n) in enumerate(TILES):
                            for hf in range(2):
                                k = 2 + 2 * t + hf
                                xs = x3[0:n, t, hf * 512:(hf + 1) * 512]
                                aux(k, v.tensor_tensor, xs, auxbank(k)[0:n, :], xs, ALU.add)
                        aux(11, v.tensor_tensor, *scaled_turn(auxbank(11), 0))
                        aux(12, v.tensor_tensor, *scaled_turn(auxbank(12), 4))
                        while cnt_[0] < VPP:
                            lstep(v.memset(small[:, 159:160], 0.0))

            def add_y(r_):
                for t, (t0, n) in enumerate(TILES):
                    for hf in range(2):
                        nm = f"sc{r_}{t}{hf}"
                        is_filled(dve, nm)
                        xs = x3[0:n, t, hf * 512:(hf + 1) * 512]
                        drain(v.tensor_tensor(xs, bank(nm)[0:n, :], xs, ALU.add), nm)
                    if r_:
                        mark(v.memset(small[:, 159:160], 0.0), f"moe{t}")

            turns(0, MID, bases[0])
            add_y(0)
            n_ov = dve.value_load(ov_n[0:1, 0:1], min_val=0, max_val=OV_MAX)
            with dve.Fori(0, OV_GROUPS) as grp:
                with dve.If(grp * OV_PER < n_ov):
                    with dve.Fori(0, OV_PER) as jj:
                        j = grp * OV_PER + jj
                        with dve.If(j < n_ov):
                            e = dve.value_load(ov_e[0:1, bass.ds(j, 1)], min_val=0, max_val=E - 1)
                            oc = [0]

                            def ostep(ins):
                                oc[0] += 1
                                ins.then_inc(v_ov, 1)
                                dve.wait_ge(v_ov, j * 5 + oc[0])

                            def omark(ins, s):
                                ins.then_inc(s, 1)
                                dve.wait_ge(s, j + 1)

                            def ovaux(k, op, *args):
                                b, m = k % 2, k // 2
                                dve.wait_ge(ov_filled[b], 1 + m + j * 7)
                                op(*args).then_inc(ov_drained[b], 1)
                                dve.wait_ge(ov_drained[b], 2 + m + j * 7)
                            rel = small[:, 156:159]
                            ostep(v.tensor_scalar(rel, rank[:, bass.ds(e, 1), :].rearrange("p a t -> p (a t)"),
                                                  ov_off[:, bass.ds(j, 1)], None, ALU.subtract))
                            ostep(v.tensor_tensor(Ssel, iotaf[:, :].unsqueeze(1).broadcast_to([P, NT, P]),
                                                  rel.unsqueeze(2).broadcast_to([P, NT, P]), ALU.is_equal))
                            ostep(v.tensor_tensor(Sgat, Ssel, gate[:, bass.ds(e, 1), :].rearrange("p a t -> p (a t)")
                                                  .unsqueeze(2).broadcast_to([P, NT, P]), ALU.mult))
                            omark(v.tensor_copy(ind[:, 0, :], ident3[:, bass.ds(e, 1)].broadcast_to([3 * E, P])), ov_sel)
                            ovaux(2, v.tensor_tensor, *scaled_turn(PS[:, 6, :], 0))
                            ovaux(3, v.tensor_tensor, *scaled_turn(PS[:, 7, :], 4))
                            dve.wait_ge(ov_used, j * OV_CHUNKS + OV_CHUNKS + 2)
                            omark(v.tensor_scalar(gbuf, PS[:, 0:2, :].rearrange("p b f -> p (b f)"), LIMIT, None, ALU.min), ovg_act)
                            dve.wait_ge(ov_used, j * OV_CHUNKS + OV_CHUNKS + 4)
                            ostep(v.tensor_scalar(ubuf, PS[:, 2:4, :].rearrange("p b f -> p (b f)"), LIMIT, -LIMIT,
                                                  ALU.min, ALU.max))
                            ostep(v.scalar_tensor_tensor(out=ubuf, in0=ubuf, scalar=1.0, in1=gbuf, op0=ALU.add, op1=ALU.mult))
                            assert oc[0] == 5
                            dve.wait_ge(ovs_act, j + 1)
                            omark(v.tensor_tensor(ubuf, ubuf, sbuf_, ALU.mult), ovh_act)
                            for t, (t0, n) in enumerate(TILES):
                                for hf in range(2):
                                    k = 8 + t * 2 + hf
                                    xs = x3[0:n, t, hf * 512:(hf + 1) * 512]
                                    ovaux(k, v.tensor_tensor, xs, PS[0:n, 6 + k % 2, :], xs, ALU.add)
                            v.memset(small[:, 155:156], 0.0)
            first_pair(1)
            turns(MID, TURNS, bases[1])
            add_y(1)
            for t, (t0, n) in enumerate(TILES):
                dve.wait_ge(a_mark, AM[f"ss3{t}"])
                rsqrt_of(rstd[0:n, t:t + 1], ss[0:n, t:t + 1], 1.0 / D_MODEL)
                mark(v.tensor_scalar(h3[0:n, t, :], x3[0:n, t, :], rstd[0:n, t:t + 1], None, ALU.mult), f"h3{t}")
            evac_hT("tT", "ln_ple")
            for t, (t0, n) in enumerate(TILES):
                for hf in range(2):
                    cs = slice(hf * 512, (hf + 1) * 512)
                    is_drained(dve, f"pp{t}{hf}")
                    is_drained(dve, f"pg{t}{hf}")
                    step(v.tensor_tensor(sg3[0:n, t, cs], ppb[0:n, t, cs], sg3[0:n, t, cs], ALU.mult))
                    ins = v.tensor_tensor(x3[0:n, t, cs], x3[0:n, t, cs], sg3[0:n, t, cs], ALU.add)
                    mark(ins, f"y{t}") if hf else step(ins)
            dve.wait_ge(fnb_in, 16)
            dve.wait_ge(a_mark, AM[f"ss4{NT - 1}"])
            rsqrt_of(rstd[:, :], ss[:, :], 1.0 / D_MODEL)
            for t, (t0, n) in enumerate(TILES):
                mark(v.scalar_tensor_tensor(out=h3[0:n, t, :], in0=x3[0:n, t, :], scalar=rstd[0:n, t:t + 1],
                                            in1=fnb[0:n, :], op0=ALU.mult, op1=ALU.mult), f"yout{t}")


_INS = ['x_prompt', 'x_sample', 'state_pool', 'state_conv', 'state_ssm', 'p_prompt', 'p_sample', 'ln_mix', 'w_in',
        'pool_w', 'pool_scale', 'conv_w', 'a_log', 'dt_bias', 'dn_norm', 'w_out', 'ln_moe', 'router_w', 'router_b',
        'w_gate', 'b_gate', 'w_up', 'b_up', 'w_down', 'b_down', 'ln_ple', 'w_ple_gate', 'w_ple', 'final_norm']
_OUTS = [(1, SEQ, D_MODEL), (DB, DS, D_MODEL), (1, 1, PH, POOL_W), (1, 1, CH, QKV_T * P), (1, 1, HEADS, P, P),
         (1, DB, PH, POOL_W), (1, DB, CH, QKV_T * P), (1, DB, HEADS, P, P)]


def kernel(**inputs):
    import numpy as _np
    import concourse.bacc as _bacc
    from concourse import mybir as _mybir
    from concourse.bass_utils import run_bass_kernel_spmd as _run

    nc = _bacc.Bacc("TRN2", target_bir_lowering=False, num_devices=1)
    arrays, d = {}, {}
    for name in _INS:
        a = _np.ascontiguousarray(inputs[name])
        arrays[f"in_{name}"] = a
        d[name] = nc.dram_tensor(f"in_{name}", a.shape, _mybir.dt.from_np(a.dtype), kind="ExternalInput").ap()
    o = [nc.dram_tensor(f"out_{i}", shape, _mybir.dt.float32, kind="ExternalOutput").ap()
         for i, shape in enumerate(_OUTS)]
    trunk_kernel(nc, d, o)
    r = _run(nc, [arrays], core_ids=[0])
    return tuple(r.results[0][f"out_{i}"] for i in range(len(_OUTS)))
```

```python
from contextlib import ExitStack

import concourse.bass as bass
from concourse import mybir

F32 = mybir.dt.float32
I32 = mybir.dt.int32
BF16 = mybir.dt.bfloat16
ALU = mybir.AluOpType
ACT = mybir.ActivationFunctionType
AX_X = mybir.AxisListType.X

P = 128
D_MODEL = 1024
KT = D_MODEL // P
SEQ = 256
DB, DS = 8, 8
NSAMP = DB * DS
T = SEQ + NSAMP
TILES = [(0, P), (P, P), (SEQ, NSAMP)]
NT = len(TILES)
POOL_W = 512
WINDOWS = (2, 4, 8, 16)
PG = len(WINDOWS)
PH = max(WINDOWS) - 1
HEADS = 4
CONV = 4
CH = CONV - 1
QKV_T = 3 * HEADS
IN_W = POOL_W + 4 * HEADS * P + 2 * HEADS
NB_IN = 5
E = 32
TOPK = 4
FF = 1024
LIMIT = 7.0
ALPHA = 1.702
PLE = 256
EPS = 1e-6
CAP = 64
PAIRS = E // 2
TURNS = PAIRS // 2
MID = TURNS // 2
EPAD = E + 2
RING = 8
SLOT = 4096
CPM = 4
CPP = 3 * CPM
NCH = PAIRS * CPP
TURN = 2 * CPP
UEW = (PH + SEQ) + DB * (PH + DS)
QEW = (CH + SEQ) + DB * (CH + DS)
LEVELS = 7
OV_MAX = (T * TOPK - 1) // CAP
OV_FIRST = 2
OV_OFF = [CAP, CAP + P]
OV_CHUNKS = 6
OV_USES = 10

IN_ORDER = [2, 1, 3, 0, 4]
VU = [12, 13, 14, 15, 0, 1, 2, 3]
NORMED = [4, 5, 6, 7, 0, 1, 2, 3]
ORDER = [0, 2, 1]


def chain(eng, own):
    counts = {}

    def step(ins, s=None, value=None):
        s = own if s is None else s
        counts[s.name] = counts.get(s.name, 0) + 1
        ins.then_inc(s, 1)
        eng.wait_ge(s, counts[s.name] if value is None else value)
    return step


def trunk_kernel(nc, d, o):
    with ExitStack() as ctx:
        def sb(name, shape, dt=F32):
            return ctx.enter_context(nc.sbuf_tensor(name, shape, dt))

        def sem(name):
            return ctx.enter_context(nc.semaphore(name))

        ring = sb("ring", [P, RING, SLOT])
        X = sb("x_resid", [P, NT * D_MODEL])
        H = sb("h_region", [P, QKV_T * T])
        HT = sb("ht_region", [P, KT * T])
        Q = sb("q_region", [P, QKV_T * QEW])
        U = sb("u_region", [P, PG * UEW])
        Z = sb("z_region", [P, 2 * D_MODEL])
        ident = sb("ident", [P, P])
        ones = sb("ones", [P, P])
        causal = sb("causal", [P, P])
        strict = sb("strict", [P, P])
        seg = sb("seg", [NSAMP, NSAMP])
        segcausal = sb("segcausal", [NSAMP, NSAMP])
        ident3 = sb("ident3", [3 * E, EPAD])
        lmask = sb("lmask", [P, LEVELS, P])
        iotaf = sb("iotaf", [P, P])
        vecs = sb("vecs", [P, 77])
        wrout = sb("wrout", [P, KT, E])
        small = sb("small", [P, 160])
        rank = sb("rank", [P, EPAD, NT])
        gate = sb("gate", [P, EPAD, NT])
        ov_off = sb("ov_off", [P, OV_MAX])
        ov_e = sb("ov_e", [P, OV_MAX], I32)
        ov_n = sb("ov_n", [P, 1], I32)

        ptmp = sb("ptmp", [P, UEW])
        iti = ptmp[:, 0:P].bitcast(I32)

        PS = ctx.enter_context(nc.psum_tensor("ps", [P, 8, 512], F32))

        x3 = X[:, :].rearrange("p (t d) -> p t d", t=NT)
        h3 = H[:, 0:NT * D_MODEL].rearrange("p (t d) -> p t d", t=NT)
        ct = H[:, :].rearrange("p (c t) -> p c t", c=QKV_T)
        hT = HT[:, :].rearrange("p (k t) -> p k t", k=KT)
        qe = Q[:, :].rearrange("p (c t) -> p c t", c=QKV_T)
        ue = U[:, :].rearrange("p (c t) -> p c t", c=PG)
        zT = Z[:, 0:PG * T].rearrange("p (c t) -> p c t", c=PG)
        ptmp2 = Z[:, PG * T:PG * T + UEW]
        wtail = Z[:, 1736:1800].rearrange("p (k c) -> p k c", k=KT)
        VEC = {"ln_mix": 0, "ln_moe": 8, "ln_ple": 16, "pool_scale": 24, "dn_norm": 28, "conv_w": 29}

        def vec(name, i=0, n=1):
            return vecs[:, VEC[name] + i:VEC[name] + i + n]

        def sm(at, *shape):
            n = 1
            for s in shape:
                n *= s
            v = small[:, at:at + n]
            return v.rearrange("p (a b) -> p a b", a=shape[0]) if len(shape) == 2 else v
        ss = sm(0, NT)
        rstd = sm(3, NT)
        beta = sm(6, NT, HEADS)
        gl = sm(18, NT, HEADS)
        gc = sm(30, NT, HEADS)
        egc = sm(42, NT, HEADS)
        kdec = sm(54, NT, HEADS)
        egl = sm(66, NT, HEADS)
        egs = sm(78, HEADS, DB)
        alog = sm(110, HEADS)
        dtb = sm(114, HEADS)
        inv16 = sm(118, 16)
        rb = small[0:E, 134:135]
        tmp12 = sm(136, NT, HEADS)
        oss = sm(150, 4)

        sqb = [X[:, 0:T], X[:, T:2 * T]]
        rnb = [X[:, o_:o_ + T] for o_ in (640, 2304, 2624)]
        poolw = X[:, 1024:1536].rearrange("p (g d) -> p g d", g=PG)
        clast = X[:, 1536:1536 + QKV_T * DB * CH].rearrange("p (c r) -> p c r", c=QKV_T)
        ulast = X[:, 2048:2048 + PG * NSAMP].rearrange("p (c r) -> p c r", c=PG)
        convord = {c: i for i, c in enumerate([4, 5, 6, 7, 0, 1, 2, 3, 8, 9, 10, 11])}

        def prompt_cols(v, c, hist):
            return v[:, c, hist:hist + SEQ]

        def sample_cols(v, c, hist, lo=None, n=DS):
            lo = hist if lo is None else lo
            base = hist + SEQ
            return v[:, c, base:base + DB * (hist + DS)].rearrange("p (b w) -> p b w", b=DB)[:, :, lo:lo + n]

        def quads(region, n):
            return [region[0:n, i * HEADS * n:(i + 1) * HEADS * n].rearrange("p (h t) -> p h t", h=HEADS)
                    for i in range(6)]
        scratch = [quads(X[:, :], P), quads(ring[:, 4, :], P), quads(U[:, :], NSAMP)]
        kN = Q[:, 0:1536].rearrange("p (t h d) -> p t h d", t=NT, h=HEADS)
        vN = Q[:, 1536:3072].rearrange("p (t h d) -> p t h d", t=NT, h=HEADS)
        S1 = Q[:, 3072:3584].rearrange("p (h d) -> p h d", h=HEADS)
        kqS = Q[:, 3584:4096].rearrange("p (h t) -> p h t", h=HEADS)
        oN = [scratch[0][5], scratch[1][5],
              ring[0:NSAMP, 4, 3072:3584].rearrange("p (h d) -> p h d", h=HEADS)]
        qS2 = ring[0:NSAMP, 4, 3584:4096].rearrange("p (h d) -> p h d", h=HEADS)
        vmask = U[0:NSAMP, 0:1024].rearrange("p (b d) -> p b d", b=DB)
        s0 = ring[:, 7, :].rearrange("p (b h e) -> p b h e", b=DB, h=HEADS)
        tilepart = [(causal, ones, 0, P), (causal, ones, P, P), (segcausal, seg, SEQ, NSAMP)]

        st_conv = ring[0:DB * CH, 7, 0:QKV_T * P]
        st_pool = ring[0:DB * PH, 7, 1536:2048]
        vrows = ring[0:77, 7, 2048:2176]
        outrow = ring[:, 6, :]

        xg = HT[:, 0:1024]
        xgT = HT[:, 1024:2048].rearrange("p (k s) -> p k s", k=KT)
        ind = HT[0:3 * E, 2048:2176].bitcast(BF16).rearrange("p (b s) -> p b s", b=2)
        gbuf, ubuf, sbuf_, hidf = (Q[:, i * 1024:(i + 1) * 1024] for i in range(4))
        hidT = hidf.rearrange("p (k s) -> p k s", k=KT)
        ybuf = U[:, 0:1024]
        Ssel = U[:, 1024:1408].rearrange("p (t s) -> p t s", t=NT)
        Sgat = U[:, 1408:1792].rearrange("p (t s) -> p t s", t=NT)
        SgT = [H[:, 3072 + 384 * b:3456 + 384 * b].rearrange("p (t s) -> p t s", t=NT) for b in range(2)]
        bias3 = Z[0:3 * E, 0:1536].bitcast(BF16)
        biases = [bias3[:, m * FF:(m + 1) * FF] for m in range(3)]
        bias_f = ring[0:3 * E, 4, 0:3072]

        def rt(i):
            return Q[:, T + i * 96:T + 96 + i * 96].rearrange("p (t e) -> p t e", t=NT)
        logT = Q[0:E, 0:T]
        Lg, gtm, eqm, cum, sel, exq = (rt(i) for i in range(6))
        m8 = Q[:, 1700:1724].rearrange("p (t e) -> p t e", t=NT)
        ngt = Q[:, 1724:1727]
        den = Q[:, 1727:1730]
        cnt = Q[:, 1730:1762]
        flg = Q[:, 1762:1826].rearrange("p (e b) -> p e b", b=2)
        pos = Q[:, 1826:1890]
        evec = Q[:, 1890:1954].rearrange("p (e b) -> p e b", b=2)
        ovec = Q[:, 1954:2018].rearrange("p (e b) -> p e b", b=2)
        ove_f = Q[:, 2018:2018 + OV_MAX]
        cmp_ = Q[:, 2048:2048 + OV_MAX * 64].rearrange("p (j x) -> p j x", j=OV_MAX)

        wple = ring[:, 0, 0:2048].rearrange("p (k f) -> p k f", k=2)
        pin = ring[:, 1, 0:768].rearrange("p (t f) -> p t f", t=NT)
        pT = ring[:, 1, 1024:1024 + 2 * T].rearrange("p (k t) -> p k t", k=2)
        wpg = ring[:, 2:4, :].rearrange("p s (k f) -> p (s k) f", k=4)
        ppb = ring[:, 4, 0:3072].rearrange("p (t f) -> p t f", t=NT)
        sg3 = Q[:, 0:3072].rearrange("p (t f) -> p t f", t=NT)
        fnb = ring[:, 1, 2048:3072]

        vecs_in = sem("vecs_in")
        x_in = [sem(f"x_in{t}") for t in range(NT)]
        win_in = [sem(f"win_in{b}") for b in range(NB_IN)]
        wtail_in = sem("wtail_in")
        smalls_in = sem("smalls_in")
        hist_in = sem("hist_in")
        wout_in = sem("wout_in")
        s0_in = sem("s0_in")
        xagain_in = [sem(f"xagain_in{t}") for t in range(NT)]
        bias_in = sem("bias_in")
        chunk_in = [sem(f"chunk_in{c}") for c in range(TURN)]
        ovch_in = [sem(f"ovch_in{c}") for c in range(OV_CHUNKS)]
        wpg_in = sem("wpg_in")
        tail_in = sem("tail_in")
        fnb_in = sem("fnb_in")
        out_done = sem("out_done")
        chunk_used = sem("chunk_used")
        ov_used = sem("ov_used")
        ov_filled = [sem(f"ov_filled{b}") for b in range(2)]
        ov_drained = [sem(f"ov_drained{b}") for b in range(2)]
        win_used = sem("win_used")
        filled = [sem(f"filled{b}") for b in range(8)]
        drained = [sem(f"drained{b}") for b in range(8)]
        consts = sem("consts")
        h_ready = sem("h_ready")
        ext_zero = sem("ext_zero")
        acc_ready = sem("acc_ready")
        ct_ready = sem("ct_ready")
        sq_ready = sem("sq_ready")
        norm_ready = sem("norm_ready")
        d_ready = sem("d_ready")
        v_step = sem("v_step")
        a_step = sem("a_step")
        g_step = sem("g_step")
        v_mark = sem("v_mark")
        a_mark = sem("a_mark")
        VM = {n: i + 1 for i, n in enumerate(
            ["ba", "sp_in", "g", "gcs"] + [f"diff{t}" for t in range(NT)] + [f"U{t}" for t in range(NT)]
            + ["kd", "rs0", "rs2", "rs1", "S2", "x20", "h20", "x22", "h22", "split", "x21", "h21", "m8", "sel",
               "gates", "S0", "ybuf_zero", "table"]
            + [f"moe{t}" for t in range(NT)] + [f"h3{t}" for t in range(NT)]
            + [f"y{w}{t}" for t in range(NT) for w in ("", "out")])}
        AM = {n: i + 1 for i, n in enumerate(
            ["ss", "exps", "ea", "lg", "gexp"] + [f"E{t}" for t in range(NT)]
            + [f"ss2{t}" for t in ORDER] + ["exq"] + [f"ss3{t}" for t in range(NT)] + [f"ss4{t}" for t in range(NT)])}
        g_ready = sem("g_ready")
        small_zero = sem("small_zero")
        inv_ready = sem("inv_ready")
        root_ready = sem("root_ready")
        acc_pool = sem("acc_pool")
        vmasked = sem("vmasked")
        packed = sem("packed")
        poolw_in = sem("poolw_in")
        pool_stored = sem("pool_stored")
        ssm_stored = sem("ssm_stored")
        hist_stored = sem("hist_stored")
        s0_stored = sem("s0_stored")
        v_loop = sem("v_loop")
        v_ov = sem("v_ov")
        pair_sel = sem("pair_sel")
        g_act = sem("g_act")
        sig_act = sem("sig_act")
        up_act = sem("up_act")
        y_act = sem("y_act")
        ovy_act = sem("ovy_act")
        hid_act = sem("hid_act")
        ov_sel = sem("ov_sel")
        ov_next = sem("ov_next")
        ovg_act = sem("ovg_act")
        ovs_act = sem("ovs_act")
        ovh_act = sem("ovh_act")

        uses, fills = {}, [0] * 8

        def use(name, bank):
            uses[name] = (bank, fills[bank])
            fills[bank] += 1

        rr = [0]

        def nxt(name, banks=range(8)):
            banks = list(banks)
            use(name, banks[rr[0] % len(banks)])
            rr[0] += 1

        for n in ["vec", "sc", "sp"] + [f"hT{t}{hf}" for t in range(NT) for hf in range(2)] + ["ba"]:
            nxt(n)
        for b in IN_ORDER[:2]:
            for c in range(4):
                nxt(f"pr{4 * b + c}")
        nxt("gcs")
        nxt("egs")
        for i in range(8):
            nxt(f"pr{VU[i]}")
            nxt(f"ss{i}")
        for n in ["pr16", "npp", "nps", "pr17", "pr18", "pr19", "cnp0", "cnp1", "cnp2", "cns0", "cns1", "cns2"]:
            nxt(n)
        for g in range(PG):
            nxt(f"pm{g}")
        for t in range(NT):
            nxt(f"G{t}")
            nxt(f"kk{t}")
            nxt(f"qk{t}")
        for n in ["kqs", "T0", "kN0", "kN1", "kN2", "T1", "vN0", "vN1", "vN2", "T2"]:
            nxt(n)
        for s in range(1, LEVELS):
            ts = [t for t in range(NT) if t < 2 or s < 3]
            for t in ts:
                nxt(f"P{s}{t}")
            for t in ts:
                if s < LEVELS - 1 and (t < 2 or s < 2):
                    nxt(f"Q{s}{t}")
                nxt(f"QT{s}{t}")
            if s == 2:
                nxt("R2k")
                nxt("R2q")
        for n in ["v0", "v2", "S1", "o0", "kS1", "o2", "qS1", "v1", "oT0", "o1", "oT2", "S2",
                  "op00", "op01", "oT1", "op20", "op21", "op10", "rT00", "rT01", "rT20", "rT21", "op11",
                  "ns0a", "ns0b", "ns1a", "ns1b", "rT10", "rT11"]:
            nxt(n)
        for n in ["lg", "lgT", "ns2a", "ns2b", "rk", "ns3a", "ns3b"]:
            nxt(n)
        for n, b in (("ga", 6), ("gb", 7), ("xta", 6), ("xtb", 7), ("sgt", 6)):
            use(n, b)
        base = list(fills)
        for b in (6, 7):
            fills[b] += 13 * TURNS
        for t in range(NT):
            for hf in range(2):
                use(f"sc{t}{hf}", 6 + hf)
        use("pT0", 0), use("pT1", 1)
        for n in ([f"pp{t}{hf}" for t in range(NT) for hf in range(2)]
                  + [f"tT{t}{hf}" for t in range(NT) for hf in range(2)]
                  + [f"pg{t}{hf}" for t in range(NT) for hf in range(2)]):
            nxt(n)

        def bank(name):
            return PS[:, uses[name][0], :]

        def product_of(prefix, t, hf):
            n = TILES[t][1]
            p0 = hf * n if n < P else 0
            return bank(f"{prefix}{t}{hf}")[p0:p0 + n, :]

        def can_fill(eng, name):
            b, k = uses[name]
            if k:
                eng.wait_ge(drained[b], k)

        def is_filled(eng, name):
            b, k = uses[name]
            eng.wait_ge(filled[b], k + 1)

        def is_drained(eng, name):
            b, k = uses[name]
            eng.wait_ge(drained[b], k + 1)

        def fsem(name):
            return filled[uses[name][0]]

        def dsem(name):
            return drained[uses[name][0]]

        chunk_src = {"g": d["w_gate"][0], "u": d["w_up"][0], "d": d["w_down"][0]}

        def load_chunk(eng, c, e, s):
            cc = c % CPP
            r = (cc % CPM) * 2 * P
            for a_ in range(2):
                w = chunk_src["gud"[cc // CPM]][bass.ds(e + a_, 1)]
                eng.dma_start(slot(c)[:, a_], w[:, r:r + 2 * P, :].rearrange("a (k p) f -> p (a k) f", p=P)
                              ).then_inc(s, 16)

        def slot(c):
            return ring[:, c % RING, :].rearrange("p (a k f) -> p a k f", a=2, k=2)

        def ov_chunk(e, c):
            w = chunk_src["gud"[c // 2]][bass.ds(e, 1)]
            r = (c % 2) * 4 * P
            return w[:, r:r + 4 * P, :].rearrange("a (k p) f -> p (a k) f", p=P)

        block = ctx.enter_context(nc.Block())

        @block.sync
        def _(sp):
            for t, (t0, n) in enumerate(TILES):
                src = d["x_prompt"][0, t0:t0 + n] if t < 2 else d["x_sample"].rearrange("b s d -> (b s) d")
                sp.dma_start(x3[0:n, t, :], src).then_inc(x_in[t], 16)
            r = 0
            for n in ("ln_mix", "ln_moe", "ln_ple", "pool_scale", "dn_norm"):
                k = d[n].shape[1] // P
                sp.dma_start(vrows[r:r + k, :], d[n][0].rearrange("(k p) -> k p", p=P)).then_inc(vecs_in, 16)
                r += k
            sp.dma_start(vrows[r:r + CONV * QKV_T, :],
                         d["conv_w"][0].rearrange("j (c p) -> (j c) p", p=P)).then_inc(vecs_in, 16)
            sp.dma_start(st_conv, d["state_conv"][0].rearrange("b r c -> (b r) c")).then_inc(hist_in, 16)
            sp.dma_start(st_pool, d["state_pool"][0].rearrange("b r c -> (b r) c")).then_inc(hist_in, 16)
            sp.wait_ge(small_zero, 1)
            sp.dma_start(alog, d["a_log"][0:1, :].broadcast_to([P, HEADS])).then_inc(smalls_in, 16)
            sp.dma_start(dtb, d["dt_bias"][0:1, :].broadcast_to([P, HEADS])).then_inc(smalls_in, 16)
            sp.dma_start(rb, d["router_b"][0].rearrange("(e a) -> e a", a=1)).then_inc(smalls_in, 16)
            sp.dma_start(wtail[:, :, :], d["w_in"][0, :, NB_IN * 512:IN_W].rearrange("(k p) c -> p k c", p=P)
                         ).then_inc(wtail_in, 16)
            for i, b in enumerate(IN_ORDER):
                sp.dma_start(ring[:, i, :].rearrange("p (k c) -> p k c", k=KT),
                             d["w_in"][0, :, b * 512:(b + 1) * 512].rearrange("(k p) c -> p k c", p=P)
                             ).then_inc(win_in[i], 16)
            sp.dma_start(wrout[:, :, :], d["router_w"][0].rearrange("(k p) e -> p k e", p=P)).then_inc(smalls_in, 16)
            sp.wait_ge(h_ready, NT)
            sp.dma_start(poolw, d["pool_w"][0].rearrange("g c e -> c g e")).then_inc(poolw_in, 16)
            is_drained(sp, "vec"), is_drained(sp, "sc"), is_drained(sp, "sp")
            sp.dma_start(s0, d["state_ssm"][0].rearrange("b h d e -> d b h e")).then_inc(s0_in, 16)
            sp.dma_start(ring[:, 5, :].rearrange("p (k f) -> p k f", k=4),
                         d["w_out"][0, 0:512].rearrange("(k p) f -> p k f", p=P)).then_inc(wout_in, 16)
            for c in range(4):
                sp.wait_ge(win_used, c + 1)
                load_chunk(sp, c, 0, chunk_in[c])
            sp.wait_ge(hist_stored, 16 * 4)
            sp.dma_start(ring[:, 6, :].rearrange("p (k f) -> p k f", k=4),
                         d["w_out"][0, 512:1024].rearrange("(k p) f -> p k f", p=P)).then_inc(wout_in, 16)
            is_drained(sp, "oT0")
            for t in ORDER:
                t0, n = TILES[t]
                src = d["x_prompt"][0, t0:t0 + n] if t < 2 else d["x_sample"].rearrange("b s d -> (b s) d")
                sp.dma_start(x3[0:n, t, :], src).then_inc(xagain_in[t], 16)
            is_drained(sp, "oT2"), is_drained(sp, "oT1")
            for m, n in enumerate(("b_gate", "b_up", "b_down")):
                for part in range(3):
                    sp.dma_start(bias_f[part * E:(part + 1) * E, m * FF:(m + 1) * FF], d[n][0]).then_inc(bias_in, 16)
            sp.wait_ge(v_mark, VM["split"])
            load_chunk(sp, 4, 0, chunk_in[4])
            for c in range(5, 8):
                if c < 7:
                    is_filled(sp, "op11")
                else:
                    sp.wait_ge(s0_stored, 16)
                load_chunk(sp, c, 0, chunk_in[c])
            def turn_loads(lo, hi):
                with sp.Fori(lo, hi - 1) as i:
                    for c in range(TURN):
                        cc = (c + RING) % TURN
                        e = i * 4 + 4 * ((c + RING) // TURN) + 2 * (cc // CPP)
                        sp.wait_ge(chunk_used, i * TURN + c + 1)
                        load_chunk(sp, cc, e, chunk_in[cc])
                for c in range(TURN - RING):
                    cc = c + RING
                    sp.wait_ge(chunk_used, (hi - 1) * TURN + c + 1)
                    load_chunk(sp, cc, 4 * (hi - 1) + 2 * (cc // CPP), chunk_in[cc])
            turn_loads(0, MID)
            sp.nop().then_inc(ov_used, OV_CHUNKS)
            sp.wait_ge(v_mark, VM["table"])
            n_ov = sp.value_load(ov_n[0:1, 0:1], min_val=0, max_val=OV_MAX)

            def overflow_block(j):
                e = sp.value_load(ov_e[0:1, bass.ds(j, 1)], min_val=0, max_val=E - 1)
                for c in range(OV_CHUNKS):
                    sp.wait_ge(chunk_used, MID * TURN - RING + c + 1)
                    sp.wait_ge(ov_used, j * OV_CHUNKS + c + 1)
                    sp.dma_start(ring[:, c, :].rearrange("p (k f) -> p k f", k=4), ov_chunk(e, c)
                                 ).then_inc(ovch_in[c], 16)

            with sp.Fori(0, OV_FIRST) as j:
                with sp.If(j < n_ov):
                    overflow_block(j)
            with sp.If(n_ov > OV_FIRST):
                with sp.Fori(OV_FIRST, OV_MAX) as j:
                    with sp.If(j < n_ov):
                        overflow_block(j)
            for c in [6, 7] + list(range(OV_CHUNKS)):
                sp.wait_ge(chunk_used, MID * TURN - RING + c + 1)
                if c < OV_CHUNKS:
                    sp.wait_ge(ov_used, n_ov * OV_CHUNKS + (c + 1))
                load_chunk(sp, c, 4 * MID, chunk_in[c])
            turn_loads(MID, TURNS)
            sp.wait_ge(chunk_used, NCH - CPM)
            for t, (t0, n) in enumerate(TILES):
                src = d["p_prompt"][0, 0, t0:t0 + n] if t < 2 else d["p_sample"][0].rearrange("b s d -> (b s) d")
                sp.dma_start(pin[0:n, t, :], src).then_inc(tail_in, 16)
            sp.dma_start(wple, d["w_ple"][0].rearrange("(k p) f -> p k f", p=P)).then_inc(tail_in, 16)
            sp.dma_start(wpg, d["w_ple_gate"][0].rearrange("(k p) f -> p k f", p=P)).then_inc(wpg_in, 16)
            sp.dma_start(fnb, d["final_norm"].rearrange("(a f) -> a f", a=1).broadcast_to([P, D_MODEL])
                         ).then_inc(fnb_in, 16)
            for t, (t0, n) in enumerate(TILES):
                sp.wait_ge(v_mark, VM[f"yout{t}"])
                dst = o[0][0, t0:t0 + n] if t < 2 else o[1].rearrange("b s d -> (b s) d")
                sp.dma_start(dst, h3[0:n, t, :]).then_inc(out_done, 16)
            sp.wait_ge(out_done, 16 * NT)
            sp.wait_ge(pool_stored, 16)
            sp.wait_ge(ssm_stored, 16)

        @block.gpsimd
        def _(pool):
            step = chain(pool, g_step)
            g = nc.gpsimd
            step(g.memset(ident[:, :], 0.0))
            step(g.affine_select(out=ident[:, :], in_=ident[:, :], compare_op=ALU.not_equal, fill=1.0, base=0,
                                 pattern=[[-1, P]], channel_multiplier=1), consts)
            for c in range(PG):
                g.memset(ue[:, c, 0:PH], 0.0).then_inc(ext_zero, 1)
            for c in range(QKV_T):
                g.memset(qe[:, c, 0:CH], 0.0).then_inc(ext_zero, 1)
            step(g.memset(ones[:, :], 1.0), consts)
            step(g.iota(iti[:, :], pattern=[[1, P]], base=0, channel_multiplier=0))
            step(g.tensor_copy(iotaf[:, :], iti[:, :]))
            for m, b in ((causal, 0), (strict, -1)):
                step(g.memset(m[:, :], 1.0))
                step(g.affine_select(out=m[:, :], in_=m[:, :], compare_op=ALU.is_ge, fill=0.0, base=b,
                                     pattern=[[1, P]], channel_multiplier=-1))
            step(g.memset(seg[:, :], 1.0))
            sv = seg[:, :].rearrange("p (b s) -> p b s", b=DB)
            step(g.affine_select(out=sv, in_=sv, compare_op=ALU.is_ge, fill=0.0, base=0,
                                 pattern=[[-DS, DB], [0, DS]], channel_multiplier=1))
            step(g.affine_select(out=sv, in_=sv, compare_op=ALU.is_ge, fill=0.0, base=DS - 1,
                                 pattern=[[DS, DB], [0, DS]], channel_multiplier=-1))
            step(g.tensor_tensor(segcausal[:, :], causal[0:NSAMP, 0:NSAMP], seg[:, :], ALU.mult))
            step(g.memset(lmask[:, :, :], 0.0))
            v0 = lmask[:, 0, :].rearrange("p (b h s) -> p b h s", h=2, s=1)[:, :, 1, :]
            step(g.affine_select(out=v0, in_=v0, compare_op=ALU.not_equal, fill=1.0, base=0,
                                 pattern=[[-2, P // 2], [0, 1]], channel_multiplier=1))
            for s in range(1, LEVELS):
                z = 1 << s
                nb = P // (2 * z)
                vs = lmask[:, s, :].rearrange("p (b h s) -> p b h s", h=2, s=z)[:, :, 0, :]
                step(g.memset(vs, 1.0))
                step(g.affine_select(out=vs, in_=vs, compare_op=ALU.is_ge, fill=0.0, base=-z,
                                     pattern=[[-2 * z, nb], [0, z]], channel_multiplier=1))
                step(g.affine_select(out=vs, in_=vs, compare_op=ALU.is_ge, fill=0.0, base=2 * z - 1,
                                     pattern=[[2 * z, nb], [0, z]], channel_multiplier=-1))
            for part in range(3):
                rows = slice(part * E, (part + 1) * E)
                step(g.tensor_copy(ident3[rows, :], ident[rows, part * E:part * E + EPAD]))
            step(g.memset(rank[:, E:EPAD, :], -1.0))
            step(g.memset(gate[:, E:EPAD, :], 0.0), consts)
            pool.wait_ge(h_ready, NT)
            is_drained(pool, "sc")
            for c in [4, 5, 6, 7, 0, 1, 2, 3, 8, 9, 10, 11]:
                is_drained(pool, f"pr{c + 4}")
                step(g.tensor_copy(clast[:, c, :].rearrange("p (b r) -> p b r", b=DB),
                                   sample_cols(qe, c, CH, DS, CH)), packed)
            is_drained(pool, "sp")
            for c in range(PG):
                is_drained(pool, f"pr{c}")
                step(g.tensor_copy(ulast[:, c, :].rearrange("p (b r) -> p b r", b=DB),
                                   sample_cols(ue, c, PH)), packed)
            for c in range(PG):
                if c:
                    pool.wait_ge(acc_pool, c)
                src = ue[:, c, :]
                for k in range(c + 1):
                    off = 1 << k
                    dst = (ptmp[:, :], ptmp2)[(c - k) % 2]
                    step(g.tensor_copy(dst[:, 0:off], src[:, 0:off]))
                    step(g.tensor_tensor(dst[:, off:UEW], src[:, off:UEW], src[:, 0:UEW - off], ALU.add),
                         g_ready if k == c else None)
                    src = dst
            pool.wait_ge(s0_in, 16)
            is_drained(pool, "egs")
            is_filled(pool, "kqs")
            for h in range(HEADS):
                step(g.tensor_tensor(s0[:, :, h, :], s0[:, :, h, :],
                                     egs[:, h, :].unsqueeze(2).broadcast_to([P, DB, P]), ALU.mult), g_ready)
            is_drained(pool, "v2")
            is_drained(pool, f"QT20")
            is_filled(pool, "o2")
            for h in range(HEADS):
                if h:
                    is_filled(pool, f"ns{h - 1}b")
                step(g.tensor_tensor(vmask, vN[0:NSAMP, 2, h, :].unsqueeze(1).broadcast_to([NSAMP, DB, P]),
                                     seg[:, 0:NSAMP:DS].unsqueeze(2).broadcast_to([NSAMP, DB, P]), ALU.mult), vmasked)

        @block.scalar
        def _(act):
            step = chain(act, a_step)
            a = nc.scalar

            rooted = [0]

            def root(ap):
                rooted[0] += 1
                act.wait_ge(inv_ready, rooted[0])
                step(a.activation(ap, ap, ACT.Sqrt), root_ready)

            def copy(out, in_, name):
                is_filled(act, name)
                step(a.activation(out, in_, ACT.Copy), dsem(name), uses[name][1] + 1)

            for t, (t0, n) in enumerate(TILES):
                act.wait_ge(x_in[t], 16)
                act.wait_ge(small_zero, 1)
                step(a.activation(h3[0:n, t, :], x3[0:n, t, :], ACT.Square, accum_out=ss[0:n, t:t + 1]),
                     a_mark if t == NT - 1 else None, AM["ss"] if t == NT - 1 else None)
            root(rstd[:, :])
            copy(vecs[:, :], bank("vec")[:, 0:77], "vec")
            act.wait_ge(ext_zero, PG + QKV_T)
            is_filled(act, "sc")
            scv = bank("sc")[:, 0:QKV_T * DB * CH].rearrange("p (c b r) -> p c b r", c=QKV_T, b=DB)
            for c in range(QKV_T):
                ins = a.activation(sample_cols(qe, c, CH, 0, CH), scv[:, c], ACT.Copy)
                step(ins, dsem("sc") if c == QKV_T - 1 else None, uses["sc"][1] + 1)
            is_filled(act, "sp")
            spv = bank("sp")[:, 0:PG * DB * PH].rearrange("p (c b r) -> p c b r", c=PG, b=DB)
            for c in range(PG):
                ins = a.activation(sample_cols(ue, c, PH, 0, PH), spv[:, c], ACT.Copy)
                step(ins, dsem("sp") if c == PG - 1 else None, uses["sp"][1] + 1)

            def silu_conv(c):
                act.wait_ge(acc_ready, convord[c] + 1)
                step(a.activation(ct[:, c, :], ct[:, c, :], ACT.Silu), ct_ready)

            def square(i):
                if i >= 2:
                    is_filled(act, f"ss{i - 2}")
                step(a.activation(sqb[i % 2], ct[:, NORMED[i], :], ACT.Square), sq_ready)

            def evacuate(c):
                name = f"pr{c}"
                is_filled(act, name)
                src = bank(name)
                if c >= 16:
                    step(a.activation(zT[:, c - 16, :], src[:, 0:T], ACT.Silu), dsem(name), uses[name][1] + 1)
                    return
                v, cc, hist = (ue, c, PH) if c < 4 else (qe, c - 4, CH)
                step(a.activation(prompt_cols(v, cc, hist), src[:, 0:SEQ], ACT.Copy))
                step(a.activation(sample_cols(v, cc, hist), src[:, SEQ:T].rearrange("p (b s) -> p b s", b=DB),
                                  ACT.Copy), dsem(name), uses[name][1] + 1)

            act.wait_ge(v_mark, VM["ba"])
            step(a.activation(beta[:, :, :], beta[:, :, :], ACT.Exp, scale=-1.0), a_mark, AM["exps"])
            act.wait_ge(smalls_in, 64)
            step(a.activation(alog, alog, ACT.Exp), a_mark, AM["ea"])
            act.wait_ge(v_mark, VM["sp_in"])
            step(a.activation(tmp12[:, :, :], tmp12[:, :, :], ACT.Exp, scale=-1.0))
            step(a.activation(tmp12[:, :, :], tmp12[:, :, :], ACT.Ln, bias=1.0), a_mark, AM["lg"])
            prev = []
            for b in IN_ORDER[:2]:
                for c in range(4 * b, 4 * b + 4):
                    evacuate(c)
                    if prev:
                        silu_conv(prev.pop(0))
                    prev.append(c - 4)
            square(0)
            square(1)
            silu_conv(prev.pop(0))
            act.wait_ge(v_mark, VM["gcs"])
            step(a.activation(egc[:, :, :], gc[:, :, :], ACT.Exp))
            step(a.activation(kdec[:, :, :], kdec[:, :, :], ACT.Exp))
            step(a.activation(egl[:, :, :], egl[:, :, :], ACT.Exp), a_mark, AM["gexp"])
            is_filled(act, "egs")
            step(a.activation(egs[:, :, :], bank("egs")[:, 0:HEADS * DB].rearrange("p (h b) -> p h b", h=HEADS),
                              ACT.Exp), dsem("egs"), uses["egs"][1] + 1)
            for i in range(8):
                evacuate(VU[i])
                if 1 <= i <= 4:
                    silu_conv(7 + i)
                if i:
                    root(rnb[(i - 1) % 3])
                if i + 2 < 8:
                    square(i + 2)
            root(rnb[7 % 3])
            evacuate(16)
            copy(outrow[0:PH, 3072:3584], bank("npp")[0:PH, :], "npp")
            copy(outrow[0:NSAMP, 3584:4096], bank("nps")[0:NSAMP, :], "nps")
            evacuate(17)
            evacuate(18)
            evacuate(19)
            for i in range(3):
                copy(outrow[0:CH, i * 512:(i + 1) * 512], bank(f"cnp{i}")[0:CH, :], f"cnp{i}")
            for i in range(3):
                copy(outrow[0:DB * CH, 1536 + i * 512:2048 + i * 512], bank(f"cns{i}")[0:DB * CH, :], f"cns{i}")
            act.dma_start(o[3][0, 0], outrow[0:CH, 0:1536]).then_inc(hist_stored, 16)
            act.dma_start(o[6][0].rearrange("b r c -> (b r) c"), outrow[0:DB * CH, 1536:3072]).then_inc(hist_stored, 16)
            act.dma_start(o[2][0, 0], outrow[0:PH, 3072:3584]).then_inc(hist_stored, 16)
            act.dma_start(o[5][0, :, PH - DS:PH, :], outrow[0:NSAMP, 3584:4096]).then_inc(hist_stored, 16)
            act.dma_start(o[5][0, :, 0:PH - DS, :], d["state_pool"][0, :, DS:PH, :]).then_inc(pool_stored, 16)
            for t, (t0, n) in enumerate(TILES):
                act.wait_ge(v_mark, VM[f"diff{t}"])
                step(a.activation(scratch[t][0], scratch[t][0], ACT.Exp), a_mark, AM[f"E{t}"])
            for t, (t0, n) in enumerate(TILES):
                copy(kN[0:n, t], bank(f"kN{t}")[0:n, :].rearrange("p (h d) -> p h d", h=HEADS), f"kN{t}")
            for t, (t0, n) in enumerate(TILES):
                copy(vN[0:n, t], bank(f"vN{t}")[0:n, :].rearrange("p (h d) -> p h d", h=HEADS), f"vN{t}")
            for t in ORDER:
                root(tmp12[0:TILES[t][1], t, :])
            act.wait_ge(v_mark, VM["S2"])
            act.dma_start(o[4][0, 0].rearrange("h d e -> d h e"), S1).then_inc(ssm_stored, 16)
            for t in ORDER:
                t0, n = TILES[t]
                act.wait_ge(v_mark, VM[f"x2{t}"])
                step(a.activation(h3[0:n, t, :], x3[0:n, t, :], ACT.Square, accum_out=ss[0:n, t:t + 1]),
                     a_mark, AM[f"ss2{t}"])
                root(rstd[0:n, t:t + 1])
            is_filled(act, "lg")
            step(a.activation(logT, bank("lg")[0:E, 0:T], ACT.Identity, bias=rb), dsem("lg"), uses["lg"][1] + 1)
            act.wait_ge(v_mark, VM["m8"])
            step(a.activation(exq[:, :, :], exq[:, :, :], ACT.Exp), a_mark, AM["exq"])
            act.wait_ge(v_mark, VM["S0"])
            act.dma_start(o[7][0].rearrange("b h d e -> d b h e"), s0).then_inc(s0_stored, 16)
            copy(xg[:, 0:512], bank("ga"), "ga")
            copy(xg[:, 512:1024], bank("gb"), "gb")
            copy(SgT[0][:, :, :], bank("sgt")[:, 0:384].rearrange("p (t s) -> p t s", t=NT), "sgt")

            def turns(lo, hi):
                with act.Fori(lo, hi) as i:
                    for half in range(2):
                        def lstep(ins, s, v):
                            ins.then_inc(s, 1)
                            act.wait_ge(s, v)

                        def aux(k, out, in_):
                            l = 13 * half + k
                            b, m = 6 + l % 2, l // 2
                            act.wait_ge(filled[b], base[b] + 1 + m + i * 13)
                            lstep(a.activation(out, in_, ACT.Copy), drained[b], base[b] + 1 + m + i * 13)

                        act.wait_ge(g_act, i * 2 + half + 2)
                        lstep(a.activation(sbuf_, gbuf, ACT.Sigmoid, scale=ALPHA), sig_act, i * 2 + half + 1)
                        aux(0, xg[:, 0:512], PS[:, 6 + (13 * half) % 2, :])
                        aux(1, xg[:, 512:1024], PS[:, 6 + (13 * half + 1) % 2, :])
                        aux(8, hidf[:, 0:512], PS[:, 6 + (13 * half + 8) % 2, :])
                        aux(9, hidf[:, 512:1024], PS[:, 6 + (13 * half + 9) % 2, :])
                        aux(10, SgT[1 - half][:, :, :],
                            PS[:, 6 + (13 * half + 10) % 2, 0:384].rearrange("p (t s) -> p t s", t=NT))
                        act.wait_ge(chunk_used, i * TURN + (half + 1) * CPP)
                        lstep(a.activation(ybuf, PS[:, 4:6, :].rearrange("p b f -> p (b f)"), ACT.Copy),
                              y_act, i * 2 + half + 2)
            turns(0, MID)
            act.wait_ge(v_mark, VM["table"])
            n_ov = act.value_load(ov_n[0:1, 0:1], min_val=0, max_val=OV_MAX)

            def overflow_block(j):
                def ovaux(k, out, in_, last=False):
                    b, m = k % 2, k // 2
                    act.wait_ge(ov_filled[b], 1 + m + j * OV_USES)
                    ins = a.activation(out, in_, ACT.Copy)
                    ins.then_inc(ov_drained[b], 1)
                    if not last:
                        act.wait_ge(ov_drained[b], 2 + m + j * OV_USES)
                ovaux(0, xg[:, 0:512], PS[:, 6, :])
                ovaux(1, xg[:, 512:1024], PS[:, 7, :])
                act.wait_ge(ovg_act, j + 1)
                a.activation(sbuf_, gbuf, ACT.Sigmoid, scale=ALPHA).then_inc(ovs_act, 1)
                ovaux(4, hidf[:, 0:512], PS[:, 6, :])
                ovaux(5, hidf[:, 512:1024], PS[:, 7, :])
                ovaux(6, SgT[0][:, 0:2, :], PS[:, 6, 0:256].rearrange("p (t s) -> p t s", t=2))
                ovaux(7, SgT[0][:, 2, :], PS[:, 7, 0:128])
                act.wait_ge(ov_used, j * OV_CHUNKS + 2 * OV_CHUNKS)
                a.activation(gbuf, PS[:, 4:6, :].rearrange("p b f -> p (b f)"), ACT.Copy).then_inc(ovy_act, 1)
                ovaux(8, xg[:, 0:512], PS[:, 6, :])
                ovaux(9, xg[:, 512:1024], PS[:, 7, :])
                ovaux(18, SgT[0][:, 0:2, :], PS[:, 6, 0:256].rearrange("p (t s) -> p t s", t=2))
                ovaux(19, SgT[0][:, 2, :], PS[:, 7, 0:128], last=True)

            with act.Fori(0, OV_FIRST) as j:
                with act.If(j < n_ov):
                    overflow_block(j)
            with act.If(n_ov > OV_FIRST):
                with act.Fori(OV_FIRST, OV_MAX) as j:
                    with act.If(j < n_ov):
                        overflow_block(j)
            turns(MID, TURNS)
            copy(pT[:, 0, :], bank("pT0")[:, 0:T], "pT0")
            copy(pT[:, 1, :], bank("pT1")[:, 0:T], "pT1")
            for t, (t0, n) in enumerate(TILES):
                act.wait_ge(v_mark, VM[f"moe{t}"])
                step(a.activation(h3[0:n, t, :], x3[0:n, t, :], ACT.Square, accum_out=ss[0:n, t:t + 1]),
                     a_mark, AM[f"ss3{t}"])
                root(rstd[0:n, t:t + 1])
            for t, (t0, n) in enumerate(TILES):
                for hf in range(2):
                    copy(ppb[0:n, t, hf * 512:(hf + 1) * 512], bank(f"pp{t}{hf}")[0:n, :], f"pp{t}{hf}")

            for t, (t0, n) in enumerate(TILES):
                for hf in range(2):
                    nm = f"pg{t}{hf}"
                    is_filled(act, nm)
                    step(a.activation(sg3[0:n, t, hf * 512:(hf + 1) * 512], product_of("pg", t, hf), ACT.Sigmoid),
                         dsem(nm), uses[nm][1] + 1)
                act.wait_ge(v_mark, VM[f"y{t}"])
                step(a.activation(h3[0:n, t, :], x3[0:n, t, :], ACT.Square, accum_out=ss[0:n, t:t + 1]),
                     a_mark, AM[f"ss4{t}"])
                root(rstd[0:n, t:t + 1])

        @block.tensor
        def _(pe):
            mm = nc.tensor.matmul
            seen = [0] * 8

            def fill(name):
                b, k = uses[name]
                assert k == seen[b], (name, k, seen[b])
                seen[b] += 1
                can_fill(pe, name)
                return PS[:, b, :]

            def tr(out, in_):
                n = in_.shape[0]
                return nc.tensor.transpose(out, in_, ident[0:n, 0:n])

            pe.wait_ge(consts, 1)
            pe.wait_ge(vecs_in, 16 * 6)
            tr(fill("vec")[:, 0:77], vrows).then_inc(fsem("vec"), 1)
            pe.wait_ge(hist_in, 32)
            ps = fill("sc")
            for c in range(QKV_T):
                last = tr(ps[:, c * 24:(c + 1) * 24], st_conv[:, c * P:(c + 1) * P])
            last.then_inc(fsem("sc"), 1)
            ps = fill("sp")
            for c in range(PG):
                last = tr(ps[:, c * 120:(c + 1) * 120], st_pool[:, c * P:(c + 1) * P])
            last.then_inc(fsem("sp"), 1)

            def transposes(prefix, ready=None, order=range(NT)):
                for t in order:
                    t0, n = TILES[t]
                    if ready:
                        pe.wait_ge(v_mark, VM[f"{ready}{t}"])
                    for hf in range(2):
                        ps = fill(f"{prefix}{t}{hf}")
                        for k in range(4):
                            c0 = (hf * 4 + k) * P
                            last = tr(ps[:, k * n:(k + 1) * n], h3[0:n, t, c0:c0 + P])
                        last.then_inc(fsem(f"{prefix}{t}{hf}"), 1)

            pe.wait_ge(h_ready, NT)
            transposes("hT")
            for t in range(NT):
                for hf in range(2):
                    is_drained(pe, f"hT{t}{hf}")
            pe.wait_ge(wtail_in, 16)
            ps = fill("ba")
            for t, (t0, n) in enumerate(TILES):
                for k in range(KT):
                    last = mm(ps[0:n, t * 8:(t + 1) * 8], hT[:, k, t0:t0 + n], wtail[:, k, :],
                              start=(k == 0), stop=(k == KT - 1))
            last.then_inc(fsem("ba"), 1)
            def project(c):
                i = IN_ORDER.index(c // 4)
                if c % 4 == 0:
                    pe.wait_ge(win_in[i], 16)
                w = ring[:, i, :].rearrange("p (k c) -> p k c", k=KT)
                name = f"pr{c}"
                ps = fill(name)
                for k in range(KT):
                    last = mm(ps[:, 0:T], w[:, k, (c % 4) * P:(c % 4 + 1) * P], hT[:, k, :],
                              start=(k == 0), stop=(k == KT - 1))
                last.then_inc(fsem(name), 1)
                if c % 4 == 3:
                    is_filled(pe, name)
                    pe.nop().then_inc(win_used, 1)

            for b in IN_ORDER[:2]:
                for c in range(4):
                    project(4 * b + c)
            pe.wait_ge(consts, 3)
            pe.wait_ge(v_mark, VM["g"])
            ps = fill("gcs")
            for t, (L, one, t0, n) in enumerate(tilepart):
                mm(ps[0:n, t * 4:t * 4 + 4], L[0:n, 0:n], gl[0:n, t, :], start=True, stop=True)
                last = mm(ps[0:n, 12 + t * 4:16 + t * 4], one[0:n, 0:n], gl[0:n, t, :], start=True, stop=True)
            last.then_inc(fsem("gcs"), 1)
            ps = fill("egs")
            for h in range(HEADS):
                last = mm(ps[:, h * DB:(h + 1) * DB], gl[0:NSAMP, 2, h:h + 1].broadcast_to([NSAMP, P]),
                          seg[:, 0:NSAMP:DS], start=True, stop=True)
            last.then_inc(fsem("egs"), 1)
            for i in range(8):
                project(VU[i])
                ps = fill(f"ss{i}")
                pe.wait_ge(sq_ready, i + 1)
                mm(ps[:, 0:T], ones[:, :], sqb[i % 2], start=True, stop=True).then_inc(fsem(f"ss{i}"), 1)
            project(16)
            pe.wait_ge(packed, QKV_T + PG)
            ps = fill("npp")
            for c in range(PG):
                last = tr(ps[0:PH, c * P:(c + 1) * P], ue[:, c, SEQ:SEQ + PH])
            last.then_inc(fsem("npp"), 1)
            ps = fill("nps")
            for c in range(PG):
                last = tr(ps[0:NSAMP, c * P:(c + 1) * P], ulast[:, c, :])
            last.then_inc(fsem("nps"), 1)
            project(17)
            project(18)
            project(19)
            for i in range(3):
                ps = fill(f"cnp{i}")
                for c in range(4):
                    last = tr(ps[0:CH, c * P:(c + 1) * P], qe[:, 4 * i + c, SEQ:SEQ + CH])
                last.then_inc(fsem(f"cnp{i}"), 1)
            for i in range(3):
                ps = fill(f"cns{i}")
                for c in range(4):
                    last = tr(ps[0:DB * CH, c * P:(c + 1) * P], clast[:, 4 * i + c, :])
                last.then_inc(fsem(f"cns{i}"), 1)
            pe.wait_ge(poolw_in, 16)
            for g in range(PG):
                pe.wait_ge(d_ready, g + 1)
                ps = fill(f"pm{g}")
                mm(ps[:, 0:SEQ], poolw[:, g, :], prompt_cols(ue, g, PH), start=True, stop=True)
                mm(ps[:, SEQ:T], poolw[:, g, :], sample_cols(ue, g, PH), start=True, stop=True
                   ).then_inc(fsem(f"pm{g}"), 1)

            def per_head(name, n, m, lhs, rhs):
                ps = fill(name)
                for h in range(HEADS):
                    last = mm(ps[0:n, h * m:(h + 1) * m], lhs(h), rhs(h), start=True, stop=True)
                last.then_inc(fsem(name), 1)

            pe.wait_ge(norm_ready, 8)
            pe.wait_ge(ct_ready, QKV_T)
            for t, (L, one, t0, n) in enumerate(tilepart):
                per_head(f"G{t}", n, n, lambda h: gl[0:n, t, h:h + 1].broadcast_to([n, n]), lambda h: L[0:n, 0:n])
                per_head(f"kk{t}", n, n, lambda h: ct[:, 4 + h, t0:t0 + n], lambda h: ct[:, 4 + h, t0:t0 + n])
                per_head(f"qk{t}", n, n, lambda h: ct[:, 4 + h, t0:t0 + n], lambda h: ct[:, h, t0:t0 + n])
            ps = fill("kqs").rearrange("p (h q t) -> p h q t", h=HEADS, q=2)
            pe.wait_ge(s0_in, 16)
            for h in range(HEADS):
                for b in range(DB):
                    c = SEQ + b * DS
                    last = mm(ps[:, h, :, b * DS:(b + 1) * DS], s0[:, b, h, :], ct[:, h:h + 5:4, c:c + DS],
                              start=True, stop=True)
            last.then_inc(fsem("kqs"), 1)
            for t, (t0, n) in enumerate(TILES):
                pe.wait_ge(v_mark, VM[f"U{t}"])
                ps = fill(f"T{t}")
                for h in range(HEADS):
                    last = tr(ps[0:n, h * n:(h + 1) * n], scratch[t][3][:, h, :])
                last.then_inc(fsem(f"T{t}"), 1)
                if t < 2:
                    pre, c0 = (("kN", 4), ("vN", 8))[t]
                    for u, (u0, m) in enumerate(TILES):
                        ps = fill(f"{pre}{u}")
                        for h in range(HEADS):
                            last = tr(ps[0:m, h * P:(h + 1) * P], ct[:, c0 + h, u0:u0 + m])
                        last.then_inc(fsem(f"{pre}{u}"), 1)
            for s in range(1, LEVELS):
                ts = [t for t in range(NT) if t < 2 or s < 3]
                for t in ts:
                    n = TILES[t][1]
                    sc = scratch[t]
                    if s == 1:
                        is_drained(pe, f"T{t}")
                    else:
                        is_drained(pe, f"QT{s - 1}{t}")
                    per_head(f"P{s}{t}", n, n, lambda h: sc[2][:, h, :], lambda h: sc[4][:, h, :])
                for t in ts:
                    n = TILES[t][1]
                    sc = scratch[t]
                    is_drained(pe, f"P{s}{t}")
                    if f"Q{s}{t}" in uses:
                        per_head(f"Q{s}{t}", n, n, lambda h: sc[3][:, h, :], lambda h: sc[5][:, h, :])
                    per_head(f"QT{s}{t}", n, n, lambda h: sc[5][:, h, :], lambda h: sc[3][:, h, :])
                if s == 2:
                    is_drained(pe, "kqs")
                    for nm, q in (("R2k", 1), ("R2q", 0)):
                        ps = fill(nm)
                        for h in range(HEADS):
                            last = tr(ps[0:NSAMP, h * P:(h + 1) * P], kqS[:, h, q * NSAMP:(q + 1) * NSAMP])
                        last.then_inc(fsem(nm), 1)
            pe.wait_ge(v_mark, VM["kd"])
            is_drained(pe, f"QT{LEVELS - 1}0")
            per_head("v0", P, P, lambda h: scratch[0][3][:, h, :], lambda h: vN[:, 0, h, :])
            is_drained(pe, "R2k"), is_drained(pe, "QT22")
            per_head("v2", NSAMP, P, lambda h: scratch[2][3][:, h, :], lambda h: vN[0:NSAMP, 2, h, :])
            is_drained(pe, "v0")
            per_head("S1", P, P, lambda h: kN[:, 0, h, :], lambda h: vN[:, 0, h, :])
            per_head("o0", P, P, lambda h: scratch[0][1][:, h, :], lambda h: vN[:, 0, h, :])
            is_drained(pe, "S1")
            per_head("kS1", P, P, lambda h: ct[:, 4 + h, P:SEQ], lambda h: S1[:, h, :])
            is_drained(pe, "v2")
            per_head("o2", NSAMP, P, lambda h: scratch[2][1][:, h, :], lambda h: vN[0:NSAMP, 2, h, :])
            per_head("qS1", P, P, lambda h: ct[:, h, P:SEQ], lambda h: S1[:, h, :])
            is_drained(pe, "kS1"), is_drained(pe, f"QT{LEVELS - 1}1")
            per_head("v1", P, P, lambda h: scratch[1][3][:, h, :], lambda h: vN[:, 1, h, :])

            def turn_outputs(t):
                t0, n = TILES[t]
                pe.wait_ge(v_mark, VM[f"rs{t}"])
                ps = fill(f"oT{t}")
                for h in range(HEADS):
                    last = tr(ps[:, h * n:(h + 1) * n], oN[t][0:n, h, :])
                last.then_inc(fsem(f"oT{t}"), 1)

            def state_update(h):
                pe.wait_ge(vmasked, h + 1)
                for q in range(2):
                    nm = f"ns{h}{'ab'[q]}"
                    mm(fill(nm), kN[0:NSAMP, 2, h, :],
                       vmask[:, 4 * q:4 * q + 4, :].rearrange("p b d -> p (b d)"), start=True, stop=True
                       ).then_inc(fsem(nm), 1)

            wo = ring[:, 5:7, :].rearrange("p s (k f) -> p (s k) f", k=4)

            def full_product(prefix, t, w, between=None):
                t0, n = TILES[t]
                if n == P:
                    for hf in range(2):
                        if hf and between:
                            between()
                        ps = fill(f"{prefix}{t}{hf}")
                        for k in range(KT):
                            last = mm(ps, hT[:, k, t0:t0 + n], w[:, k, hf * 512:(hf + 1) * 512],
                                      start=(k == 0), stop=(k == KT - 1))
                        last.then_inc(fsem(f"{prefix}{t}{hf}"), 1)
                    return
                halves = [fill(f"{prefix}{t}{hf}")[hf * n:(hf + 1) * n, :] for hf in range(2)]
                for k in range(KT):
                    for hf in range(2):
                        last = mm(halves[hf], hT[:, k, t0:t0 + n], w[:, k, hf * 512:(hf + 1) * 512],
                                  start=(k == 0), stop=(k == KT - 1))
                        if k == KT - 1:
                            last.then_inc(fsem(f"{prefix}{t}{hf}"), 1)

            def output_projection(t, between=None):
                is_drained(pe, f"oT{t}")
                full_product("op", t, wo, between)

            turn_outputs(0)
            is_drained(pe, "v1")
            per_head("o1", P, P, lambda h: scratch[1][1][:, h, :], lambda h: vN[:, 1, h, :])
            turn_outputs(2)
            per_head("S2", P, P, lambda h: kN[:, 1, h, :], lambda h: vN[:, 1, h, :])
            pe.wait_ge(wout_in, 32)
            for g in range(PG):
                is_drained(pe, f"pm{g}")
            output_projection(0)
            turn_outputs(1)
            output_projection(2)
            output_projection(1, lambda: transposes("rT", "h2", ORDER[:2]))
            state_update(0)
            state_update(1)
            transposes("rT", "h2", ORDER[2:])
            pe.wait_ge(smalls_in, 64)
            for t in range(NT):
                for hf in range(2):
                    is_drained(pe, f"rT{t}{hf}")
            ps = fill("lg")
            for k in range(KT):
                last = mm(ps[0:E, 0:T], wrout[:, k, :], hT[:, k, :], start=(k == 0), stop=(k == KT - 1))
            last.then_inc(fsem("lg"), 1)
            is_drained(pe, "lg")
            ps = fill("lgT")
            for t, (t0, n) in enumerate(TILES):
                last = tr(ps[0:n, t * E:(t + 1) * E], logT[:, t0:t0 + n])
            last.then_inc(fsem("lgT"), 1)
            state_update(2)
            pe.wait_ge(v_mark, VM["sel"])
            ps = fill("rk")
            for t in range(NT):
                for u in range(t):
                    mm(ps[:, t * E:(t + 1) * E], ones[:, :], sel[:, u, :], start=(u == 0), stop=False)
                mm(ps[:, t * E:(t + 1) * E], strict[:, :], sel[:, t, :], start=(t == 0), stop=True)
            for u in range(NT):
                last = mm(ps[:, NT * E:(NT + 1) * E], ones[:, :], sel[:, u, :], start=(u == 0), stop=(u == NT - 1))
            last.then_inc(fsem("rk"), 1)

            def gather(k0, fills):
                for hf in range(2):
                    ps, sm_ = fills(k0 + hf)
                    for t in range(NT):
                        last = mm(ps, Ssel[:, t, :], h3[:, t, hf * 512:(hf + 1) * 512], start=(t == 0), stop=(t == NT - 1))
                    last.then_inc(sm_, 1)

            def turn(k0, fills, src):
                for hf in range(2):
                    ps, sm_ = fills(k0 + hf)
                    for k in range(4):
                        c0 = (hf * 4 + k) * P
                        last = tr(ps[:, k * P:(k + 1) * P], src[:, c0:c0 + P])
                    last.then_inc(sm_, 1)

            state_update(3)
            pe.wait_ge(v_mark, VM["split"])
            for s in (g_act, up_act, y_act):
                pe.nop().then_inc(s, 1)
            def turns(lo, hi, n_ov=None):
                with pe.Fori(lo, hi) as i:
                    for half in range(2):
                        pair = i * 2 + half

                        def aux(k):
                            l = 13 * half + k
                            b, m = 6 + l % 2, l // 2
                            pe.wait_ge(drained[b], base[b] + m + i * 13)
                            return PS[:, b, :], filled[b]

                        def product(c0, b0, lhs, bias):
                            for hf in range(2):
                                mm(PS[:, b0 + hf, :], ind[:, half, :],
                                   biases[bias][:, hf * 512:(hf + 1) * 512], start=True, stop=False, skip_group_check=True)
                            for c in range(c0, c0 + CPM):
                                pe.wait_ge(chunk_in[half * CPP + c], i * 32 + 32)
                                w = slot(half * CPP + c)
                                for kk in range(2):
                                    k = (c - c0) * 2 + kk
                                    for hf in range(2):
                                        for a_ in range(2):
                                            last = mm(PS[64 * a_:64 * a_ + 64, b0 + hf, :], lhs[:, k, 64 * a_:64 * a_ + 64],
                                                      w[:, a_, kk, hf * 512:(hf + 1) * 512],
                                                      start=False, stop=(k == KT - 1),
                                                      skip_group_check=True)
                                last.then_inc(chunk_used, 1)

                        pe.wait_ge(pair_sel, pair + 1)
                        pe.wait_ge(drained[6], base[6] + i * 13 + 7 * half)
                        pe.wait_ge(drained[7], base[7] + i * 13 + 6 * half)
                        if n_ov is not None and half == 0:
                            for s in ov_drained:
                                pe.wait_ge(s, n_ov * OV_USES + 1)
                        pe.wait_ge(g_act, pair + 1)
                        product(0, 0, xgT, 0)
                        pe.wait_ge(up_act, pair + 1)
                        product(CPM, 2, xgT, 1)
                        pe.wait_ge(pair_sel, pair + 2)
                        gather(0, aux)
                        pe.wait_ge(y_act, pair + 1)
                        pe.wait_ge(v_mark, VM["ybuf_zero"])
                        for t, (t0, n) in enumerate(TILES):
                            for hf in range(2):
                                ps, sm_ = aux(2 + 2 * t + hf)
                                mm(ps[0:n, :], SgT[1 - half][:, t, 0:n], ybuf[:, hf * 512:(hf + 1) * 512],
                                   start=True, stop=True).then_inc(sm_, 1)
                        pe.wait_ge(hid_act, pair + 1)
                        turn(8, aux, ubuf)
                        ps, sm_ = aux(10)
                        for t in range(NT):
                            last = tr(ps[:, t * P:(t + 1) * P], Sgat[:, t, :])
                        last.then_inc(sm_, 1)
                        turn(11, aux, xg)
                        product(2 * CPM, 4, hidT, 2)
            def scatter(fillb, sg, y):
                for t, (t0, n) in enumerate(TILES):
                    for hf in range(2):
                        ps, sm_ = fillb(t, hf)
                        mm(ps[0:n, :], sg[:, t, 0:n], y[:, hf * 512:(hf + 1) * 512], start=True, stop=True
                           ).then_inc(sm_, 1)

            pe.wait_ge(pair_sel, 1)
            names = ["ga", "gb", "xta", "xtb", "sgt"]
            gather(0, lambda k: (fill(names[k]), fsem(names[k])))
            is_drained(pe, "ga"), is_drained(pe, "gb")
            turn(2, lambda k: (fill(names[k]), fsem(names[k])), xg)
            ps = fill("sgt")
            for t in range(NT):
                last = tr(ps[:, t * P:(t + 1) * P], Sgat[:, t, :])
            last.then_inc(fsem("sgt"), 1)
            is_drained(pe, "xta"), is_drained(pe, "xtb"), is_drained(pe, "sgt")
            turns(0, MID)
            for b in (6, 7):
                pe.wait_ge(drained[b], base[b] + 13 * MID)
            pe.wait_ge(y_act, 2 * MID + 1)
            for s in ov_drained:
                pe.nop().then_inc(s, 1)
            pe.wait_ge(v_mark, VM["table"])
            n_ov = pe.value_load(ov_n[0:1, 0:1], min_val=0, max_val=OV_MAX)

            def overflow_block(j):
                def ovaux(k):
                    b, m = k % 2, k // 2
                    pe.wait_ge(ov_drained[b], m + 1 + j * OV_USES)
                    return PS[:, 6 + b, :], ov_filled[b]

                def ovproduct(c0, b0, lhs, bias):
                    for hf in range(2):
                        mm(PS[:, b0 + hf, :], ind[:, 0, :],
                           biases[bias][:, hf * 512:(hf + 1) * 512], start=True, stop=False)
                    for c in range(c0, c0 + 2):
                        pe.wait_ge(ovch_in[c], j * 16 + 16)
                        w = ring[:, c, :].rearrange("p (k f) -> p k f", k=4)
                        for kk in range(4):
                            k = (c - c0) * 4 + kk
                            for hf in range(2):
                                last = mm(PS[:, b0 + hf, :], lhs[:, k, :], w[:, kk, hf * 512:(hf + 1) * 512],
                                          start=False, stop=(k == KT - 1))
                        last.then_inc(ov_used, 1)

                def ovdrained(k):
                    pe.wait_ge(ov_drained[k % 2], k // 2 + 2 + j * OV_USES)

                pe.wait_ge(ov_sel, j + 1)
                gather(0, ovaux)
                ovdrained(0), ovdrained(1)
                turn(2, ovaux, xg)
                ovdrained(2), ovdrained(3)
                ovproduct(0, 0, xgT, 0)
                ovproduct(2, 2, xgT, 1)
                pe.wait_ge(ovh_act, j + 1)
                turn(4, ovaux, ubuf)

                def turn_gates(k0):
                    for k, ts in ((k0, (0, 1)), (k0 + 1, (2,))):
                        ps, sm_ = ovaux(k)
                        for q, t in enumerate(ts):
                            last = tr(ps[:, q * P:(q + 1) * P], Sgat[:, t, :])
                        last.then_inc(sm_, 1)
                turn_gates(6)
                ovdrained(4), ovdrained(5)
                ovproduct(4, 4, hidT, 2)
                pe.wait_ge(ov_next, j + 1)
                gather(8, ovaux)
                pe.wait_ge(ovy_act, j + 1)
                ovdrained(6), ovdrained(7)
                scatter(lambda t, hf: ovaux(10 + 2 * t + hf), SgT[0], gbuf)
                ovdrained(8), ovdrained(9)
                turn(16, ovaux, xg)
                turn_gates(18)

            with pe.Fori(0, OV_FIRST) as j:
                with pe.If(j < n_ov):
                    overflow_block(j)
            with pe.If(n_ov > OV_FIRST):
                with pe.Fori(OV_FIRST, OV_MAX) as j:
                    with pe.If(j < n_ov):
                        overflow_block(j)
            turns(MID, TURNS, n_ov)
            for b in (6, 7):
                seen[b] += 13 * TURNS
            pe.wait_ge(tail_in, 16 * 4)
            for k in range(2):
                ps = fill(f"pT{k}")
                for t, (t0, n) in enumerate(TILES):
                    last = tr(ps[:, t0:t0 + n], pin[0:n, t, k * P:(k + 1) * P])
                last.then_inc(fsem(f"pT{k}"), 1)
            pe.wait_ge(y_act, PAIRS + 1)
            scatter(lambda t, hf: (fill(f"sc{t}{hf}"), fsem(f"sc{t}{hf}")), SgT[1], ybuf)
            is_drained(pe, "pT0"), is_drained(pe, "pT1")
            for t, (t0, n) in enumerate(TILES):
                for hf in range(2):
                    cs = slice(hf * 512, (hf + 1) * 512)
                    ps = fill(f"pp{t}{hf}")
                    for k in range(2):
                        last = mm(ps[0:n, :], pT[:, k, t0:t0 + n], wple[:, k, cs], start=(k == 0), stop=(k == 1))
                    last.then_inc(fsem(f"pp{t}{hf}"), 1)
            transposes("tT", "h3")
            pe.wait_ge(wpg_in, 16)
            for t, (t0, n) in enumerate(TILES):
                is_drained(pe, f"tT{t}0"), is_drained(pe, f"tT{t}1")
                full_product("pg", t, wpg)

        @block.vector
        def _(dve):
            step = chain(dve, v_step)
            v = nc.vector
            marked = [0]
            roots = [0]

            def mark(ins, name):
                marked[0] += 1
                assert VM[name] == marked[0], (name, VM[name], marked[0])
                ins.then_inc(v_mark, 1)
                dve.wait_ge(v_mark, marked[0])

            def drain(ins, name):
                step(ins, dsem(name), uses[name][1] + 1)

            def over(ap, h, m):
                n = ap.shape[0]
                return ap.unsqueeze(2).broadcast_to([n, h, m])

            def heads(ap, m):
                n = ap.shape[0]
                return ap.unsqueeze(1).broadcast_to([n, HEADS, m])

            def rsqrt_of(ap, in_, scale, eps=EPS):
                step(v.tensor_scalar(ap, in_, scale, eps, ALU.mult, ALU.add))
                step(v.reciprocal(ap, ap), inv_ready)
                roots[0] += 1
                dve.wait_ge(root_ready, roots[0])

            step(v.memset(small[:, :], 0.0), small_zero)
            dve.wait_ge(a_mark, AM["ss"])
            rsqrt_of(rstd[:, :], ss[:, :], 1.0 / D_MODEL)
            for t, (t0, n) in enumerate(TILES):
                step(v.tensor_scalar(h3[0:n, t, :], x3[0:n, t, :], rstd[0:n, t:t + 1], None, ALU.mult), h_ready)

            def evac_hT(prefix, ln, order=range(NT)):
                for t in order:
                    t0, n = TILES[t]
                    for hf in range(2):
                        name = f"{prefix}{t}{hf}"
                        is_filled(dve, name)
                        w = vec(ln, hf * 4, 4).unsqueeze(2).broadcast_to([P, 4, n])
                        drain(v.tensor_tensor(hT[:, hf * 4:hf * 4 + 4, t0:t0 + n],
                                              bank(name)[:, 0:4 * n].rearrange("p (k t) -> p k t", k=4), w,
                                              ALU.mult), name)
            is_drained(dve, "vec")
            evac_hT("hT", "ln_mix")
            is_filled(dve, "ba")
            bav = bank("ba")[:, 0:24].rearrange("p (t c) -> p t c", t=NT)
            dve.wait_ge(smalls_in, 64)
            for t, (t0, n) in enumerate(TILES):
                step(v.tensor_tensor(tmp12[0:n, t, :], bav[0:n, t, HEADS:2 * HEADS], dtb[0:n, :], ALU.add))
                ins = v.tensor_copy(beta[0:n, t, :], bav[0:n, t, 0:HEADS])
                drain(ins, "ba") if t == NT - 1 else step(ins)
            mark(v.tensor_scalar(gl[:, :, :], tmp12[:, :, :], 0.0, None, ALU.max), "ba")
            mark(v.scalar_tensor_tensor(out=tmp12[:, :, :], in0=tmp12[:, :, :], scalar=-1.0, in1=tmp12[:, :, :],
                                        op0=ALU.mult, op1=ALU.max), "sp_in")

            def conv(c):
                is_drained(dve, f"pr{c + 4}")
                is_drained(dve, "sc")
                dve.wait_ge(ext_zero, PG + QKV_T)
                for out, col in ((ct[:, c, 0:SEQ], lambda j: qe[:, c, j:j + SEQ]),
                                 (ct[:, c, SEQ:T].rearrange("p (b s) -> p b s", b=DB),
                                  lambda j: sample_cols(qe, c, CH, j))):
                    step(v.tensor_scalar(out, col(0), vec("conv_w", c), None, ALU.mult))
                    for j in range(1, CONV):
                        ins = v.scalar_tensor_tensor(out=out, in0=col(j), scalar=vec("conv_w", j * QKV_T + c),
                                                     in1=out, op0=ALU.mult, op1=ALU.add)
                        step(ins, acc_ready if j == CONV - 1 and len(out.shape) == 3 else None)

            dve.wait_ge(a_mark, AM["lg"])
            step(v.tensor_scalar(beta[:, :, :], beta[:, :, :], 1.0, None, ALU.add))
            step(v.reciprocal(beta[:, :, :], beta[:, :, :]))
            step(v.tensor_tensor(gl[:, :, :], gl[:, :, :], tmp12[:, :, :], ALU.add))
            step(v.tensor_tensor(gl[:, :, :], gl[:, :, :], alog.unsqueeze(1).broadcast_to([P, NT, HEADS]), ALU.mult))
            mark(v.tensor_scalar(gl[:, :, :], gl[:, :, :], -1.0, None, ALU.mult), "g")
            for c in [4, 5, 6, 7, 0, 1, 2, 3]:
                conv(c)
            is_filled(dve, "gcs")
            for t, (t0, n) in enumerate(TILES):
                step(v.tensor_copy(gc[0:n, t, :], bank("gcs")[0:n, t * 4:t * 4 + 4]))
                ins = v.tensor_copy(egl[0:n, t, :], bank("gcs")[0:n, 12 + t * 4:16 + t * 4])
                drain(ins, "gcs") if t == NT - 1 else step(ins)
            mark(v.tensor_tensor(kdec[:, :, :], egl[:, :, :], gc[:, :, :], ALU.subtract), "gcs")
            for i in range(8 + 1):
                if i < 8:
                    f = float(P) if NORMED[i] < 4 else 1.0
                    is_filled(dve, f"ss{i}")
                    drain(v.tensor_scalar(rnb[i % 3], bank(f"ss{i}")[:, 0:T], f, f * EPS, ALU.mult, ALU.add), f"ss{i}")
                    step(v.reciprocal(rnb[i % 3], rnb[i % 3]), inv_ready)
                if i < 4:
                    conv(8 + i)
                if i:
                    roots[0] += 1
                    dve.wait_ge(root_ready, roots[0])
                    c = NORMED[i - 1]
                    step(v.tensor_tensor(ct[:, c, :], ct[:, c, :], rnb[(i - 1) % 3], ALU.mult), norm_ready)
            dve.wait_ge(consts, 3)
            step(v.tensor_scalar(inv16, iotaf[:, 0:16], 1.0, None, ALU.add))
            step(v.reciprocal(inv16, inv16))
            is_filled(dve, "npp"), is_filled(dve, "nps")
            for c, w in enumerate(WINDOWS):
                dve.wait_ge(g_ready, c + 1)
                pv = ptmp[:, :].unsqueeze(1)
                iv = inv16[:, 0:w]
                step(v.tensor_tensor(ptmp[:, PH:PH + w], ptmp[:, PH:PH + w], iv, ALU.mult))
                u0 = ue[:, c, PH:PH + w]
                step(v.tensor_tensor(u0, ptmp[:, PH:PH + w], u0, ALU.subtract))
                u1 = ue[:, c, PH + w:PH + SEQ]
                step(v.scalar_tensor_tensor(out=u1, in0=ptmp[:, PH + w:PH + SEQ], scalar=1.0 / w, in1=u1,
                                            op0=ALU.mult, op1=ALU.subtract))
                u2 = sample_cols(ue, c, PH)
                step(v.scalar_tensor_tensor(out=u2, in0=sample_cols(pv, 0, PH), scalar=1.0 / w, in1=u2,
                                            op0=ALU.mult, op1=ALU.subtract), d_ready)
                step(v.memset(small[:, 159:160], 0.0), acc_pool)
            for g in range(PG):
                is_filled(dve, f"pm{g}")
                drain(v.tensor_scalar(hT[:, g, :], bank(f"pm{g}")[:, 0:T], vec("pool_scale", g), None, ALU.mult), f"pm{g}")

            def ps4(name, n, m):
                return bank(name)[0:n, 0:HEADS * m].rearrange("p (h t) -> p h t", h=HEADS)

            for t, (t0, n) in enumerate(TILES):
                D = scratch[t][0]
                is_filled(dve, f"G{t}")
                drain(v.tensor_tensor(D, ps4(f"G{t}", n, n), over(gc[0:n, t, :], HEADS, n), ALU.subtract), f"G{t}")
                mark(v.tensor_scalar(D, D, 0.0, None, ALU.min), f"diff{t}")
            for t, (L, one, t0, n) in enumerate(tilepart):
                D, At, N, Um, Tm, Pm = scratch[t]
                dve.wait_ge(a_mark, AM[f"E{t}"])
                step(v.tensor_tensor(D, D, heads(L[0:n, 0:n], n), ALU.mult))
                is_filled(dve, f"kk{t}")
                drain(v.tensor_tensor(N, ps4(f"kk{t}", n, n), D, ALU.mult), f"kk{t}")
                is_filled(dve, f"qk{t}")
                drain(v.tensor_tensor(At, ps4(f"qk{t}", n, n), D, ALU.mult), f"qk{t}")
                step(v.tensor_tensor(N, N, over(beta[0:n, t, :], HEADS, n), ALU.mult))
                step(v.tensor_tensor(Pm, N, heads(lmask[0:n, 0, 0:n], n), ALU.mult))
                mark(v.tensor_tensor(Um, heads(ident[0:n, 0:n], n), Pm, ALU.subtract), f"U{t}")
            is_filled(dve, "kqs")
            drain(v.tensor_copy(kqS, bank("kqs").rearrange("p (h t) -> p h t", h=HEADS)), "kqs")
            for t, (t0, n) in enumerate(TILES):
                is_filled(dve, f"T{t}")
                drain(v.tensor_copy(scratch[t][4], ps4(f"T{t}", n, n)), f"T{t}")
            for s in range(1, LEVELS):
                ts = [t for t in range(NT) if t < 2 or s < 3]
                for t in ts:
                    n = TILES[t][1]
                    is_filled(dve, f"P{s}{t}")
                    drain(v.tensor_tensor(scratch[t][5], ps4(f"P{s}{t}", n, n), heads(lmask[0:n, s, 0:n], n), ALU.mult),
                          f"P{s}{t}")
                for t in ts:
                    n = TILES[t][1]
                    for nm, m in ((f"Q{s}{t}", 4), (f"QT{s}{t}", 3)):
                        if nm in uses:
                            is_filled(dve, nm)
                            drain(v.tensor_tensor(scratch[t][m], scratch[t][m], ps4(nm, n, n), ALU.subtract), nm)
                if s == 3:
                    is_drained(dve, "vN2")
                    dve.wait_ge(a_mark, AM["gexp"])
                    is_filled(dve, "R2k")
                    step(v.tensor_tensor(oN[2], ps4("R2k", NSAMP, P), over(egc[0:NSAMP, 2, :], HEADS, P), ALU.mult))
                    drain(v.tensor_tensor(vN[0:NSAMP, 2], vN[0:NSAMP, 2], oN[2], ALU.subtract), "R2k")
                    is_filled(dve, "R2q")
                    drain(v.tensor_tensor(qS2, ps4("R2q", NSAMP, P), over(egc[0:NSAMP, 2, :], HEADS, P), ALU.mult),
                          "R2q")
                if s == 4:
                    for t, (t0, n) in enumerate(TILES):
                        is_drained(dve, f"kN{t}")
                        ins = v.tensor_tensor(kN[0:n, t], kN[0:n, t], over(kdec[0:n, t, :], HEADS, P), ALU.mult)
                        mark(ins, "kd") if t == NT - 1 else step(ins)

            def new_value(t, name):
                n = TILES[t][1]
                is_filled(dve, name)
                drain(v.tensor_tensor(vN[0:n, t], ps4(name, n, P), over(beta[0:n, t, :], HEADS, P), ALU.mult), name)

            def output_norm(t):
                n = TILES[t][1]
                sq = scratch[0 if t == 0 else 1][0][0:n]
                m = tmp12[0:n, t, :]
                step(v.tensor_tensor(sq, oN[t][0:n], oN[t][0:n], ALU.mult))
                step(v.tensor_reduce(m, sq, AX_X, ALU.add))
                step(v.tensor_scalar(m, m, 1.0 / P, EPS, ALU.mult, ALU.add))
                step(v.reciprocal(m, m), inv_ready)

            def output_scale(t):
                n = TILES[t][1]
                roots[0] += 1
                dve.wait_ge(root_ready, roots[0])
                mark(v.tensor_tensor(oN[t][0:n], oN[t][0:n], over(tmp12[0:n, t, :], HEADS, P), ALU.mult), f"rs{t}")

            def output_turned(t):
                t0, n = TILES[t]
                is_filled(dve, f"oT{t}")
                is_drained(dve, "pr19")
                drain(v.scalar_tensor_tensor(out=hT[:, 4:8, t0:t0 + n], in0=ps4(f"oT{t}", P, n),
                                             scalar=vec("dn_norm"), in1=zT[:, :, t0:t0 + n],
                                             op0=ALU.mult, op1=ALU.mult), f"oT{t}")

            new_value(0, "v0")
            is_filled(dve, "S1")
            drain(v.tensor_copy(S1, ps4("S1", P, P)), "S1")
            new_value(2, "v2")
            E1, T1 = scratch[1][0], scratch[1][4]
            is_filled(dve, "kS1")
            is_drained(dve, "vN1")
            step(v.tensor_tensor(E1, ps4("kS1", P, P), over(egc[:, 1, :], HEADS, P), ALU.mult))
            drain(v.tensor_tensor(vN[:, 1], vN[:, 1], E1, ALU.subtract), "kS1")
            is_filled(dve, "o0")
            drain(v.tensor_copy(oN[0], ps4("o0", P, P)), "o0")
            output_norm(0)
            is_filled(dve, "qS1")
            drain(v.tensor_tensor(T1, ps4("qS1", P, P), over(egc[:, 1, :], HEADS, P), ALU.mult), "qS1")
            new_value(1, "v1")
            output_scale(0)
            is_filled(dve, "o2")
            drain(v.tensor_tensor(oN[2], ps4("o2", NSAMP, P), qS2, ALU.add), "o2")
            output_norm(2)
            is_filled(dve, "o1")
            drain(v.tensor_tensor(oN[1], ps4("o1", P, P), T1, ALU.add), "o1")
            output_scale(2)
            output_norm(1)
            output_turned(0)
            output_scale(1)
            output_turned(2)
            step(v.tensor_tensor(S1, S1, over(egl[:, 1, :], HEADS, P), ALU.mult))
            is_filled(dve, "S2")
            mark(v.tensor_tensor(S1, S1, ps4("S2", P, P), ALU.add), "S2")
            drain(v.tensor_copy(oss[:, 0:1], bank("S2")[:, 0:1]), "S2")

            def state_add(h):
                dve.wait_ge(g_ready, PG + h + 1)
                for q in range(2):
                    nm = f"ns{h}{'ab'[q]}"
                    is_filled(dve, nm)
                    sv = s0[:, 4 * q:4 * q + 4, h, :]
                    drain(v.tensor_tensor(sv, sv, ps4(nm, P, P), ALU.add), nm)
            output_turned(1)

            def add_projection(t):
                t0, n = TILES[t]
                dve.wait_ge(xagain_in[t], 16)
                for hf in range(2):
                    nm = f"op{t}{hf}"
                    is_filled(dve, nm)
                    xs = x3[0:n, t, hf * 512:(hf + 1) * 512]
                    drain(v.tensor_tensor(xs, product_of("op", t, hf), xs, ALU.add), nm)
                mark(v.memset(H[64:P, 2048:3072], 0.0) if t == 2 else v.memset(small[:, 159:160], 0.0), f"x2{t}")

            def second_norm(t):
                t0, n = TILES[t]
                dve.wait_ge(a_mark, AM[f"ss2{t}"])
                rsqrt_of(rstd[0:n, t:t + 1], ss[0:n, t:t + 1], 1.0 / D_MODEL)
                mark(v.tensor_scalar(h3[0:n, t, :], x3[0:n, t, :], rstd[0:n, t:t + 1], None, ALU.mult), f"h2{t}")
            add_projection(0)
            second_norm(0)
            second, third = slice(E, 2 * E), slice(2 * E, 3 * E)
            dve.wait_ge(bias_in, 16 * 9)
            step(v.tensor_copy(bias3, bias_f))
            step(v.tensor_tensor(bias3[second], bias_f[second], bias3[second], ALU.subtract))
            add_projection(2)
            second_norm(2)
            step(v.tensor_tensor(bias_f[third], bias_f[third], bias3[third], ALU.subtract))
            step(v.tensor_copy(bias3[third], bias_f[third]))
            mark(v.tensor_tensor(bias3[third], bias_f[third], bias3[third], ALU.subtract), "split")
            evac_hT("rT", "ln_moe", ORDER[:2])
            add_projection(1)
            second_norm(1)
            state_add(0)
            evac_hT("rT", "ln_moe", ORDER[2:])
            state_add(1)
            step(v.memset(Lg[:, :, :], 0.0))
            is_filled(dve, "lgT")
            for t, (t0, n) in enumerate(TILES):
                ins = v.tensor_copy(Lg[0:n, t, :], bank("lgT")[0:n, t * E:(t + 1) * E])
                drain(ins, "lgT") if t == NT - 1 else step(ins)
            for t in range(NT):
                step(v.max(m8[:, t, :], Lg[:, t, :]))
            mark(v.tensor_tensor(exq[:, :, :], Lg[:, :, :], m8[:, :, 0:1].broadcast_to([P, NT, E]), ALU.subtract), "m8")
            kth = m8[:, :, TOPK - 1:TOPK].broadcast_to([P, NT, E])
            step(v.tensor_tensor(gtm[:, :, :], Lg[:, :, :], kth, ALU.is_gt))
            step(v.tensor_tensor(eqm[:, :, :], Lg[:, :, :], kth, ALU.is_equal))
            step(v.tensor_reduce(ngt, gtm[:, :, :], AX_X, ALU.add))
            for t in range(NT):
                step(v.tensor_tensor_scan(cum[:, t, :], ones[:, 0:E], eqm[:, t, :], 0.0, ALU.mult, ALU.add))
            step(v.tensor_tensor(cum[:, :, :], cum[:, :, :], ngt.unsqueeze(2).broadcast_to([P, NT, E]), ALU.add))
            step(v.tensor_scalar(cum[:, :, :], cum[:, :, :], float(TOPK), None, ALU.is_le))
            step(v.tensor_tensor(eqm[:, :, :], eqm[:, :, :], cum[:, :, :], ALU.mult))
            step(v.tensor_tensor(sel[:, :, :], gtm[:, :, :], eqm[:, :, :], ALU.add))
            mark(v.memset(sel[NSAMP:P, NT - 1, :], 0.0), "sel")
            dve.wait_ge(a_mark, AM["exq"])
            step(v.tensor_tensor(exq[:, :, :], exq[:, :, :], sel[:, :, :], ALU.mult))
            step(v.tensor_reduce(den, exq[:, :, :], AX_X, ALU.add))
            step(v.tensor_scalar(den, den, 1e-30, None, ALU.max))
            step(v.reciprocal(den, den))
            mark(v.tensor_tensor(gate[:, 0:E, :].rearrange("p e t -> p t e"), exq[:, :, :],
                                 den.unsqueeze(2).broadcast_to([P, NT, E]), ALU.mult), "gates")
            is_filled(dve, "rk")
            rkv = bank("rk")[:, 0:NT * E].rearrange("p (t e) -> p t e", t=NT)
            rankv = rank[:, 0:E, :].rearrange("p e t -> p t e")
            step(v.scalar_tensor_tensor(out=exq[:, :, :], in0=rkv, scalar=1.0, in1=sel[:, :, :],
                                        op0=ALU.add, op1=ALU.mult))
            step(v.tensor_scalar(rankv, exq[:, :, :], -1.0, None, ALU.add))
            drain(v.tensor_copy(cnt, bank("rk")[:, NT * E:(NT + 1) * E]), "rk")

            def select(half, rank_pair, gate_pair, experts):
                io = iotaf[:, 0:CAP].unsqueeze(1).unsqueeze(1).broadcast_to([P, NT, 2, CAP])
                sv = Ssel.rearrange("p t (a s) -> p t a s", a=2)
                gv = Sgat.rearrange("p t (a s) -> p t a s", a=2)
                rv = rank_pair.rearrange("p a t -> p t a").unsqueeze(3).broadcast_to([P, NT, 2, CAP])
                ev = gate_pair.rearrange("p a t -> p t a").unsqueeze(3).broadcast_to([P, NT, 2, CAP])
                return [v.tensor_tensor, (sv, io, rv, ALU.is_equal)], [v.tensor_tensor, (gv, sv, ev, ALU.mult)], \
                    [v.tensor_copy, (ind[:, half, :].rearrange("p (a s) -> p a s", a=2),
                                     experts.unsqueeze(2).broadcast_to([3 * E, 2, CAP]))]

            def run(op):
                return op[0](*op[1])

            def scaled_turn(name, k0):
                w = vec("ln_moe", k0, 4).unsqueeze(2).broadcast_to([P, 4, P])
                return (xgT[:, k0:k0 + 4, :], name.rearrange("p (k s) -> p k s", k=4), w, ALU.mult)

            a1, a2, a3 = select(0, rank[:, 0:2, :], gate[:, 0:2, :], ident3[:, 0:2])
            step(run(a1)), step(run(a2)), step(run(a3), pair_sel)
            state_add(2)
            state_add(3)
            mark(v.memset(oss[:, 0:1], 0.0), "S0")
            for nm, k0 in (("xta", 0), ("xtb", 4)):
                is_filled(dve, nm)
                drain(v.tensor_tensor(*scaled_turn(bank(nm), k0)), nm)
            mark(v.memset(ybuf, 0.0), "ybuf_zero")
            is_filled(dve, "sgt")
            for bi, off in enumerate(OV_OFF):
                step(v.tensor_scalar(flg[:, :, bi], cnt, float(off), None, ALU.is_gt))
                step(v.memset(ovec[:, :, bi], float(off)))
                step(v.tensor_copy(evec[:, :, bi], iotaf[:, 0:E]))
            flat = flg.rearrange("p e b -> p (e b)")
            step(v.tensor_tensor_scan(pos, ones[:, 0:2 * E], flat, 0.0, ALU.mult, ALU.add))
            step(v.tensor_tensor(evec, evec, flg, ALU.mult))
            step(v.tensor_tensor(ovec, ovec, flg, ALU.mult))
            dve.wait_ge(ssm_stored, 16)
            for src, dst in ((evec, ove_f), (ovec, ov_off[:, :])):
                step(v.tensor_tensor(cmp_, pos.unsqueeze(1).broadcast_to([P, OV_MAX, 64]),
                                     iotaf[:, 1:OV_MAX + 1].unsqueeze(2).broadcast_to([P, OV_MAX, 64]), ALU.is_equal))
                step(v.tensor_tensor(cmp_, cmp_, src.rearrange("p e b -> p (e b)").unsqueeze(1)
                                     .broadcast_to([P, OV_MAX, 64]), ALU.mult))
                step(v.tensor_reduce(dst, cmp_, AX_X, ALU.add))
            step(v.tensor_copy(ov_e[:, :], ove_f))
            mark(v.tensor_copy(ov_n[:, :], pos[:, 63:64]), "table")

            def turns(lo, hi):
                with dve.Fori(lo, hi) as i:
                    VPP = 3 + 2
                    for half in range(2):
                        pair = i * 2 + half
                        cnt_ = [0]

                        def lstep(ins):
                            cnt_[0] += 1
                            k = half * VPP + cnt_[0]
                            ins.then_inc(v_loop, 1)
                            dve.wait_ge(v_loop, i * (2 * VPP) + k)

                        def lmark(ins, s, value):
                            ins.then_inc(s, 1)
                            dve.wait_ge(s, value)

                        def aux(k, op, *args):
                            l = 13 * half + k
                            b, m = 6 + l % 2, l // 2
                            dve.wait_ge(filled[b], base[b] + 1 + m + i * 13)
                            lmark(op(*args), drained[b], base[b] + 1 + m + i * 13)

                        def auxbank(k):
                            return PS[:, 6 + (13 * half + k) % 2, :]
                        e = i * 4 + 2 * half + 2
                        a1, a2, a3 = select(1 - half, rank[:, bass.ds(e, 2), :], gate[:, bass.ds(e, 2), :],
                                            ident3[:, bass.ds(e, 2)])
                        lstep(run(a1)), lstep(run(a2))
                        dve.wait_ge(chunk_used, i * TURN + half * CPP + CPM)
                        lmark(v.tensor_scalar(gbuf, PS[:, 0:2, :].rearrange("p b f -> p (b f)"), LIMIT, None, ALU.min),
                              g_act, pair + 2)
                        lmark(run(a3), pair_sel, pair + 2)
                        dve.wait_ge(chunk_used, i * TURN + half * CPP + 2 * CPM)
                        lmark(v.tensor_scalar(ubuf, PS[:, 2:4, :].rearrange("p b f -> p (b f)"), LIMIT, -LIMIT,
                                              ALU.min, ALU.max), up_act, pair + 2)
                        lstep(v.scalar_tensor_tensor(out=ubuf, in0=ubuf, scalar=1.0, in1=gbuf, op0=ALU.add, op1=ALU.mult))
                        dve.wait_ge(sig_act, pair + 1)
                        lmark(v.tensor_tensor(ubuf, ubuf, sbuf_, ALU.mult), hid_act, pair + 1)
                        for t, (t0, n) in enumerate(TILES):
                            for hf in range(2):
                                k = 2 + 2 * t + hf
                                xs = x3[0:n, t, hf * 512:(hf + 1) * 512]
                                aux(k, v.tensor_tensor, xs, auxbank(k)[0:n, :], xs, ALU.add)
                        aux(11, v.tensor_tensor, *scaled_turn(auxbank(11), 0))
                        aux(12, v.tensor_tensor, *scaled_turn(auxbank(12), 4))
                        while cnt_[0] < VPP:
                            lstep(v.memset(small[:, 159:160], 0.0))

            turns(0, MID)
            n_ov = dve.value_load(ov_n[0:1, 0:1], min_val=0, max_val=OV_MAX)

            def overflow_block(j):
                e = dve.value_load(ov_e[0:1, bass.ds(j, 1)], min_val=0, max_val=E - 1)
                oc = [0]

                def ostep(ins):
                    oc[0] += 1
                    ins.then_inc(v_ov, 1)
                    dve.wait_ge(v_ov, j * 7 + oc[0])

                def omark(ins, s):
                    ins.then_inc(s, 1)
                    dve.wait_ge(s, j + 1)

                def ovaux(k, op, *args):
                    b, m = k % 2, k // 2
                    dve.wait_ge(ov_filled[b], 1 + m + j * OV_USES)
                    op(*args).then_inc(ov_drained[b], 1)
                    dve.wait_ge(ov_drained[b], 2 + m + j * OV_USES)
                rel = small[:, 156:159]
                ostep(v.tensor_scalar(rel, rank[:, bass.ds(e, 1), :].rearrange("p a t -> p (a t)"),
                                      ov_off[:, bass.ds(j, 1)], None, ALU.subtract))
                ostep(v.tensor_tensor(Ssel, iotaf[:, :].unsqueeze(1).broadcast_to([P, NT, P]),
                                      rel.unsqueeze(2).broadcast_to([P, NT, P]), ALU.is_equal))
                ostep(v.tensor_tensor(Sgat, Ssel, gate[:, bass.ds(e, 1), :].rearrange("p a t -> p (a t)")
                                      .unsqueeze(2).broadcast_to([P, NT, P]), ALU.mult))
                omark(v.tensor_copy(ind[:, 0, :], ident3[:, bass.ds(e, 1)].broadcast_to([3 * E, P])), ov_sel)
                ovaux(2, v.tensor_tensor, *scaled_turn(PS[:, 6, :], 0))
                ovaux(3, v.tensor_tensor, *scaled_turn(PS[:, 7, :], 4))
                dve.wait_ge(ov_used, j * OV_CHUNKS + OV_CHUNKS + 2)
                omark(v.tensor_scalar(gbuf, PS[:, 0:2, :].rearrange("p b f -> p (b f)"), LIMIT, None, ALU.min), ovg_act)
                dve.wait_ge(ov_used, j * OV_CHUNKS + OV_CHUNKS + 4)
                ostep(v.tensor_scalar(ubuf, PS[:, 2:4, :].rearrange("p b f -> p (b f)"), LIMIT, -LIMIT,
                                      ALU.min, ALU.max))
                ostep(v.scalar_tensor_tensor(out=ubuf, in0=ubuf, scalar=1.0, in1=gbuf, op0=ALU.add, op1=ALU.mult))
                assert oc[0] == 5
                dve.wait_ge(ovs_act, j + 1)
                omark(v.tensor_tensor(ubuf, ubuf, sbuf_, ALU.mult), ovh_act)
                e1 = 4 * MID
                a1, a2, a3 = select(0, rank[:, e1:e1 + 2, :], gate[:, e1:e1 + 2, :], ident3[:, e1:e1 + 2])
                dve.wait_ge(ov_filled[0], 4 + j * OV_USES)
                dve.wait_ge(ov_filled[1], 4 + j * OV_USES)
                ostep(run(a1)), ostep(run(a2))
                dve.wait_ge(ov_used, j * OV_CHUNKS + OV_CHUNKS + 5)
                omark(run(a3), ov_next)
                for t, (t0, n) in enumerate(TILES):
                    for hf in range(2):
                        k = 10 + t * 2 + hf
                        xs = x3[0:n, t, hf * 512:(hf + 1) * 512]
                        ovaux(k, v.tensor_tensor, xs, PS[0:n, 6 + k % 2, :], xs, ALU.add)
                ovaux(16, v.tensor_tensor, *scaled_turn(PS[:, 6, :], 0))
                ovaux(17, v.tensor_tensor, *scaled_turn(PS[:, 7, :], 4))
                dve.wait_ge(ov_filled[1], 10 + j * OV_USES)
                v.memset(small[:, 155:156], 0.0)

            with dve.Fori(0, OV_FIRST) as j:
                with dve.If(j < n_ov):
                    overflow_block(j)
            with dve.If(n_ov > OV_FIRST):
                with dve.Fori(OV_FIRST, OV_MAX) as j:
                    with dve.If(j < n_ov):
                        overflow_block(j)
            turns(MID, TURNS)
            for t, (t0, n) in enumerate(TILES):
                for hf in range(2):
                    nm = f"sc{t}{hf}"
                    is_filled(dve, nm)
                    xs = x3[0:n, t, hf * 512:(hf + 1) * 512]
                    drain(v.tensor_tensor(xs, bank(nm)[0:n, :], xs, ALU.add), nm)
                mark(v.memset(small[:, 159:160], 0.0), f"moe{t}")
            for t, (t0, n) in enumerate(TILES):
                dve.wait_ge(a_mark, AM[f"ss3{t}"])
                rsqrt_of(rstd[0:n, t:t + 1], ss[0:n, t:t + 1], 1.0 / D_MODEL)
                mark(v.tensor_scalar(h3[0:n, t, :], x3[0:n, t, :], rstd[0:n, t:t + 1], None, ALU.mult), f"h3{t}")
            evac_hT("tT", "ln_ple")
            for t, (t0, n) in enumerate(TILES):
                for hf in range(2):
                    cs = slice(hf * 512, (hf + 1) * 512)
                    is_drained(dve, f"pp{t}{hf}")
                    is_drained(dve, f"pg{t}{hf}")
                    step(v.tensor_tensor(sg3[0:n, t, cs], ppb[0:n, t, cs], sg3[0:n, t, cs], ALU.mult))
                    ins = v.tensor_tensor(x3[0:n, t, cs], x3[0:n, t, cs], sg3[0:n, t, cs], ALU.add)
                    mark(ins, f"y{t}") if hf else step(ins)
                dve.wait_ge(fnb_in, 16)
                dve.wait_ge(a_mark, AM[f"ss4{t}"])
                rsqrt_of(rstd[0:n, t:t + 1], ss[0:n, t:t + 1], 1.0 / D_MODEL)
                mark(v.scalar_tensor_tensor(out=h3[0:n, t, :], in0=x3[0:n, t, :], scalar=rstd[0:n, t:t + 1],
                                            in1=fnb[0:n, :], op0=ALU.mult, op1=ALU.mult), f"yout{t}")


_INS = ['x_prompt', 'x_sample', 'state_pool', 'state_conv', 'state_ssm', 'p_prompt', 'p_sample', 'ln_mix', 'w_in',
        'pool_w', 'pool_scale', 'conv_w', 'a_log', 'dt_bias', 'dn_norm', 'w_out', 'ln_moe', 'router_w', 'router_b',
        'w_gate', 'b_gate', 'w_up', 'b_up', 'w_down', 'b_down', 'ln_ple', 'w_ple_gate', 'w_ple', 'final_norm']
_OUTS = [(1, SEQ, D_MODEL), (DB, DS, D_MODEL), (1, 1, PH, POOL_W), (1, 1, CH, QKV_T * P), (1, 1, HEADS, P, P),
         (1, DB, PH, POOL_W), (1, DB, CH, QKV_T * P), (1, DB, HEADS, P, P)]


def kernel(**inputs):
    import numpy as _np
    import concourse.bacc as _bacc
    from concourse import mybir as _mybir
    from concourse.bass_utils import run_bass_kernel_spmd as _run

    nc = _bacc.Bacc("TRN2", target_bir_lowering=False, num_devices=1)
    arrays, d = {}, {}
    for name in _INS:
        a = _np.ascontiguousarray(inputs[name])
        arrays[f"in_{name}"] = a
        d[name] = nc.dram_tensor(f"in_{name}", a.shape, _mybir.dt.from_np(a.dtype), kind="ExternalInput").ap()
    o = [nc.dram_tensor(f"out_{i}", shape, _mybir.dt.float32, kind="ExternalOutput").ap()
         for i, shape in enumerate(_OUTS)]
    trunk_kernel(nc, d, o)
    r = _run(nc, [arrays], core_ids=[0])
    return tuple(r.results[0][f"out_{i}"] for i in range(len(_OUTS)))
```
